# Optimizing a Trainium2 kernel written in Bass

```python
import math
import numpy as np
import jax
import jax.numpy as jnp
from jax import lax

D_MODEL = 1024
BATCH = 1
SEQ = 512
DEPTH = 1

GRID_W = 64
CTX_LEN = 256
EPS = 1e-6
ROPE_BASE = 10000.0
Q_BLOCK = 128
N_MOD = 6

S5_WIDTH = D_MODEL // 4
S5_GROUP = 16
S5_GROUPS = S5_WIDTH // S5_GROUP
S5_STATE = 64
S5_DT_MIN = 0.001
S5_DT_MAX = 0.1

DIFF_HEADS = 4
DIFF_HEAD_DIM = 64
DIFF_V_DIM = 2 * DIFF_HEAD_DIM
DIFF_QK_WIDTH = DIFF_HEADS * 2 * DIFF_HEAD_DIM
DIFF_WIDTH = DIFF_HEADS * DIFF_V_DIM
DIFF_SCALE = DIFF_HEAD_DIM ** -0.5

MLA_HEADS = 4
MLA_Q_RANK = D_MODEL // 4
MLA_KV_RANK = D_MODEL // 8
MLA_NOPE = 64
MLA_ROPE = 32
MLA_V = 64
MLA_WIDTH = MLA_HEADS * MLA_V
MLA_SCALE = (MLA_NOPE + MLA_ROPE) ** -0.5

MIX_WIDTH = S5_WIDTH + DIFF_WIDTH + MLA_WIDTH
IN_SIZES = (S5_WIDTH, DIFF_QK_WIDTH, DIFF_QK_WIDTH, DIFF_WIDTH, MLA_Q_RANK, MLA_KV_RANK, MLA_ROPE)
IN_WIDTH = sum(IN_SIZES)

MOE_GROUPS = 4
MOE_PER_GROUP = 8
MOE_EXPERTS = MOE_GROUPS * MOE_PER_GROUP
MOE_TOP_K = 2
MOE_HIDDEN = D_MODEL // 2

kernel_name = "hybrid_s5_diffattn_mla_hmoe_dit"

def rms_norm(x, g):
    xf = x.astype(jnp.float32)
    y = xf * lax.rsqrt(jnp.mean(xf * xf, axis=-1, keepdims=True) + EPS)
    return (y * g.astype(jnp.float32)).astype(x.dtype)

def modulate(h, shift, scale):
    return h * (1 + scale) + shift

def adaln_terms(cvec, w_mod, b_mod):
    return jnp.split(jax.nn.silu(cvec) @ w_mod + b_mod, N_MOD, axis=-1)

def split_in_proj(z):
    return jnp.split(z, np.cumsum(IN_SIZES)[:-1].tolist(), axis=-1)

def axial_rope_tables(length, dim):
    rows = length // GRID_W
    row, col = jnp.meshgrid(jnp.arange(rows, dtype=jnp.float32),
                            jnp.arange(GRID_W, dtype=jnp.float32), indexing="ij")
    n_freq = dim // 4
    freqs = ROPE_BASE ** (-jnp.arange(n_freq, dtype=jnp.float32) / n_freq)
    ang = jnp.concatenate([row.reshape(-1, 1) * freqs, col.reshape(-1, 1) * freqs], axis=-1)
    return jnp.cos(ang), jnp.sin(ang)

def axial_rope(x, cos, sin):
    shape = (1, x.shape[1]) + (1,) * (x.ndim - 3) + (cos.shape[-1],)
    cos = cos.reshape(shape)
    sin = sin.reshape(shape)
    xf = x.astype(jnp.float32)
    x1 = xf[..., 0::2]
    x2 = xf[..., 1::2]
    out = jnp.stack([x1 * cos - x2 * sin, x1 * sin + x2 * cos], axis=-1).reshape(x.shape)
    return out.astype(x.dtype)

def sweep_query_blocks(fn, q):
    b, length = q.shape[:2]
    nb = length // Q_BLOCK
    qb = jnp.moveaxis(q.reshape((b, nb, Q_BLOCK) + q.shape[2:]), 1, 0)
    out = jnp.moveaxis(lax.map(fn, qb), 0, 1)
    return out.reshape((b, length) + out.shape[3:])

def _lin_combine(e1, e2):
    a1, b1 = e1
    a2, b2 = e2
    return a1 * a2, a2 * b1 + b2

def linear_scan(lam_bar, bu, h0, reverse):
    a = jnp.broadcast_to(lam_bar, (1, bu.shape[1]) + lam_bar.shape)
    a_cum, h = lax.associative_scan(_lin_combine, (a, bu), reverse=reverse, axis=1)
    if h0 is not None:
        h = h + a_cum * h0[:, None]
    return h

def s5_mixer(u_ctx, u_lat, a_re, a_im, log_step, b_re, b_im, c_re, c_im, d_skip, w_glu, b_glu, need_ctx):
    def to_groups(u):
        u = u.astype(jnp.float32)
        return u.reshape(u.shape[:2] + (S5_GROUPS, S5_GROUP)).astype(jnp.complex64)

    uc = to_groups(u_ctx)
    ul = to_groups(u_lat)
    ys_lat = []
    ys_ctx = []
    for direction in range(2):
        reverse = direction == 1
        lam = lax.complex(a_re[direction].astype(jnp.float32), a_im[direction].astype(jnp.float32))
        step = jnp.exp(log_step[direction].astype(jnp.float32))[:, None]
        lam_bar = jnp.exp(lam * step)
        b_mat = lax.complex(b_re[direction].astype(jnp.float32), b_im[direction].astype(jnp.float32))
        b_bar = ((lam_bar - 1.0) / lam)[..., None] * b_mat
        c_mat = lax.complex(c_re[direction].astype(jnp.float32), c_im[direction].astype(jnp.float32))
        h_ctx = linear_scan(lam_bar, jnp.einsum("gpn,blgn->blgp", b_bar, uc), None, reverse)
        h0 = h_ctx[:, 0] if reverse else h_ctx[:, -1]
        h_lat = linear_scan(lam_bar, jnp.einsum("gpn,blgn->blgp", b_bar, ul), h0, reverse)
        ys_lat.append(jnp.real(jnp.einsum("gnp,blgp->blgn", c_mat, h_lat)))
        if need_ctx:
            ys_ctx.append(jnp.real(jnp.einsum("gnp,blgp->blgn", c_mat, h_ctx)))

    def readout(y, u):
        y = y.reshape(u.shape) + d_skip.astype(jnp.float32) * u.astype(jnp.float32)
        y = jax.nn.gelu(y)
        y = y * jax.nn.sigmoid(y @ w_glu.astype(jnp.float32) + b_glu.astype(jnp.float32))
        return y.astype(u.dtype)

    y_lat = readout(ys_lat[0] + ys_lat[1], u_lat)
    y_ctx = readout(ys_ctx[0] + ys_ctx[1], u_ctx) if need_ctx else None
    return y_ctx, y_lat

def diff_mixer(q_ctx, k_ctx, v_ctx, q_lat, k_lat, v_lat, lambdas, subln_g, lam_init, cos, sin, need_ctx):
    def heads(t, tail):
        return t.reshape(t.shape[:2] + tail)

    q_ctx, k_ctx = heads(q_ctx, (DIFF_HEADS, 2, DIFF_HEAD_DIM)), heads(k_ctx, (DIFF_HEADS, 2, DIFF_HEAD_DIM))
    q_lat, k_lat = heads(q_lat, (DIFF_HEADS, 2, DIFF_HEAD_DIM)), heads(k_lat, (DIFF_HEADS, 2, DIFF_HEAD_DIM))
    v_ctx, v_lat = heads(v_ctx, (DIFF_HEADS, DIFF_V_DIM)), heads(v_lat, (DIFF_HEADS, DIFF_V_DIM))
    q_lat = axial_rope(q_lat, cos, sin)
    k_lat = axial_rope(k_lat, cos, sin)
    lf = lambdas.astype(jnp.float32)
    lam = jnp.exp(jnp.sum(lf[0] * lf[1])) - jnp.exp(jnp.sum(lf[2] * lf[3])) + lam_init

    def attend(q, k, v):
        s = jnp.einsum("bqhmd,bkhmd->bhmqk", q, k).astype(jnp.float32) * DIFF_SCALE
        p = jax.nn.softmax(s, axis=-1)
        p = p[:, :, 0] - lam * p[:, :, 1]
        return jnp.einsum("bhqk,bkhe->bqhe", p.astype(v.dtype), v)

    def finish(o):
        o = rms_norm(o, subln_g) * (1.0 - lam_init)
        return o.reshape(o.shape[:2] + (DIFF_WIDTH,))

    k_all = jnp.concatenate([k_ctx, k_lat], axis=1)
    v_all = jnp.concatenate([v_ctx, v_lat], axis=1)
    o_lat = finish(sweep_query_blocks(lambda qb: attend(qb, k_all, v_all), q_lat))
    o_ctx = finish(attend(q_ctx, k_ctx, v_ctx)) if need_ctx else None
    return o_ctx, o_lat

def mla_mixer(cq_ctx, ckv_ctx, kr_ctx, cq_lat, ckv_lat, kr_lat, q_norm_g, w_uq, kv_norm_g, w_ukv, cos, sin, need_ctx):
    def qkv(cq, ckv, kr, use_rope):
        b, length = cq.shape[:2]
        q = (rms_norm(cq, q_norm_g) @ w_uq).reshape(b, length, MLA_HEADS, MLA_NOPE + MLA_ROPE)
        kv = (rms_norm(ckv, kv_norm_g) @ w_ukv).reshape(b, length, MLA_HEADS, MLA_NOPE + MLA_V)
        q_nope, q_rope = q[..., :MLA_NOPE], q[..., MLA_NOPE:]
        k_nope, v = kv[..., :MLA_NOPE], kv[..., MLA_NOPE:]
        if use_rope:
            q_rope = axial_rope(q_rope, cos, sin)
            kr = axial_rope(kr, cos, sin)
        k_rope = jnp.broadcast_to(kr[:, :, None, :], (b, length, MLA_HEADS, MLA_ROPE))
        return (jnp.concatenate([q_nope, q_rope], axis=-1),
                jnp.concatenate([k_nope, k_rope], axis=-1), v)

    def attend(q, k, v):
        s = jnp.einsum("bqhd,bkhd->bhqk", q, k).astype(jnp.float32) * MLA_SCALE
        p = jax.nn.softmax(s, axis=-1)
        o = jnp.einsum("bhqk,bkhe->bqhe", p.astype(v.dtype), v)
        return o.reshape(o.shape[:2] + (MLA_WIDTH,))

    q_c, k_c, v_c = qkv(cq_ctx, ckv_ctx, kr_ctx, False)
    q_l, k_l, v_l = qkv(cq_lat, ckv_lat, kr_lat, True)
    k_all = jnp.concatenate([k_c, k_l], axis=1)
    v_all = jnp.concatenate([v_c, v_l], axis=1)
    o_lat = sweep_query_blocks(lambda qb: attend(qb, k_all, v_all), q_l)
    o_ctx = attend(q_c, k_c, v_c) if need_ctx else None
    return o_ctx, o_lat

def hier_moe(h, w_group, b_group, w_router, b_router, w1, w3, w2):
    t = h.shape[0]
    g_logits = (h @ w_group).astype(jnp.float32) + b_group.astype(jnp.float32)
    g_prob = jax.nn.softmax(g_logits, axis=-1)
    g_idx = jnp.argmax(g_logits, axis=-1)
    e_logits = ((h @ w_router).astype(jnp.float32) + b_router.astype(jnp.float32)).reshape(t, MOE_GROUPS, MOE_PER_GROUP)
    within = jnp.take_along_axis(e_logits, g_idx[:, None, None], axis=1)[:, 0]
    top_vals, top_idx = lax.top_k(within, MOE_TOP_K)
    w = jax.nn.softmax(top_vals, axis=-1) * jnp.take_along_axis(g_prob, g_idx[:, None], axis=1)
    eid = g_idx[:, None] * MOE_PER_GROUP + top_idx
    gates = jnp.sum(jax.nn.one_hot(eid, MOE_EXPERTS, dtype=jnp.float32) * w[..., None], axis=1)
    out = jnp.zeros(h.shape, jnp.float32)
    for e in range(MOE_EXPERTS):
        hid = jax.nn.silu(h @ w1[e]) * (h @ w3[e])
        out = out + gates[:, e:e + 1] * (hid @ w2[e]).astype(jnp.float32)
    return out.astype(h.dtype)

def setup_inputs(seed: int = 0) -> dict:
    key = jax.random.key(seed)
    ks = iter(jax.random.split(key, 48))

    def nrm(shape, scale):
        return jax.random.normal(next(ks), shape, jnp.float32) * scale

    d = D_MODEL
    dir_gp = (DEPTH, 2, S5_GROUPS, S5_STATE)
    n_idx = jnp.arange(S5_STATE, dtype=jnp.float32)
    log_lo, log_hi = math.log(S5_DT_MIN), math.log(S5_DT_MAX)
    return {
        "x": nrm((BATCH, SEQ, d), 1.0),
        "c": nrm((BATCH, d), 1.0),
        "ctx": nrm((BATCH, CTX_LEN, d), 1.0),
        "c_ctx": nrm((d,), 1.0),
        "w_mod": nrm((DEPTH, d, N_MOD * d), d ** -0.5),
        "b_mod": nrm((DEPTH, N_MOD * d), 0.02),
        "norm_mix_g": 1.0 + nrm((DEPTH, d), 0.02),
        "norm_ffn_g": 1.0 + nrm((DEPTH, d), 0.02),
        "w_in": nrm((DEPTH, d, IN_WIDTH), d ** -0.5),
        "s5_a_re": -0.5 + nrm(dir_gp, 0.01),
        "s5_a_im": jnp.pi * n_idx + nrm(dir_gp, 0.01),
        "s5_log_step": log_lo + (log_hi - log_lo) * jax.random.uniform(next(ks), (DEPTH, 2, S5_GROUPS), jnp.float32),
        "s5_b_re": nrm(dir_gp + (S5_GROUP,), (2 * S5_GROUP) ** -0.5),
        "s5_b_im": nrm(dir_gp + (S5_GROUP,), (2 * S5_GROUP) ** -0.5),
        "s5_c_re": nrm((DEPTH, 2, S5_GROUPS, S5_GROUP, S5_STATE), S5_STATE ** -0.5),
        "s5_c_im": nrm((DEPTH, 2, S5_GROUPS, S5_GROUP, S5_STATE), S5_STATE ** -0.5),
        "s5_d": nrm((DEPTH, S5_WIDTH), 1.0),
        "s5_w_glu": nrm((DEPTH, S5_WIDTH, S5_WIDTH), S5_WIDTH ** -0.5),
        "s5_b_glu": nrm((DEPTH, S5_WIDTH), 0.02),
        "diff_lambda": nrm((DEPTH, 4, DIFF_HEAD_DIM), 0.1),
        "diff_subln_g": 1.0 + nrm((DEPTH, DIFF_V_DIM), 0.02),
        "mla_q_norm_g": 1.0 + nrm((DEPTH, MLA_Q_RANK), 0.02),
        "mla_w_uq": nrm((DEPTH, MLA_Q_RANK, MLA_HEADS * (MLA_NOPE + MLA_ROPE)), MLA_Q_RANK ** -0.5),
        "mla_kv_norm_g": 1.0 + nrm((DEPTH, MLA_KV_RANK), 0.02),
        "mla_w_ukv": nrm((DEPTH, MLA_KV_RANK, MLA_HEADS * (MLA_NOPE + MLA_V)), MLA_KV_RANK ** -0.5),
        "w_out": nrm((DEPTH, MIX_WIDTH, d), MIX_WIDTH ** -0.5),
        "moe_w_group": nrm((DEPTH, d, MOE_GROUPS), d ** -0.5),
        "moe_b_group": nrm((DEPTH, MOE_GROUPS), 0.01),
        "moe_w_router": nrm((DEPTH, d, MOE_EXPERTS), d ** -0.5),
        "moe_b_router": nrm((DEPTH, MOE_EXPERTS), 0.01),
        "moe_w1": nrm((DEPTH, MOE_EXPERTS, d, MOE_HIDDEN), d ** -0.5),
        "moe_w3": nrm((DEPTH, MOE_EXPERTS, d, MOE_HIDDEN), d ** -0.5),
        "moe_w2": nrm((DEPTH, MOE_EXPERTS, MOE_HIDDEN, d), MOE_HIDDEN ** -0.5),
        "final_norm_g": 1.0 + nrm((d,), 0.02),
    }

def reference(x, c, ctx, c_ctx, w_mod, b_mod, norm_mix_g, norm_ffn_g, w_in,
              s5_a_re, s5_a_im, s5_log_step, s5_b_re, s5_b_im, s5_c_re, s5_c_im, s5_d, s5_w_glu, s5_b_glu,
              diff_lambda, diff_subln_g, mla_q_norm_g, mla_w_uq, mla_kv_norm_g, mla_w_ukv, w_out,
              moe_w_group, moe_b_group, moe_w_router, moe_b_router, moe_w1, moe_w3, moe_w2, final_norm_g):
    b, length, d = x.shape
    cos_d, sin_d = axial_rope_tables(length, DIFF_HEAD_DIM)
    cos_m, sin_m = axial_rope_tables(length, MLA_ROPE)
    xc = ctx
    for l in range(DEPTH):
        need_ctx = l < DEPTH - 1
        sh_m, sc_m, g_m, sh_f, sc_f, g_f = [t[:, None, :] for t in adaln_terms(c, w_mod[l], b_mod[l])]
        csh_m, csc_m, cg_m, csh_f, csc_f, cg_f = adaln_terms(c_ctx, w_mod[l], b_mod[l])

        z_lat = split_in_proj(modulate(rms_norm(x, norm_mix_g[l]), sh_m, sc_m) @ w_in[l])
        z_ctx = split_in_proj(modulate(rms_norm(xc, norm_mix_g[l]), csh_m, csc_m) @ w_in[l])
        s5_c, s5_l = s5_mixer(z_ctx[0], z_lat[0], s5_a_re[l], s5_a_im[l], s5_log_step[l], s5_b_re[l], s5_b_im[l],
                              s5_c_re[l], s5_c_im[l], s5_d[l], s5_w_glu[l], s5_b_glu[l], need_ctx)
        lam_init = 0.8 - 0.6 * math.exp(-0.3 * l)
        df_c, df_l = diff_mixer(z_ctx[1], z_ctx[2], z_ctx[3], z_lat[1], z_lat[2], z_lat[3],
                                diff_lambda[l], diff_subln_g[l], lam_init, cos_d, sin_d, need_ctx)
        ml_c, ml_l = mla_mixer(z_ctx[4], z_ctx[5], z_ctx[6], z_lat[4], z_lat[5], z_lat[6],
                               mla_q_norm_g[l], mla_w_uq[l], mla_kv_norm_g[l], mla_w_ukv[l], cos_m, sin_m, need_ctx)
        x = x + g_m * (jnp.concatenate([s5_l, df_l, ml_l], axis=-1) @ w_out[l])
        if need_ctx:
            xc = xc + cg_m * (jnp.concatenate([s5_c, df_c, ml_c], axis=-1) @ w_out[l])

        h = modulate(rms_norm(x, norm_ffn_g[l]), sh_f, sc_f).reshape(-1, d)
        moe_args = (moe_w_group[l], moe_b_group[l], moe_w_router[l], moe_b_router[l], moe_w1[l], moe_w3[l], moe_w2[l])
        if need_ctx:
            hc = modulate(rms_norm(xc, norm_ffn_g[l]), csh_f, csc_f).reshape(-1, d)
            f = hier_moe(jnp.concatenate([h, hc], axis=0), *moe_args)
            xc = xc + cg_f * f[b * length:].reshape(xc.shape)
            f = f[:b * length]
        else:
            f = hier_moe(h, *moe_args)
        x = x + g_f * f.reshape(x.shape)
    return rms_norm(x, final_norm_g)


_drawn_inputs = setup_inputs


def setup_inputs(seed=0):
    import zlib

    import numpy as np

    out = dict(_drawn_inputs(seed))
    spreads = {}
    factors = {'s5_a_re': 200.0,
     's5_b_glu': 37.849,
     'diff_subln_g': 7.898,
     'mla_q_norm_g': 7.554,
     'mla_kv_norm_g': 3.261,
     'moe_b_group': 16.63,
     'moe_b_router': 12.706,
     'final_norm_g': 24.539,
     'norm_ffn_g': 2.681,
     's5_a_im': 41.824,
     's5_log_step': 45.744,
     's5_b_re': 64.0,
     's5_b_im': 38.504,
     's5_c_re': 64.0,
     's5_c_im': 55.84}
    for name, (base, spread) in spreads.items():
        noise = np.random.default_rng([zlib.crc32(name.encode()), seed]).standard_normal(out[name].shape)
        drawn = base * np.exp(spread * noise) if base else spread * noise
        out[name] = jnp.asarray(drawn.astype(out[name].dtype))
    for name, factor in factors.items():
        out[name] = (out[name] * factor).astype(out[name].dtype)
    return out
```

```python
import math
from contextlib import ExitStack

import concourse.bass as bass
from concourse import mybir

F32 = mybir.dt.float32
I32 = mybir.dt.int32
ALU = mybir.AluOpType
ACT = mybir.ActivationFunctionType
AX = mybir.AxisListType
P = 128

D = 1024
KD = D // P
LAT, CTX = 512, 256
TOK = CTX + LAT
NT, NCT = TOK // P, CTX // P
NLT = LAT // P
GRID_W = 64
EPS = 1e-6
ROPE_BASE = 10000.0

S5W, GRP, NG, NS = 256, 16, 16, 64
NPAIR = NG // 2
CH = 8
NCH = TOK // CH
NCC = CTX // CH
NCL = LAT // CH
NPOW = CH + 1
KW = (2 * CH - 1) * GRP

DH, DHD = 4, 64
MH, MN, MR, MV = 4, 64, 32, 64
MQ = MN + MR
QRANK, KVRANK = 256, 128
DSCALE = DHD ** -0.5
MSCALE = MQ ** -0.5
LAM_INIT = 0.8 - 0.6 * math.exp(-0.3 * 0)

NE, EPG, NGR = 32, 8, 4
HID = D // 2
TOPK = 2
NBLK = NE + (LAT * TOPK - NE) // P
SLOT_NONE = 65535

MAGIC = 1.5 * 2.0 ** 23
TWO_PI_DOWN = 6.283185
INV_2PI = 1.0 / (2.0 * math.pi)

R_C, R_CC, R_BMOD, R_GMIX, R_GFFN = 0, 8, 16, 64, 72
R_SD, R_BGLU, R_QN, R_KVN, R_SUB, R_ARE, R_AIM, NROW = 80, 82, 84, 86, 87, 88, 104, 120

M_SH, M_SC, M_G, F_SH, F_SC, F_G = range(6)

Z_Q, Z_K, Z_V, Z_M = 256, 768, 1280, 1792
Z_ALL = 2208


def stream_plan():
    mod = lambda term: [("mod", 2 * term), ("mod", 2 * term + 1)]
    first = mod(M_SH) + mod(M_SC) + [("in", Z_Q - S5W, S5W), ("in", Z_Q, 512), ("in", Z_K, 512), ("in", Z_V, 512),
                                     ("in", Z_M, Z_ALL - Z_M)]
    return first + mod(F_SH) + mod(F_SC) + mod(M_G) + mod(F_G) + [("out", 0), ("out", 1)]


def build(nc, a, out):
    ctx = ExitStack()
    sems = {}

    def sem(name):
        if name not in sems:
            sems[name] = ctx.enter_context(nc.semaphore(name))
        return sems[name]

    class Chain:

        def __init__(self, eng, name):
            self.eng, self.sem, self.n = eng, sem(name), 0

        def __call__(self, ins):
            self.n += 1
            ins.then_inc(self.sem, 1)
            return ins

        def settle(self):
            self.eng.wait_ge(self.sem, self.n)

    with ctx:
        def sb(name, shape, dt=F32):
            return ctx.enter_context(nc.sbuf_tensor(name, shape, dt))

        RING = 3
        W = sb("W", [P, RING, 4096])
        HTR = sb("HTR", [P, 6144])
        QKV = sb("QKV", [P, 8192])
        MP = sb("MP", [P, 7168])
        S5R = sb("S5R", [P, 9984])
        ZR = sb("ZR", [P, 1984])
        CST = sb("CST", [P, 3 * P])
        ident, ones, tri = CST[:, 0:P], CST[:, P:2 * P], CST[:, 2 * P:3 * P]
        rows = sb("rows", [P, P])
        cols = sb("cols", [P, NROW])
        silu_c = sb("silu_c", [P, KD, 2])
        silu_t = sb("silu_t", [P, 2 * KD])
        silu_cb = S5R[:, 8704:9728].rearrange("p (k n) -> p k n", k=KD)
        modrow = S5R[0:2, 7680:8704].rearrange("p (b n) -> p b n", b=2)
        modc = sb("modc", [P, 48, 2])
        gmc = sb("gmc", [P, KD, 2])
        gfc = sb("gfc", [P, KD])
        GM = sb("GM", [P, D])
        wglu = sb("wglu", [P, 2, S5W])
        wuq = sb("wuq", [P, 2, MH * MQ])
        wukv = sb("wukv", [P, MH * (MN + MV)])
        wrt = sb("wrt", [P, KD, NGR + NE])
        brt = sb("brt", [P, NGR + NE])
        lamr = S5R[:, 0:4 * DHD]
        sml = sb("sml", [P, 512])
        turn = sb("turn", [P, 3, NLT, 48])
        freq = sb("freq", [P, 24])
        pos_i = sb("pos_i", [P, 2, NLT], I32)
        pos_f = sb("pos_f", [P, 2, NLT])
        lst = sb("lst", [16, 2])
        lsb = sb("lsb", [16, 2, NS])
        mul_i = sb("mul_i", [P, 2, NPOW + NCH], I32)
        mul_f = sb("mul_f", [P, 2, NPOW + NCH])
        s5p = sb("s5p", [P, 12, 16])
        epsb = sb("epsb", [P, 1])
        QR = sb("QR", [P, 2, 512])
        io_i = sb("io_i", [P, NBLK], I32)
        io_f = sb("io_f", [P, NBLK])
        pair_i = sb("pair_i", [P, TOPK, NLT, 2], I32)
        slots = sb("slots", [P, NBLK, 2], I32)
        btab = sb("btab", [1, NBLK + 1], I32)
        pos_k = sb("pos_k", [P, TOPK, NLT], I32)
        gidx = sb("gidx", [P, 1], I32)
        sidx = sb("sidx", [P, 1], I32)
        held = sb("held", [1, 8])

        PS = ctx.enter_context(nc.psum_tensor("PS", [P, 4096], F32))

        def bank(b, n=512, off=0):
            return PS[:, 512 * b + off:512 * b + off + n]

        hT = HTR[:, :].rearrange("p (k t) -> p k t", k=KD)
        xs = QKV[:, 0:6144].rearrange("p (t d) -> p t d", t=NT)
        xh = MP[:, 5120:7168].rearrange("p (b d) -> p b d", b=2)
        QT = QKV[:, 0:2048].rearrange("p (h t) -> p h t", h=DH)
        KT = QKV[:, 2048:5120].rearrange("p (h t) -> p h t", h=DH)
        VV = QKV[:, 5120:8192].rearrange("p (t e) -> p t e", t=NT)
        mix = MP[:, 0:4096].rearrange("p (k t) -> p k t", k=KD)
        pbuf = MP[:, 4096:7168].rearrange("p (b s) -> p b s", b=4)
        pT = HTR[:, :].rearrange("p (b k q) -> p b k q", b=2, k=NT)
        MQT = S5R[:, 0:2048].rearrange("p (h t) -> p h t", h=MH)
        MKT = S5R[:, 2048:5120].rearrange("p (h t) -> p h t", h=MH)
        MVV = S5R[:, 5120:6656].rearrange("p (t e) -> p t e", t=NT)
        sq = S5R[:, 6656:7168]
        rms = S5R[:, 7168:7680]
        CQT = ZR[:, 0:1024].rearrange("p (k t) -> p k t", k=2)
        CKVT = ZR[:, 1024:1792]
        KR = ZR[:, 1792:1984].rearrange("p (t r) -> p t r", t=NT)
        UT = S5R[:, 0:1536].rearrange("p (h j c) -> p h j c", h=2, j=CH)
        UU = S5R[:, 1536:3072].rearrange("p (g c) -> p g c", g=NG)
        yacc = S5R[:, 3072:4096].rearrange("p (g c) -> p g c", g=NG)
        CL = S5R[:, 4096:6400].rearrange("p (r q k n) -> p r q k n", r=2, q=NPAIR, k=NPOW)
        PBT = S5R[:, 6400:8448].rearrange("p (r q s) -> p r q s", r=2, q=NPAIR)
        TPL = S5R[:, 6400:8448].rearrange("p (g m) -> p g m", g=NG)
        ECS = S5R[:, 8448:9984].rearrange("p (r q c) -> p r q c", r=2, q=NPAIR)
        X0 = 1024
        st1 = MP[:, X0:X0 + 1152]
        st2 = MP[:, X0 + 1152:X0 + 2304]
        PB = MP[:, X0 + 2304:X0 + 4352].rearrange("p (r q i n) -> p r q i n", r=2, q=NPAIR, i=CH)
        ksb = MP[0:2 * GRP, X0 + 2304:X0 + 3328].rearrange("p (q m) -> p q m", q=NPAIR)
        GG = MP[:, X0:X0 + 1536].rearrange("p (r q c) -> p r q c", r=2, q=NPAIR)
        gt1 = MP[:, X0 + 1536:X0 + 2304].rearrange("p (q c) -> p q c", q=NPAIR)
        gt2 = MP[:, X0 + 2304:X0 + 3072].rearrange("p (q c) -> p q c", q=NPAIR)
        HH = MP[:, X0 + 3072:X0 + 3072 + 2 * NPAIR * (NCH + 1)].rearrange("p (r q c) -> p r q c", r=2, q=NPAIR)
        BC = MP[:, 0:1024].rearrange("p (r q n) -> p r q n", r=4, q=16)
        cn = QR[:, :, :].rearrange("p b (i s) -> p (b i) s", i=4)
        YT = S5R[:, 6400:7424].rearrange("p (h j c) -> p h j c", h=2, j=CH)
        YG = S5R[:, 7424:8448].rearrange("p (h j c) -> p h j c", h=2, j=CH)
        yt1 = S5R[:, 8448:9472].rearrange("p (h j c) -> p h j c", h=2, j=CH)
        LP = MP[:, 6928:7072].rearrange("p (r q k) -> p r q k", r=2, q=NPAIR)
        EM = MP[:, 7072:7144].rearrange("p (q k) -> p q k", q=NPAIR)
        BBar = ZR[:, 0:512].rearrange("p (r q m) -> p r q m", r=2, q=NPAIR)
        XN = QKV[:, 0:4096].rearrange("p (t d) -> p t d", t=NLT)
        GF = QKV[:, 4096:5120]
        fng = QKV[:, 5120:6144]
        ot1 = QKV[:, 6144:7168]
        hfT = HTR[:, 0:4096].rearrange("p (k t) -> p k t", k=KD)
        xhf = S5R[:, 0:2048].rearrange("p (b d) -> p b d", b=2)
        hg = S5R[:, 2048:3072]
        hgT = S5R[:, 3072:4096].rearrange("p (k s) -> p k s", k=KD)
        hid = S5R[:, 4096:4608]
        hidT = S5R[:, 4608:5120].rearrange("p (k s) -> p k s", k=4)
        ysb = S5R[:, 5120:6144]
        sg = S5R[:, 6144:6656]
        rt = S5R[:, 6656:9984]
        logit = rt[:, 0:144].rearrange("p (t e) -> p t e", t=NLT)
        mask = rt[:, 144:272].rearrange("p (t e) -> p t e", t=NLT)
        oneh = rt[:, 272:528].rearrange("p (k t e) -> p k t e", k=TOPK, t=NLT)
        emsk = rt[:, 528:656].rearrange("p (t e) -> p t e", t=NLT)
        ra = rt[:, 656:784].rearrange("p (t e) -> p t e", t=NLT)
        rb = rt[:, 784:912].rearrange("p (t e) -> p t e", t=NLT)
        tri_inc, tri128 = rt[:, 1000:1032], rt[:, 1032:1064]
        nb_b, nbv, endv = rt[:, 1064:1192], rt[:, 1192:1193], rt[:, 1193:1194]
        nbt = rt[:, 1194:1198]
        cmpb = rt[:, 1200:1200 + NBLK + 1]
        goh = rt[:, 1260:1276].rearrange("p (t g) -> p t g", t=NLT)
        gra = rt[:, 1276:1292].rearrange("p (t g) -> p t g", t=NLT)
        gidxf = rt[:, 1292:1308].rearrange("p (t g) -> p t g", t=NLT)
        junk = rt[:, 2304:3328]
        rp = MP[:, 5648:6672].rearrange("p (i n) -> p i n", i=4)
        jk = MP[:, 6672:6928]
        wts = sb("wts", [P, 8, NLT])
        yk = MP[:, 0:4096].rearrange("p (b k d) -> p b k d", b=2, k=TOPK)
        fin = MP[:, 4096:6144].rearrange("p (b d) -> p b d", b=2)

        def dram(name, shape, dt=F32):
            return nc.dram_tensor(name, shape, dt).ap()

        u_d = dram("u_d", [2 * P, CH, NCH])
        k_d = dram("k_d", [2, 2 * GRP, NPAIR, KW])
        y_d = dram("y_d", [2 * P, CH, NCL])
        xh_d = dram("xh_d", [LAT, D])
        slot_d = dram("slot_d", [NBLK * P, 2], I32)
        pair_d = dram("pair_d", [TOPK * LAT, D])

        plan = stream_plan()
        NL = len(plan)
        at = {what: n for n, what in enumerate(plan)}
        W1S, W3S, W2S = NL % RING, (NL + 1) % RING, (NL + 2) % RING
        w1s = W[:, W1S, :].rearrange("p (k h) -> p k h", k=KD)
        w3s = W[:, W3S, :].rearrange("p (k h) -> p k h", k=KD)
        w2s = W[:, W2S, :].rearrange("p (k d) -> p k d", k=4)

        def wslot(n, width=512):
            return W[:, n % RING, 0:KD * width].rearrange("p (k n) -> p k n", k=KD)

        ztiles = [("u", h) for h in range(4)]
        ztiles += [("q", t) for t in range(NCT, NT)] + [("k", t) for t in range(NT)]
        ztiles += [("v", t) for t in range(NT)] + [("m", t) for t in range(NT)]
        ztiles += [("uq", t) for t in range(NCT, NT)] + [("ukv", t) for t in range(NT)]
        zi = {w: n for n, w in enumerate(ztiles)}
        turns = [w for w in ztiles if w[0] in ("q", "k", "m", "uq", "ukv")]
        ti = {w: n for n, w in enumerate(turns)}

        blocks = [("d", h, t) for h in range(DH) for t in range(NLT)] + [("l", h, t) for h in range(MH) for t in range(NLT)]
        units = [(b, m) for b, w in enumerate(blocks) for m in range(2 if w[0] == "d" else 1)]
        unit0 = {b: min(u for u, (bb, _) in enumerate(units) if bb == b) for b in range(len(blocks))}
        NHD = DH + MH
        late = [(F_SH, 0), (F_SH, 1), (F_SC, 0), (F_SC, 1), (M_G, 0), (M_G, 1), (F_G, 0), (F_G, 1)]
        late_at = {2 + 3 * n: w for n, w in enumerate(late)}
        LG = {}
        n7 = 0
        for b in range(len(blocks)):
            if b in late_at:
                LG[("mod", b)] = n7
                n7 += 1
            if b >= 4 and b % 4 == 0 and b // 4 - 1 < DH:
                LG[("rms", b // 4 - 1)] = n7
                n7 += 1

        def used(n):
            what = plan[n]
            if what[0] == "out":
                return sem("op"), 2 * NLT
            if what[0] == "in":
                kind = "uqkvm"[[Z_Q - S5W, Z_Q, Z_K, Z_V, Z_M].index(what[1])]
                return sem("z"), max(i for w, i in zi.items() if w[0] == kind) + 1
            two = [m for m in plan if m[0] == "mod" and m[1] // 2 in (M_SH, M_SC, F_SH, F_SC)]
            one = [m for m in plan if m[0] == "mod" and m[1] // 2 in (M_G, F_G)]
            return (sem("mod_two"), two.index(what) + 1) if what in two else (sem("mod_wide"), one.index(what) + 1)

        block = ctx.enter_context(nc.Block())

        @block.sync
        def _(sp):
            for t in range(NT):
                src = a["ctx"][0, t * P:(t + 1) * P, :] if t < NCT else a["x"][0, (t - NCT) * P:(t - NCT + 1) * P, :]
                sp.dma_start(xs[:, t, :], src).then_inc(sem(f"x_in{t}"), 16)

            for n, what in enumerate(plan):
                if n >= RING:
                    sp.wait_ge(*used(n - RING))
                if what == ("out", 1):
                    sp.wait_ge(sem("scores"), unit0[DH * NLT])
                    for t in range(NLT):
                        sp.dma_start(XN[:, t, :], a["x"][0, t * P:(t + 1) * P, :]).then_inc(sem("xr_in"), 16)
                    sp.dma_start(GF, a["b_mod"][0][F_G * D:(F_G + 1) * D].partition_broadcast(P)).then_inc(sem("gf_in"), 16)
                if what[0] == "mod":
                    src = a["w_mod"][0][:, 512 * what[1]:512 * (what[1] + 1)]
                elif what[0] == "in":
                    src = a["w_in"][0][:, what[1]:what[1] + what[2]]
                else:
                    src = a["w_out"][0][:, 512 * what[1]:512 * (what[1] + 1)]
                sp.dma_start(wslot(n, src.shape[1]), src.rearrange("(k p) n -> p k n", p=P)).then_inc(
                    sem(f"ring_in{n % RING}"), 16)
            sp.wait_ge(sem("pv"), DH)
            sp.dma_start(fng, a["final_norm_g"].partition_broadcast(P)).then_inc(sem("fng_in"), 16)

            sp.wait_ge(sem("routed"), 1)
            last2 = sp.value_load(btab[0:1, NBLK:NBLK + 1], min_val=LAT * TOPK // P - 2, max_val=NBLK - 2)

            def load(dst, name, b, used, loaded, count):
                e = sp.value_load(btab[0:1, b:b + 1] if isinstance(b, int) else btab[0:1, bass.ds(b, 1)],
                                  min_val=0, max_val=NE - 1)
                if used is not None:
                    sp.wait_ge(sem(used), count)
                src = a[name][0][bass.ds(e, 1)].rearrange("e (k p) n -> p (e k) n", p=P)
                sp.dma_start(dst, src).then_inc(sem(loaded), 16)

            sp.wait_ge(sem("op"), 2 * NLT)
            load(w1s, "moe_w1", 0, None, "w1_in", 0)
            load(w3s, "moe_w3", 0, None, "w3_in", 0)
            load(w2s, "moe_w2", 0, None, "w2_in", 0)
            load(w1s, "moe_w1", 1, "w1_used", "w1_in", 1)
            load(w3s, "moe_w3", 1, "w3_used", "w3_in", 1)
            with sp.Fori(2, last2 + 2) as b:
                load(w1s, "moe_w1", b, "w1_used", "w1_in", b)
                load(w3s, "moe_w3", b, "w3_used", "w3_in", b)
                load(w2s, "moe_w2", b - 1, "w2_used", "w2_in", b - 1)
            load(w2s, "moe_w2", last2 + 1, "w2_used", "w2_in", last2 + 1)

            sp.wait_ge(sem("moe_done"), 1)
            for t in range(NLT):
                if t >= 2:
                    sp.wait_ge(sem("x_out"), t - 1)
                for k in range(TOPK):
                    sp.dma_start(yk[:, t % 2, k, :], pair_d[k * LAT + t * P:k * LAT + (t + 1) * P, :]).then_inc(
                        sem(f"yk_in{t % 2}"), 16)
            for t in range(NLT):
                sp.wait_ge(sem("fin"), t + 1)
                sp.dma_start(out[0, t * P:(t + 1) * P, :], fin[:, t % 2, :]).then_inc(sem(f"out_done{t % 2}"), 16)
            for par in range(2):
                sp.wait_ge(sem(f"out_done{par}"), 16 * NLT // 2)

        @block.gpsimd
        def _(pool):
            st = Chain(pool, "pool_steps")
            st(pool.memset(CST[:, 0:P], 0.0))
            st(pool.memset(ones, 1.0))
            st(pool.memset(epsb[:, :], EPS))
            st(pool.memset(held[:, :], 0.0))
            st.settle()
            st(pool.affine_select(out=ident, in_=ident, compare_op=ALU.not_equal, fill=1.0, base=0,
                                  pattern=[[-1, P]], channel_multiplier=1))
            st(pool.affine_select(out=tri, in_=ones, compare_op=ALU.is_gt, fill=0.0, base=0,
                                  pattern=[[1, P]], channel_multiplier=-1))
            for nf, off in ((16, 0), (8, 16)):
                for i in range(nf):
                    st(pool.memset(freq[:, off + i:off + i + 1], float(ROPE_BASE ** (-i / nf) * INV_2PI)))
            for half in range(2):
                r = slice(64 * half, 64 * half + 64)
                st.settle()
                st(pool.iota(pos_i[r, 0, :], pattern=[[2, NLT]], base=half, channel_multiplier=0))
                st(pool.iota(pos_i[r, 1, :], pattern=[[0, NLT]], base=0, channel_multiplier=1))
            st.settle()
            for d in range(2):
                st(pool.iota(mul_i[:, d, 0:NPOW], pattern=[[1 if d == 0 else -1, NPOW]], base=0 if d == 0 else CH,
                             channel_multiplier=0))
            st(pool.iota(mul_i[:, 0, NPOW:], pattern=[[CH, NCH]], base=0, channel_multiplier=0))
            st(pool.iota(mul_i[:, 1, NPOW:NPOW + NCC], pattern=[[-CH, NCC]], base=CH * (NCC - 1), channel_multiplier=0))
            st(pool.iota(mul_i[:, 1, NPOW + NCC:], pattern=[[-CH, NCL]], base=CH * (NCH - 1), channel_multiplier=0))
            st(pool.iota(io_i[:, :], pattern=[[1, NBLK]], base=0, channel_multiplier=0))
            for k in range(TOPK):
                st(pool.iota(pair_i[:, k, :, 0], pattern=[[P, NLT]], base=0, channel_multiplier=1))
                st(pool.iota(pair_i[:, k, :, 1], pattern=[[P, NLT]], base=k * LAT, channel_multiplier=1))
            st(pool.memset(slots[:, :, :], SLOT_NONE))
            st.settle()
            pool.memset(epsb[:, :], EPS).then_inc(sem("consts"), 1)
            pool.dma_start(slot_d.rearrange("(r b) c -> r b c", r=P), slots[:, :, :]).then_inc(sem("slots_clear"), 16)
            pool.memset(S5R[0:2 * GRP, 4096:4096 + 7 * NPAIR * GRP], 0.0).then_inc(sem("kz"), 1)
            pool.wait_ge(sem("kz"), 1)
            kz = S5R[0:2 * GRP, 4096:4096 + 7 * NPAIR * GRP].rearrange("p (q m) -> p q m", q=NPAIR)
            pool.dma_start(k_d[0][:, :, 0:7 * GRP], kz).then_inc(sem("kpad_clear"), 16)
            pool.dma_start(k_d[1][:, :, 8 * GRP:15 * GRP], kz).then_inc(sem("kpad_clear"), 16)

            pool.wait_ge(sem("z_free"), 4)
            for h in range(2):
                pool.dma_start(u_d[h * P:(h + 1) * P], UT[:, h]).then_inc(sem("u_out"), 16)
            pool.wait_ge(sem("u_out"), 32)
            uv = u_d.rearrange("(g n) j c -> j n g c", n=GRP)
            for i in range(CH):
                pool.dma_start(UU[GRP * i:GRP * (i + 1)], uv[CH - 1 - i]).then_inc(sem("u_in"), 16)
            pool.wait_ge(sem("kpad_clear"), 32)
            for d in range(2):
                pool.wait_ge(sem("ksb"), 2 * (d + 1))
                lo = (7 if d == 0 else 0) * GRP
                pool.dma_start(k_d[d][:, :, lo:lo + P], ksb).then_inc(sem("k_out"), 16)
                pool.wait_ge(sem("k_out"), 16 * (d + 1))
                pool.wait_ge(sem("bu"), 4 * (d + 1))
                for i in range(CH):
                    pool.dma_start(TPL[GRP * i:GRP * (i + 1)].rearrange("n (q g) m -> n q g m", g=2),
                                   k_d[d].rearrange("(g n) q m -> n q g m", g=2)[:, :, :, GRP * i:GRP * i + P]).then_inc(
                        sem("t_in"), 16)
            pool.wait_ge(sem("yacc"), 4)
            yv = y_d.rearrange("(g n) j c -> j n g c", n=GRP)
            for j in range(CH):
                pool.dma_start(yv[j], yacc[GRP * j:GRP * (j + 1)]).then_inc(sem("y_out"), 16)
            pool.wait_ge(sem("y_out"), 16 * CH)
            for h in range(2):
                pool.dma_start(YT[:, h], y_d[h * P:(h + 1) * P]).then_inc(sem("y_in"), 16)

            for t in range(NLT):
                pool.wait_ge(sem("xhf"), t + 1)
                pool.dma_start(xh_d[t * P:(t + 1) * P, :], xhf[:, t % 2, :]).then_inc(sem(f"xh_out{t % 2}"), 16)
            pool.memset(hg, 0.0).then_inc(sem("hg_clear"), 1)
            pool.wait_ge(sem("slots_clear"), 16)
            pool.wait_ge(sem("pos_k"), 1)
            for k in range(TOPK):
                for t in range(NLT):
                    pool.indirect_dma_start(slot_d, bass.IndirectOffsetOnAxis(pos_k[:, k, t:t + 1], 0),
                                            pair_i[:, k, t, :], None, bounds_check=NBLK * P - 1,
                                            oob_is_err=False).then_inc(sem("slot_out"), 16)
            pool.wait_ge(sem("slot_out"), 16 * TOPK * NLT)
            pool.dma_start(slots[:, :, :], slot_d.rearrange("(r b) c -> r b c", r=P)).then_inc(sem("slot_in"), 16)
            pool.wait_ge(sem("slot_in"), 16)
            pool.wait_ge(sem("routed"), 1)
            pool.wait_ge(sem("hg_clear"), 1)
            for par in range(2):
                pool.wait_ge(sem(f"xh_out{par}"), 16 * NLT // 2)
            last2 = pool.value_load(btab[0:1, NBLK:NBLK + 1], min_val=LAT * TOPK // P - 2, max_val=NBLK - 2)

            cells = {}

            def hold(sm, count):
                pool.wait_ge(sm, count)
                if not isinstance(count, int):
                    cell = cells.setdefault(sm.name, len(cells) + 1)
                    pool.tensor_tensor(held[:, cell:cell + 1], held[:, 0:1], held[:, 0:1], ALU.add)

            def entry(b, c):
                return slots[:, b:b + 1, c] if isinstance(b, int) else slots[:, bass.ds(b, 1), c]

            def gather(b):
                pool.tensor_copy(gidx[:, :], entry(b, 0)).then_inc(sem("gidx"), 1)
                hold(sem("gidx"), b + 1)
                pool.indirect_dma_start(hg, None, xh_d, bass.IndirectOffsetOnAxis(gidx[:, 0:1], 0),
                                        bounds_check=LAT - 1, oob_is_err=False).then_inc(sem("hg_in"), 16)

            def scatter(b):
                if not isinstance(b, int):
                    hold(sem("y_sc"), 16 * b)
                pool.tensor_copy(sidx[:, :], entry(b, 1)).then_inc(sem("sidx"), 1)
                hold(sem("sidx"), b + 1)
                hold(sem("ysb"), 2 * b + 2)
                pool.indirect_dma_start(pair_d, bass.IndirectOffsetOnAxis(sidx[:, 0:1], 0), ysb, None,
                                        bounds_check=TOPK * LAT - 1, oob_is_err=False).then_inc(sem("y_sc"), 16)

            gather(0)
            hold(sem("hg_tr"), 1)
            gather(1)
            hold(sem("hg_tr"), 2)
            gather(2)
            scatter(0)
            with pool.Fori(1, last2) as b:
                hold(sem("hg_tr"), b + 2)
                gather(b + 2)
                scatter(b)
            scatter(last2)
            scatter(last2 + 1)
            hold(sem("y_sc"), 16 * (last2 + 2))
            pool.memset(gidx[:, :], 0).then_inc(sem("moe_done"), 1)

        @block.tensor
        def _(pe):
            mm, tr = pe.matmul, pe.transpose
            pe.wait_ge(sem("consts"), 1)
            pe.wait_ge(sem("rows_in"), 16 * 12)
            tr(bank(0, NROW), rows[0:NROW, :], ident[0:NROW, 0:NROW]).then_inc(sem("cols_t"), 1)
            pe.wait_ge(sem("lsb"), 1)
            tr(bank(4, 16), lsb[:, :, :].rearrange("p g s -> p (g s)"), ident[0:16, 0:16]).then_inc(sem("ls_t"), 1)

            def ring_wait(n):
                pe.wait_ge(sem(f"ring_in{n % RING}"), 16 * (n // RING + 1))

            def mod_rows(n, dst, wide):
                ring_wait(n)
                for k in range(KD):
                    ins = mm(dst, silu_cb[:, k, :] if wide else silu_c[:, k, :], wslot(n)[:, k, :],
                             start=(k == 0), stop=(k == KD - 1))
                ins.then_inc(sem("mod_wide" if wide else "mod_two"), 1)

            def turn_mod(i, b):
                pe.wait_ge(sem("modrow"), i + 1)
                for j in range(4):
                    ins = tr(bank(b, 2, 2 * j), modrow[:, i % 2, j * P:(j + 1) * P], ident[0:2, 0:2])
                ins.then_inc(sem("modt"), 1)

            pe.wait_ge(sem("silu_c"), 1)
            for n in range(4):
                if n >= 2:
                    pe.wait_ge(sem("modrow"), n - 1)
                mod_rows(n, PS[0:2, 512 * (6 + n % 2):512 * (7 + n % 2)], False)
                if n >= 1:
                    pe.wait_ge(sem("modc"), n)
                turn_mod(n, 5)

            for t in range(NT):
                pe.wait_ge(sem("xh"), t + 1)
                if t >= 2:
                    pe.wait_ge(sem("hT_a"), t - 1)
                    pe.wait_ge(sem("hT_d"), t - 1)
                for k in range(KD):
                    ins = tr(bank(2 * (t % 2) + k // 4, P, (k % 4) * P), xh[:, t % 2, k * P:(k + 1) * P], ident)
                ins.then_inc(sem("xh_tr"), 1)
            pe.wait_ge(sem("hT_a"), NT)
            pe.wait_ge(sem("hT_d"), NT)

            def z_bank(w):
                n = zi[w]
                if n >= 4:
                    pe.wait_ge(sem("z_free"), n - 3)
                return bank(n % 4)

            n = at[("in", 0, S5W)]
            ring_wait(n)
            for h in range(4):
                dst = z_bank(("u", h))
                t0, nt = (0, 512) if h % 2 == 0 else (512, 256)
                for k in range(KD):
                    ins = mm(dst[:, 0:nt], wslot(n, S5W)[:, k, (h // 2) * P:(h // 2 + 1) * P], hT[:, k, t0:t0 + nt],
                             start=(k == 0), stop=(k == KD - 1))
                ins.then_inc(sem("z"), 1)

            pe.wait_ge(sem("cn_in"), 16 * 4)
            for i in range(8):
                ins = tr(bank(6 + i // 4, P, (i % 4) * P), cn[:, i, :], ident)
            ins.then_inc(sem("ct_t"), 1)
            pe.wait_ge(sem("bc"), 1)

            def turn_tile(w):
                n = ti[w]
                pe.wait_ge(sem("qr"), n + 1)
                if n >= 2:
                    pe.wait_ge(sem("turned_out"), n - 1)
                b = 4 + n % 2
                src = QR[:, n % 2, :]
                if w[0] in ("q", "k"):
                    for h in range(DH):
                        ins = tr(bank(b, P, h * P), src[:, h * P:(h + 1) * P], ident)
                elif w[0] == "m":
                    lat = w[1] >= NCT
                    for j in range(0 if lat else 2, 3):
                        ins = tr(bank(b, P, j * P), src[:, j * P:(j + 1) * P], ident)
                else:
                    for h in range(MH):
                        ins = tr(PS[0:MQ, 512 * b + h * P:512 * b + (h + 1) * P], src[:, h * MQ:(h + 1) * MQ], ident)
                ins.then_inc(sem("turned"), 1)

            def project(kind, t):
                w = (kind, t)
                dst = z_bank(w)
                tok = slice(t * P, (t + 1) * P)
                if kind in "qkvm":
                    col, width = {"q": (Z_Q, 512), "k": (Z_K, 512), "v": (Z_V, 512), "m": (Z_M, Z_ALL - Z_M)}[kind]
                    n = at[("in", col, width)]
                    ring_wait(n)
                    c0 = QRANK if kind == "m" and t < NCT else 0
                    for k in range(KD):
                        ins = mm(dst[:, c0:width], hT[:, k, tok], wslot(n, width)[:, k, c0:width],
                                 start=(k == 0), stop=(k == KD - 1))
                elif kind == "uq":
                    lt = slice((t - NCT) * P, (t - NCT + 1) * P)
                    for k in range(2):
                        ins = mm(dst[:, 0:MH * MQ], CQT[:, k, lt], wuq[:, k, :], start=(k == 0), stop=(k == 1))
                else:
                    ins = mm(dst, CKVT[:, tok], wukv[:, :], start=True, stop=True)
                ins.then_inc(sem("z"), 1)

            def group(kind, first):
                for t in range(first, NT):
                    project(kind, t)
                    if t > first and (kind, t) in ti:
                        turn_tile((kind, t - 1))
                if (kind, NT - 1) in ti:
                    turn_tile((kind, NT - 1))

            def s5_inputs(d):
                pe.wait_ge(sem("pb"), d + 1)
                for c in range(4):
                    n4 = 4 * d + c
                    if n4 >= 1:
                        pe.wait_ge(sem("pbt"), n4)
                    for j in range(4):
                        r, q = divmod(4 * c + j, NPAIR)
                        ins = tr(bank(6, P, j * P), PB[:, r, q].rearrange("p i n -> p (i n)"), ident)
                    ins.then_inc(sem("pb_t"), 1)
                pe.wait_ge(sem("cl"), d + 1)
                k0 = 0 if d == 0 else 1
                for c in range(2):
                    n2 = 2 * d + c
                    if n2 >= 1:
                        pe.wait_ge(sem("ksb"), n2)
                    for j in range(4):
                        q = 4 * c + j
                        for r in range(2):
                            ins = mm(PS[0:2 * GRP, 3584 + j * P:3584 + (j + 1) * P], BBar[:, r, q, :],
                                     CL[:, r, q, k0:k0 + CH, :].rearrange("p k n -> p (k n)"),
                                     start=(r == 0), stop=(r == 1))
                    ins.then_inc(sem("kk"), 1)
                pe.wait_ge(sem("pbt"), 4 * (d + 1))
                pe.wait_ge(sem("u_in"), 16 * CH)
                for c in range(4):
                    r, hq = divmod(c, 2)
                    n4 = 4 * d + c
                    if n4 >= 1:
                        pe.wait_ge(sem("bu_out"), n4)
                    for j in range(4):
                        q = 4 * hq + j
                        for g2 in range(2):
                            ins = mm(PS[NS * g2:NS * g2 + NS, 512 * 6 + j * NCH:512 * 6 + (j + 1) * NCH],
                                     PBT[:, r, q, NS * g2:NS * g2 + NS], UU[:, 2 * q + g2, :], start=True, stop=True)
                    ins.then_inc(sem("bu"), 1)

            def s5_outputs(d):
                pe.wait_ge(sem("t_in"), 16 * CH * (d + 1))
                pe.wait_ge(sem("hh"), d + 1)
                k0, c0 = (1, NCC - 1) if d == 0 else (0, NCC + 1)
                for g2 in range(2):
                    if d == 1:
                        pe.wait_ge(sem("yacc"), 2)
                    s = slice(NS * g2, NS * g2 + NS)
                    for q in range(NPAIR):
                        dst = bank(7 - g2, NCL, q * NCL)
                        mm(dst, TPL[:, 2 * q + g2, :], UU[:, 2 * q + g2, NCC:NCH], start=True, stop=False)
                        for r in range(2):
                            ins = mm(dst, CL[s, r, q, k0:k0 + CH, :].rearrange("p k n -> p (k n)"),
                                     HH[s, r, q, c0:c0 + NCL], start=False, stop=(r == 1))
                    ins.then_inc(sem("yy"), 1)

            group("q", NCT)
            s5_inputs(0)
            group("k", 0)
            s5_outputs(0)
            group("v", 0)
            pe.wait_ge(sem("yacc"), 2)
            s5_inputs(1)
            group("m", 0)
            s5_outputs(1)

            pe.wait_ge(sem("yg"), 1)
            pe.wait_ge(sem("small_in"), 16 * 7)
            pe.wait_ge(sem("yacc"), 4)
            for mo in range(2):
                for k in range(2):
                    ins = mm(bank(6 + mo), wglu[:, k, mo * P:(mo + 1) * P], YG[:, k].rearrange("p j c -> p (j c)"),
                             start=(k == 0), stop=(k == 1))
            ins.then_inc(sem("glu"), 1)

            pe.wait_ge(sem("turned_out"), ti[("m", NT - 1)] + 1)
            pe.wait_ge(sem("s5_mix"), 2)
            group("uq", NCT)
            group("ukv", 0)
            pe.wait_ge(sem("turned_out"), len(turns))
            pe.wait_ge(sem("z_free"), len(ztiles))

            def scores(b):
                kind, h, t = blocks[b]
                for m in range(2 if kind == "d" else 1):
                    u = unit0[b] + m
                    if u >= 2:
                        pe.wait_ge(sem("probs"), u - 1)
                    if kind == "d":
                        s, kt, qt = slice(DHD * m, DHD * m + DHD), KT, QT
                    else:
                        s, kt, qt = slice(0, MQ), MKT, MQT
                    base = 1024 * (u % 2)
                    for k0, kn in ((0, 512), (512, TOK - 512)):
                        ins = mm(PS[:, base + k0:base + k0 + kn], qt[s, h, t * P:(t + 1) * P], kt[s, h, k0:k0 + kn],
                                 start=True, stop=True)
                    ins.then_inc(sem("scores"), 1)

            def turn_probs(b):
                pe.wait_ge(sem("pc"), b + 1)
                if b >= 1:
                    pe.wait_ge(sem("pt_out"), b)
                kind, h, t = blocks[b]
                src = pbuf[:, 2 * (b % 2) + (1 if kind == "d" else 0), :]
                for k in range(NT):
                    ins = tr(PS[:, 2048 + k * P:2048 + (k + 1) * P], src[:, k * P:(k + 1) * P], ident)
                ins.then_inc(sem("pt"), 1)

            def values(hd):
                pe.wait_ge(sem("pt_out"), 4 * hd + 4)
                if hd >= 1:
                    pe.wait_ge(sem("o_free"), hd)
                for k in range(NT):
                    lhs = VV[:, k, hd * P:(hd + 1) * P] if hd < DH else MVV[:, k, ((hd - DH) // 2) * P:((hd - DH) // 2 + 1) * P]
                    ins = mm(bank(6), lhs, pT[:, hd % 2, k, :], start=(k == 0), stop=(k == NT - 1))
                ins.then_inc(sem("pv"), 1)

            def bank7(key):
                if LG[key] >= 1:
                    pe.wait_ge(sem("b7_free"), LG[key])

            pe.wait_ge(sem("silu_cb"), 1)
            scores(0)
            for b in range(len(blocks)):
                if b + 1 < len(blocks):
                    scores(b + 1)
                if b in late_at:
                    term, half = late_at[b]
                    wide = term in (M_G, F_G)
                    bank7(("mod", b))
                    mod_rows(at[("mod", 2 * term + half)], bank(7) if wide else PS[0:2, 3584:4096], wide)
                turn_probs(b)
                if b in late_at and not wide:
                    turn_mod(4 + late.index(late_at[b]), 7)
                if b % 4 == 0 and b >= 4:
                    values(b // 4 - 1)
                    if b // 4 - 1 < DH:
                        bank7(("rms", b // 4 - 1))
                        pe.wait_ge(sem("sq"), b // 4)
                        mm(bank(7), ones, sq, start=True, stop=True).then_inc(sem("ssum"), 1)
            values(NHD - 1)

            pe.wait_ge(sem("o_free"), NHD)
            for t in range(NLT):
                for half in range(2):
                    n = at[("out", half)]
                    if t == 0:
                        ring_wait(n)
                    i = 2 * t + half
                    if i >= 4:
                        pe.wait_ge(sem("xn"), i - 3)
                    for k in range(KD):
                        ins = mm(bank(i % 4), mix[:, k, t * P:(t + 1) * P], wslot(n)[:, k, :], start=(k == 0), stop=(k == KD - 1))
                    ins.then_inc(sem("op"), 1)
            for t in range(NLT):
                pe.wait_ge(sem("xhf"), t + 1)
                if t >= 2:
                    pe.wait_ge(sem("hfT_a"), t - 1)
                    pe.wait_ge(sem("hfT_d"), t - 1)
                for k in range(KD):
                    ins = tr(bank(4 + 2 * (t % 2) + k // 4, P, (k % 4) * P), xhf[:, t % 2, k * P:(k + 1) * P], ident)
                ins.then_inc(sem("xhf_tr"), 1)
            pe.wait_ge(sem("xn"), 2 * NLT)
            for t in range(NLT):
                pe.wait_ge(sem("hfT_a"), t + 1)
                pe.wait_ge(sem("hfT_d"), t + 1)
                for k in range(KD):
                    ins = mm(bank(0, NGR + NE, t * (NGR + NE)), hfT[:, k, t * P:(t + 1) * P], wrt[:, k, :],
                             start=(k == 0), stop=(k == KD - 1))
            ins.then_inc(sem("logits"), 1)
            pe.wait_ge(sem("mask"), 1)
            for t in range(NLT):
                ins = mm(PS[0:NE, 2560:2561], mask[:, t, :], ones[:, 0:1], start=(t == 0), stop=(t == NLT - 1))
            ins.then_inc(sem("cnt"), 1)
            pe.wait_ge(sem("nb"), 1)
            mm(PS[0:NE, 2562:2563], tri_inc[0:NE, :], nbv[0:NE, 0:1], start=True, stop=True).then_inc(sem("ends"), 1)
            for t in range(NLT):
                dst = bank(6, NE, t * NE)
                mm(dst, nb_b[0:NE, :], tri128[0:NE, :], start=True, stop=False)
                for t2 in range(t):
                    mm(dst, ones, mask[:, t2, :], start=False, stop=False)
                ins = mm(dst, tri, mask[:, t, :], start=False, stop=True)
            ins.then_inc(sem("place"), 1)
            pe.wait_ge(sem("cmp"), 1)
            mm(PS[0:1, 3584:3584 + NBLK + 1], ones[0:NE, 0:1], cmpb[0:NE, :], start=True, stop=True).then_inc(sem("bt"), 1)

            pe.wait_ge(sem("routed"), 1)
            last2 = pe.value_load(btab[0:1, NBLK:NBLK + 1], min_val=LAT * TOPK // P - 2, max_val=NBLK - 2)

            def turn_rows(b):
                pe.wait_ge(sem("hg_in"), 16 * b + 16)
                if not isinstance(b, int) or b >= 1:
                    pe.wait_ge(sem("hgT_a"), b)
                    pe.wait_ge(sem("hgT_d"), b)
                for k in range(KD):
                    ins = tr(bank(k // 4, P, (k % 4) * P), hg[:, k * P:(k + 1) * P], ident)
                ins.then_inc(sem("hg_tr"), 1)

            def up(b):
                pe.wait_ge(sem("hgT_a"), b + 1)
                pe.wait_ge(sem("hgT_d"), b + 1)
                first = isinstance(b, int) and b == 0
                if not first:
                    pe.wait_ge(sem("hid"), b)
                pe.wait_ge(sem("w1_in"), 16 * b + 16)
                for k in range(KD):
                    ins = mm(bank(2), hgT[:, k, :], w1s[:, k, :], start=(k == 0), stop=(k == KD - 1))
                ins.then_inc(sem("w1_used"), 1)
                pe.wait_ge(sem("w3_in"), 16 * b + 16)
                for k in range(KD):
                    ins = mm(bank(3), hgT[:, k, :], w3s[:, k, :], start=(k == 0), stop=(k == KD - 1))
                ins.then_inc(sem("w3_used"), 1)

            def turn_hid(b):
                pe.wait_ge(sem("hid"), b + 1)
                for k in range(4):
                    ins = tr(bank(4, P, k * P), hid[:, k * P:(k + 1) * P], ident)
                ins.then_inc(sem("hid_t"), 1)

            def down(b):
                pe.wait_ge(sem("hidT"), b + 1)
                pe.wait_ge(sem("w2_in"), 16 * b + 16)
                if not isinstance(b, int) or b >= 1:
                    pe.wait_ge(sem("ysb"), 2 * b)
                for n in range(2):
                    for k in range(4):
                        ins = mm(bank(5 + n), hidT[:, k, :], w2s[:, k, 512 * n:512 * (n + 1)], start=(k == 0), stop=(k == 3))
                ins.then_inc(sem("w2_used"), 1)

            turn_rows(0)
            up(0)
            turn_rows(1)
            turn_hid(0)
            up(1)
            turn_rows(2)
            down(0)
            turn_hid(1)
            with pe.Fori(2, last2 + 1) as b:
                up(b)
                turn_rows(b + 1)
                down(b - 1)
                turn_hid(b)
            up(last2 + 1)
            down(last2)
            turn_hid(last2 + 1)
            down(last2 + 1)

        @block.scalar
        def _(act):
            A = nc.scalar.activation
            def small(dst, src, name):
                act.dma_start(dst, src).then_inc(sem(name), 16)

            def vec(ap, n):
                return ap.rearrange("(r e) -> r e", e=P)[0:n]
            small(rows[R_C:R_C + 8], vec(a["c"][0], 8), "rows_in")
            small(rows[R_CC:R_CC + 8], vec(a["c_ctx"], 8), "rows_in")
            small(rows[R_BMOD:R_BMOD + 48], vec(a["b_mod"][0], 48), "rows_in")
            small(rows[R_GMIX:R_GMIX + 8], vec(a["norm_mix_g"][0], 8), "rows_in")
            small(rows[R_GFFN:R_GFFN + 8], vec(a["norm_ffn_g"][0], 8), "rows_in")
            small(rows[R_SD:R_SD + 2], vec(a["s5_d"][0], 2), "rows_in")
            small(rows[R_BGLU:R_BGLU + 2], vec(a["s5_b_glu"][0], 2), "rows_in")
            small(rows[R_QN:R_QN + 2], vec(a["mla_q_norm_g"][0], 2), "rows_in")
            small(rows[R_KVN:R_KVN + 1], vec(a["mla_kv_norm_g"][0], 1), "rows_in")
            small(rows[R_SUB:R_SUB + 1], vec(a["diff_subln_g"][0], 1), "rows_in")
            small(rows[R_ARE:R_ARE + 16], a["s5_a_re"][0].rearrange("d (q g) p -> (d q) (g p)", g=2), "rows_in")
            small(rows[R_AIM:R_AIM + 16], a["s5_a_im"][0].rearrange("d (q g) p -> (d q) (g p)", g=2), "rows_in")
            small(lst[:, :], a["s5_log_step"][0].rearrange("d (q g) -> (d q) g", g=2), "lst_in")
            small(lamr, a["diff_lambda"][0].rearrange("a b -> (a b)").partition_broadcast(P), "lam_in")
            for r, name in enumerate(("s5_b_re", "s5_b_im")):
                small(BC[:, r], a[name][0].rearrange("d (q g) p n -> (g p) (d q) n", g=2), "b_in")
            for r, name in enumerate(("s5_c_re", "s5_c_im")):
                for twice in range(2):
                    small(cn[:, 4 * r:4 * r + 4, NS * twice:NS * (twice + 1)],
                          a[name][0].rearrange("d (h g) n p -> (g n) (d h) p", h=2), "cn_in")
            small(GM[:, :], a["b_mod"][0][M_G * D:(M_G + 1) * D].partition_broadcast(P), "gm_in")
            small(wglu[:, :, :], a["s5_w_glu"][0].rearrange("(k p) n -> p k n", p=P), "small_in")
            small(wuq[:, :, :], a["mla_w_uq"][0].rearrange("(k p) n -> p k n", p=P), "small_in")
            small(wukv[:, :], a["mla_w_ukv"][0], "small_in")
            small(wrt[:, :, 0:NGR], a["moe_w_group"][0].rearrange("(k p) n -> p k n", p=P), "small_in")
            small(wrt[:, :, NGR:], a["moe_w_router"][0].rearrange("(k p) n -> p k n", p=P), "small_in")
            small(brt[:, 0:NGR], a["moe_b_group"][0].partition_broadcast(P), "small_in")
            small(brt[:, NGR:], a["moe_b_router"][0].partition_broadcast(P), "small_in")

            act.wait_ge(sem("cols"), 1)
            A(silu_t[:, :], cols[:, 0:16], ACT.Sigmoid).then_inc(sem("sig_c"), 1)

            act.wait_ge(sem("consts"), 1)

            ajk = Chain(act, "act_steps")

            def root_ms(src, n, dst, ready, what, jnk):
                ajk(A(jnk, src, ACT.Square, accum_out=dst))
                ajk.settle()
                A(dst, dst, ACT.Sqrt, scale=1.0 / n, bias=epsb[:, 0:1]).then_inc(sem(what), 1)

            for t in range(NT):
                act.wait_ge(sem(f"x_in{t}"), 16)
                root_ms(xs[:, t, :], D, sml[:, t:t + 1], None, "x_ms", junk)

            def mod_copy(i, b):
                act.wait_ge(sem("mod_two"), i + 1)
                if i >= 2:
                    act.wait_ge(sem("modt"), i - 1)
                A(modrow[:, i % 2, :], PS[0:2, 512 * b:512 * b + 512], ACT.Copy).then_inc(sem("modrow"), 1)

            for n in range(4):
                mod_copy(n, 6 + n % 2)

            act.wait_ge(sem("gmc"), 1)
            for t in range(NT):
                act.wait_ge(sem("xh_tr"), t + 1)
                v = 1 if t < NCT else 0
                for k in range(4):
                    ins = A(hT[:, k, t * P:(t + 1) * P], bank(2 * (t % 2), P, k * P), ACT.Identity,
                            scale=gmc[:, k, v:v + 1], bias=modc[:, 8 * M_SH + k, v:v + 1])
                ins.then_inc(sem("hT_a"), 1)

            act.wait_ge(sem("turns"), 1)
            A(turn[:, 2], turn[:, 0], ACT.Sin, scale=TWO_PI_DOWN).then_inc(sem("rope_t"), 1)
            A(turn[:, 1], turn[:, 1], ACT.Sin, scale=TWO_PI_DOWN).then_inc(sem("rope_t"), 1)
            act.wait_ge(sem("ls_t"), 1)
            A(s5p[:, 0, :], bank(4, 16), ACT.Exp).then_inc(sem("step"), 1)
            act.wait_ge(sem("lam_s"), 1)
            A(sml[:, 490:492], sml[:, 490:492], ACT.Exp).then_inc(sem("lam_e"), 1)
            act.wait_ge(sem("ars"), 1)
            A(s5p[:, 3, :], s5p[:, 1, :], ACT.Exp, scale=float(CH)).then_inc(sem("r8"), 1)

            def s5_tables(d):
                act.wait_ge(sem("ang"), d + 1)
                ang = (st2, st1)
                for r in range(2):
                    src = ang[r][:, 0:NPAIR * (NPOW + NCH)].rearrange("p (q m) -> p q m", q=NPAIR)
                    A(LP[:, r], src[:, :, 0:NPOW], ACT.Sin, scale=TWO_PI_DOWN)
                    A(ECS[:, r], src[:, :, NPOW:], ACT.Sin, scale=TWO_PI_DOWN)
                A(EM, EM, ACT.Exp).then_inc(sem("tabs"), 1)

            def turn_out(w):
                n = ti[w]
                act.wait_ge(sem("turned"), n + 1)
                kind, t = w
                b = 4 + n % 2
                src = bank(b).rearrange("p (h t) -> p h t", h=4)
                lt = slice((t - NCT) * P, (t - NCT + 1) * P)
                tok = slice(t * P, (t + 1) * P)
                if kind == "q":
                    ins = A(QT[:, :, lt], src, ACT.Copy)
                elif kind == "k":
                    ins = A(KT[:, :, tok], src, ACT.Copy)
                elif kind == "uq":
                    ins = A(MQT[0:MQ, :, lt], src[0:MQ], ACT.Copy)
                elif kind == "ukv":
                    ins = A(MKT[0:MQ, :, tok], src[0:MQ], ACT.Copy)
                else:
                    if t >= NCT:
                        for j in range(2):
                            A(CQT[:, j, lt], src[:, j], ACT.Copy, scale=cols[:, R_QN + j:R_QN + j + 1])
                    ins = A(CKVT[:, tok], src[:, 2], ACT.Copy, scale=cols[:, R_KVN:R_KVN + 1])
                ins.then_inc(sem("turned_out"), 1)

            def s5_evac(d):
                for c in range(4):
                    act.wait_ge(sem("pb_t"), 4 * d + c + 1)
                    A(PBT[:, c // 2, 4 * (c % 2):4 * (c % 2) + 4].rearrange("p q s -> p (q s)"), bank(6), ACT.Copy).then_inc(
                        sem("pbt"), 1)
                for c in range(2):
                    act.wait_ge(sem("kk"), 2 * d + c + 1)
                    A(ksb[:, 4 * c:4 * c + 4, :].rearrange("p q m -> p (q m)"), PS[0:2 * GRP, 3584:4096], ACT.Copy).then_inc(
                        sem("ksb"), 1)

            s5_tables(0)
            for t in range(NCT, NT):
                turn_out(("q", t))
            s5_evac(0)
            for t in range(NT):
                turn_out(("k", t))
            s5_tables(1)
            s5_evac(1)
            for t in range(NT):
                act.wait_ge(sem("z"), zi[("m", t)] + 1)
                src = bank(zi[("m", t)] % 4)
                if t >= NCT:
                    ajk(A(jk[:, 0:QRANK], src[:, 0:QRANK], ACT.Square, accum_out=sml[:, 16 + t:17 + t]))
                    ajk.settle()
                ajk(A(jk[:, 0:KVRANK], src[:, QRANK:QRANK + KVRANK], ACT.Square, accum_out=sml[:, 24 + t:25 + t]))
                ajk.settle()
                if t >= NCT:
                    A(sml[:, 16 + t:17 + t], sml[:, 16 + t:17 + t], ACT.Sqrt, scale=1.0 / QRANK, bias=epsb[:, 0:1])
                A(sml[:, 24 + t:25 + t], sml[:, 24 + t:25 + t], ACT.Sqrt, scale=1.0 / KVRANK, bias=epsb[:, 0:1]).then_inc(
                    sem("m_ms"), 1)
                turn_out(("m", t))
            act.wait_ge(sem("gelu_in"), 1)
            A(yt1, yt1, ACT.Tanh, scale=math.sqrt(2.0 / math.pi)).then_inc(sem("tanh"), 1)
            act.wait_ge(sem("glu"), 1)
            for mo in range(2):
                A(yt1[:, mo].rearrange("p j c -> p (j c)"), bank(6 + mo), ACT.Sigmoid,
                  bias=cols[:, R_BGLU + mo:R_BGLU + mo + 1]).then_inc(sem("s5_sig"), 1)
            for kind, first in (("uq", NCT), ("ukv", 0)):
                for t in range(first, NT):
                    turn_out((kind, t))

            def probs(b):
                kind, h, t = blocks[b]
                if b >= 2:
                    act.wait_ge(sem("pt"), b - 1)
                for m in range(2 if kind == "d" else 1):
                    u = unit0[b] + m
                    act.wait_ge(sem("nmax"), u + 1)
                    base = 1024 * (u % 2)
                    A(pbuf[:, 2 * (b % 2) + m, :], PS[:, base:base + TOK], ACT.Exp, bias=sml[:, 64 + u:65 + u],
                      scale=DSCALE if kind == "d" else MSCALE, accum_out=sml[:, 160 + u:161 + u]).then_inc(sem("probs"), 1)

            def probs_out(b):
                kind, h, t = blocks[b]
                hd = b // 4
                if hd >= 2:
                    act.wait_ge(sem("pv"), hd - 1)
                act.wait_ge(sem("pt"), b + 1)
                A(pT[:, hd % 2, :, t * P:(t + 1) * P], PS[:, 2048:2048 + TOK].rearrange("p (k q) -> p k q", k=NT), ACT.Copy).then_inc(sem("pt_out"), 1)

            probs(0)
            for b in range(len(blocks)):
                if b + 1 < len(blocks):
                    probs(b + 1)
                if b in late_at and late_at[b][0] in (F_SH, F_SC):
                    mod_copy(4 + late.index(late_at[b]), 7)
                probs_out(b)
                hd = b // 4 - 1
                if b % 4 == 0 and b >= 4 and hd < DH:
                    act.wait_ge(sem("pv"), hd + 1)
                    A(sq, bank(6), ACT.Square).then_inc(sem("sq"), 1)
                    act.wait_ge(sem("ssum"), hd + 1)
                    A(rms, bank(7), ACT.Sqrt, scale=1.0 / P, bias=epsb[:, 0:1]).then_inc(sem("rms"), 1)

            for t in range(NLT):
                act.wait_ge(sem("xn"), 2 * t + 2)
                root_ms(XN[:, t, :], D, sml[:, 32 + t:33 + t], None, "xn_ms", junk)
            act.wait_ge(sem("gfc"), 1)
            for t in range(NLT):
                act.wait_ge(sem("xhf_tr"), t + 1)
                for k in range(4):
                    ins = A(hfT[:, k, t * P:(t + 1) * P], bank(4 + 2 * (t % 2), P, k * P), ACT.Identity,
                            scale=gfc[:, k:k + 1], bias=modc[:, 8 * F_SH + k, 0:1])
                ins.then_inc(sem("hfT_a"), 1)
            act.wait_ge(sem("g_in"), 1)
            A(gra, gra, ACT.Exp).then_inc(sem("g_exp"), 1)
            act.wait_ge(sem("e_in"), 1)
            A(wts[:, 4, :], wts[:, 4, :], ACT.Exp).then_inc(sem("e_exp"), 1)

            act.wait_ge(sem("routed"), 1)
            last2 = act.value_load(btab[0:1, NBLK:NBLK + 1], min_val=LAT * TOPK // P - 2, max_val=NBLK - 2)

            def rows_T(b):
                act.wait_ge(sem("hg_tr"), b + 1)
                for k in range(4):
                    ins = A(hgT[:, k, :], bank(0, P, k * P), ACT.Identity, scale=gfc[:, k:k + 1],
                            bias=modc[:, 8 * F_SH + k, 0:1])
                ins.then_inc(sem("hgT_a"), 1)

            def silu(b):
                act.wait_ge(sem("w1_used"), b + 1)
                if not isinstance(b, int) or b >= 1:
                    act.wait_ge(sem("hid"), b)
                A(sg, bank(2), ACT.Silu).then_inc(sem("sg"), 1)

            def hidden_T(b):
                act.wait_ge(sem("hid_t"), b + 1)
                A(hidT.rearrange("p k s -> p (k s)"), bank(4), ACT.Copy).then_inc(sem("hidT"), 1)

            rows_T(0)
            silu(0)
            rows_T(1)
            hidden_T(0)
            silu(1)
            rows_T(2)
            hidden_T(1)
            with act.Fori(2, last2 + 1) as b:
                silu(b)
                rows_T(b + 1)
                hidden_T(b)
            silu(last2 + 1)
            hidden_T(last2 + 1)
            for t in range(NLT):
                act.wait_ge(sem("x_out"), t + 1)
                root_ms(XN[:, t, :], D, sml[:, 40 + t:41 + t], None, "f_ms", junk)

        @block.vector
        def _(dve):
            V = nc.vector
            st = Chain(dve, "dve_steps")
            tt, ts, stt, cp = V.tensor_tensor, V.tensor_scalar, V.scalar_tensor_tensor, V.tensor_copy

            def bc(ap, n, axis):
                x = ap.unsqueeze(axis)
                shape = list(x.shape)
                shape[axis] = n
                return x.to_broadcast(shape)

            def fraction(x, tmp):
                st(ts(tmp, x, MAGIC, MAGIC, ALU.add, ALU.subtract))
                st.settle()
                st(tt(x, x, tmp, ALU.subtract))
                st.settle()

            dve.wait_ge(sem("lst_in"), 16)
            cp(lsb[:, :, :], bc(lst[:, :], NS, 2)).then_inc(sem("lsb"), 1)
            dve.wait_ge(sem("cols_t"), 1)
            cp(cols[:, :], bank(0, NROW)).then_inc(sem("cols"), 1)
            dve.wait_ge(sem("cols"), 1)
            dve.wait_ge(sem("sig_c"), 1)
            tt(silu_c[:, :, :], silu_t[:, :].rearrange("p (v k) -> p k v", v=2),
               cols[:, 0:16].rearrange("p (v k) -> p k v", v=2), ALU.mult).then_inc(sem("silu_c"), 1)

            def mod_cols(i, chunk, b, freed):
                dve.wait_ge(sem("modt"), i + 1)
                ins = tt(modc[:, 4 * chunk:4 * chunk + 4, :], bank(b, 8).rearrange("p (j v) -> p j v", v=2),
                         bc(cols[:, R_BMOD + 4 * chunk:R_BMOD + 4 * chunk + 4], 2, 2), ALU.add)
                ins.then_inc(sem(freed), 1)

            for t in range(NT):
                dve.wait_ge(sem("x_ms"), t + 1)
                st(V.reciprocal(sml[:, 8 + t:9 + t], sml[:, t:t + 1]))
                st.settle()
                if t == 0:
                    dve.wait_ge(sem("kpad_clear"), 32)
                if t >= 2:
                    dve.wait_ge(sem("xh_tr"), t - 1)
                ts(xh[:, t % 2, :], xs[:, t, :], sml[:, 8 + t:9 + t], None, ALU.mult).then_inc(sem("xh"), 1)
                if t == 1:
                    for n in range(4):
                        mod_cols(n, n, 5, "modc")
                    dve.wait_ge(sem("modc"), 4)
                    for v in range(2):
                        st(stt(gmc[:, :, v], modc[:, 8 * M_SC:8 * M_SC + 8, v], 1.0, cols[:, R_GMIX:R_GMIX + 8],
                               ALU.add, ALU.mult))
                    st.settle()
                    cp(sml[:, 500:501], epsb[:, :]).then_inc(sem("gmc"), 1)
                if t >= 1:
                    for t2 in ([t - 1] if t < NT - 1 else [t - 1, t]):
                        dve.wait_ge(sem("xh_tr"), t2 + 1)
                        v = 1 if t2 < NCT else 0
                        for k in range(4, KD):
                            ins = ts(hT[:, k, t2 * P:(t2 + 1) * P], bank(2 * (t2 % 2) + 1, P, (k - 4) * P),
                                     gmc[:, k, v:v + 1], modc[:, 8 * M_SH + k, v:v + 1], ALU.mult, ALU.add)
                        ins.then_inc(sem("hT_d"), 1)

            st(cp(pos_f[:, :, :], pos_i[:, :, :]))
            st(cp(mul_f[:, :, :], mul_i[:, :, :]))
            st(cp(io_f[:, :], io_i[:, :]))
            st.settle()
            for axis in range(2):
                for f0, nf, o in ((0, 16, 16 * axis), (16, 8, 32 + 8 * axis)):
                    st(tt(turn[:, 0, :, o:o + nf], bc(pos_f[:, axis, :], nf, 2), bc(freq[:, f0:f0 + nf], NLT, 1), ALU.mult))
            st.settle()
            fraction(turn[:, 0], turn[:, 1])
            st(ts(turn[:, 1], turn[:, 0], 0.25, None, ALU.add))
            st.settle()
            fraction(turn[:, 1], turn[:, 2])
            cp(sml[:, 501:502], epsb[:, :]).then_inc(sem("turns"), 1)
            dve.wait_ge(sem("lam_in"), 16)
            lv = lamr.rearrange("p (a b s) -> p a b s", a=2, b=2)
            st(tt(rp[:, 0, 0:128].rearrange("p (a s) -> p a s", a=2), lv[:, :, 0], lv[:, :, 1], ALU.mult))
            st.settle()
            V.tensor_reduce(sml[:, 490:492], rp[:, 0, 0:128].rearrange("p (a s) -> p a s", a=2), AX.X, ALU.add).then_inc(
                sem("lam_s"), 1)
            dve.wait_ge(sem("lam_e"), 1)
            st(tt(sml[:, 492:493], sml[:, 491:492], sml[:, 490:491], ALU.subtract))
            st.settle()
            st(ts(sml[:, 493:494], sml[:, 492:493], LAM_INIT, None, ALU.subtract))
            st(ts(sml[:, 494:495], cols[:, R_SUB:R_SUB + 1], 1.0 - LAM_INIT, None, ALU.mult))

            AREC, AIMC = cols[:, R_ARE:R_ARE + 16], cols[:, R_AIM:R_AIM + 16]
            dve.wait_ge(sem("step"), 1)
            st(tt(s5p[:, 2, :], AIMC, s5p[:, 0, :], ALU.mult))
            tt(s5p[:, 1, :], AREC, s5p[:, 0, :], ALU.mult).then_inc(sem("ars"), 1)
            st.settle()
            st(ts(s5p[:, 2, :], s5p[:, 2, :], INV_2PI, None, ALU.mult))
            st.settle()
            fraction(s5p[:, 2, :], s5p[:, 4, :])
            st(tt(s5p[:, 4, :], AREC, AREC, ALU.mult))
            st(tt(s5p[:, 5, :], AIMC, AIMC, ALU.mult))
            st.settle()
            st(tt(s5p[:, 4, :], s5p[:, 4, :], s5p[:, 5, :], ALU.add))
            st.settle()
            st(V.reciprocal(s5p[:, 4, :], s5p[:, 4, :]))
            dve.wait_ge(sem("ct_t"), 1)
            ctv = PS[:, 3072:4096].rearrange("p (i q g n) -> p i q g n", i=8, q=4, g=2)
            for g2 in range(2):
                s = slice(NS * g2, NS * g2 + NS)
                for i in range(8):
                    r, d, hf = i // 4, i // 2 % 2, i % 2
                    ins = cp(BC[s, 2 + r, NPAIR * d + 4 * hf:NPAIR * d + 4 * hf + 4, :], ctv[s, i, :, g2, :])
                    if (g2, i) != (1, 7):
                        st(ins)
            ins.then_inc(sem("bc"), 1)

            for h in range(4):
                dve.wait_ge(sem("z"), h + 1)
                c0, nc_ = (0, 64) if h % 2 == 0 else (64, 32)
                cp(UT[:, h // 2, :, c0:c0 + nc_], bank(h, nc_ * CH).rearrange("p (c j) -> p j c", j=CH)).then_inc(
                    sem("z_free"), 1)

            st(V.memset(ZR[:, 0:512], 0.0))
            s5p_b = MP[:, X0 + 4352:X0 + 4608]

            def s5_setup(d):
                q0 = NPAIR * d
                nm = NPOW + NCH
                sin_a = st1[:, 0:NPAIR * nm].rearrange("p (q m) -> p q m", q=NPAIR)
                cos_a = st2[:, 0:NPAIR * nm].rearrange("p (q m) -> p q m", q=NPAIR)
                tmp = MP[:, X0 + 2304:X0 + 2304 + NPAIR * nm].rearrange("p (q m) -> p q m", q=NPAIR)
                st(tt(sin_a, bc(s5p[:, 2, q0:q0 + NPAIR], nm, 2), bc(mul_f[:, d, :], NPAIR, 1), ALU.mult))
                st(tt(EM, bc(s5p[:, 1, q0:q0 + NPAIR], NPOW, 2), bc(mul_f[:, d, 0:NPOW], NPAIR, 1), ALU.mult))
                st.settle()
                fraction(sin_a, tmp)
                st(ts(cos_a, sin_a, 0.25, None, ALU.add))
                st.settle()
                fraction(cos_a, tmp)
                cp(sml[:, 502:503], epsb[:, :]).then_inc(sem("ang"), 1)
                dve.wait_ge(sem("tabs"), d + 1)
                for r in range(2):
                    st(tt(LP[:, r], LP[:, r], EM, ALU.mult))
                st.settle()
                one = 1 if d == 0 else CH - 1
                x, y = s5p[:, 5, 0:8], LP[:, 1, :, one]
                ar, ai, iv = AREC[:, q0:q0 + NPAIR], AIMC[:, q0:q0 + NPAIR], s5p[:, 4, q0:q0 + NPAIR]
                st(ts(x, LP[:, 0, :, one], 1.0, None, ALU.subtract))
                st.settle()
                f = [s5p[:, 6 + i, 0:8] for i in range(6)]
                st(tt(f[0], x, ar, ALU.mult))
                st(tt(f[1], y, ai, ALU.mult))
                st(tt(f[2], y, ar, ALU.mult))
                st(tt(f[3], x, ai, ALU.mult))
                st.settle()
                st(tt(f[0], f[0], f[1], ALU.add))
                st(tt(f[2], f[2], f[3], ALU.subtract))
                st.settle()
                st(tt(f[4], f[0], iv, ALU.mult))
                st(tt(f[5], f[2], iv, ALU.mult))
                st.settle()
                dve.wait_ge(sem("b_in"), 32)
                br, bi = BC[:, 0, q0:q0 + NPAIR, :], BC[:, 1, q0:q0 + NPAIR, :]
                cr, ci = bc(f[4], GRP, 2), bc(f[5], GRP, 2)
                t = [st1[:, 128 * i:128 * i + 128].rearrange("p (q n) -> p q n", q=NPAIR) for i in range(4)]
                st(tt(t[0], br, cr, ALU.mult))
                st(tt(t[1], bi, ci, ALU.mult))
                st(tt(t[2], bi, cr, ALU.mult))
                st(tt(t[3], br, ci, ALU.mult))
                st.settle()
                bb = [s5p_b[:, 128 * i:128 * i + 128].rearrange("p (q n) -> p q n", q=NPAIR) for i in range(2)]
                st(tt(bb[0], t[0], t[1], ALU.subtract))
                st(tt(bb[1], t[2], t[3], ALU.add))
                st.settle()
                for g2 in range(2):
                    s = slice(NS * g2, NS * g2 + NS)
                    for r in range(2):
                        st(cp(BBar[s, r, :, GRP * g2:GRP * (g2 + 1)], bb[r][s]))

                def times_powers(dst, x0, k0, nk, negate):
                    a0 = st1[:, 0:NPAIR * nk * GRP].rearrange("p (q k n) -> p q k n", q=NPAIR, k=nk)
                    a1 = st2[:, 0:NPAIR * nk * GRP].rearrange("p (q k n) -> p q k n", q=NPAIR, k=nk)
                    lr, li = (bc(LP[:, r, :, k0:k0 + nk], GRP, 3) for r in range(2))
                    xr, xi = (bc(x0[r], nk, 2) for r in range(2))
                    st(tt(a0, lr, xr, ALU.mult))
                    st(tt(a1, li, xi, ALU.mult))
                    st.settle()
                    st(tt(dst[0], a0, a1, ALU.subtract))
                    st.settle()
                    st(tt(a0, lr, xi, ALU.mult))
                    st(tt(a1, li, xr, ALU.mult))
                    st.settle()
                    if negate:
                        st(stt(dst[1].rearrange("p q k n -> p (q k n)"), a0.rearrange("p q k n -> p (q k n)"), -1.0,
                               a1.rearrange("p q k n -> p (q k n)"), ALU.mult, ALU.subtract))
                    else:
                        st(tt(dst[1], a0, a1, ALU.add))
                    st.settle()

                k0 = 0 if d == 0 else 1
                times_powers([PB[:, 0], PB[:, 1]], bb, k0, CH, False)
                cp(sml[:, 503:504], epsb[:, :]).then_inc(sem("pb"), 1)
                if d == 0:
                    dve.wait_ge(sem("bc"), 1)
                times_powers([CL[:, 0], CL[:, 1]], [BC[:, 2, q0:q0 + NPAIR, :], BC[:, 3, q0:q0 + NPAIR, :]], 0, NPOW, True)
                cp(sml[:, 504:505], epsb[:, :]).then_inc(sem("cl"), 1)

            def s5_scan(d):
                for c in range(4):
                    r, hq = divmod(c, 2)
                    dve.wait_ge(sem("bu"), 4 * d + c + 1)
                    if c == 0:
                        dve.wait_ge(sem("k_out"), 16 * (d + 1))
                    cp(GG[:, r, 4 * hq:4 * hq + 4, :], bank(6, 4 * NCH).rearrange("p (q c) -> p q c", q=4)).then_inc(
                        sem("bu_out"), 1)
                dve.wait_ge(sem("bu_out"), 4 * (d + 1))
                co, si = ECS[:, 0], ECS[:, 1]
                st(tt(gt1, GG[:, 0], co, ALU.mult))
                st(tt(gt2, GG[:, 1], si, ALU.mult))
                st.settle()
                st(tt(gt1, gt1, gt2, ALU.add))
                st.settle()
                st(tt(gt2, GG[:, 0], si, ALU.mult))
                st(tt(GG[:, 1], GG[:, 1], co, ALU.mult))
                st.settle()
                st(tt(GG[:, 1], GG[:, 1], gt2, ALU.subtract))
                st(cp(GG[:, 0], gt1))
                st.settle()
                runs = [(0, NCH, False)] if d == 0 else [(0, NCC, True), (NCC, NCH, True)]
                for n, (c0, c1, back) in enumerate(runs):
                    for q in range(NPAIR):
                        decay = s5p[:, 3, NPAIR * d + q:NPAIR * d + q + 1].to_broadcast([P, c1 - c0])
                        for r in range(2):
                            x = GG[:, r, q, c0:c1]
                            if back:
                                x = x[:, ::-1]
                            st(V.tensor_tensor_scan(x, decay, x, 0.0 if n == 0 else GG[:, r, q, 0:1], ALU.mult, ALU.add))
                    st.settle()
                for r in range(2):
                    st(tt(gt1, GG[:, 0], ECS[:, r], ALU.mult))
                    st(tt(gt2, GG[:, 1], ECS[:, 1 - r], ALU.mult))
                    st.settle()
                    st(tt(HH[:, r, :, 0:NCH], gt1, gt2, ALU.add if r else ALU.subtract))
                    st.settle()
                if d == 1:
                    st(cp(HH[:, :, :, NCH], HH[:, :, :, 0]))
                    st.settle()
                cp(sml[:, 505:506], epsb[:, :]).then_inc(sem("hh"), 1)

            def s5_add(d):
                for h in range(2):
                    dve.wait_ge(sem("yy"), 2 * d + h + 1)
                    dst = yacc.rearrange("p (q g) c -> p q g c", g=2)[:, :, h, :]
                    src = bank(7 - h).rearrange("p (q c) -> p q c", q=NPAIR)
                    if d == 0:
                        cp(dst, src).then_inc(sem("yacc"), 1)
                    else:
                        tt(dst, src, dst, ALU.add).then_inc(sem("yacc"), 1)

            def rope(dst, src, nh, nf, t, f0, last):
                even, odd = src.rearrange("p h (f two) -> p h f two", two=2)[:, :, :, 0], \
                    src.rearrange("p h (f two) -> p h f two", two=2)[:, :, :, 1]
                de, do = dst.rearrange("p h (f two) -> p h f two", two=2)[:, :, :, 0], \
                    dst.rearrange("p h (f two) -> p h f two", two=2)[:, :, :, 1]
                c, s = (bc(turn[:, i, t, f0:f0 + nf], nh, 1) for i in (1, 2))
                r = [rp[:, i, 0:nh * nf].rearrange("p (h f) -> p h f", h=nh) for i in range(4)]
                st(tt(r[0], even, c, ALU.mult))
                st(tt(r[1], odd, s, ALU.mult))
                st(tt(r[2], even, s, ALU.mult))
                st(tt(r[3], odd, c, ALU.mult))
                st.settle()
                st(tt(de, r[0], r[1], ALU.subtract))
                st(tt(do, r[2], r[3], ALU.add))
                st.settle()

            def evacuate(w):
                kind, t = w
                dve.wait_ge(sem("z"), zi[w] + 1)
                src = bank(zi[w] % 4)
                n = ti.get(w)
                if n is not None:
                    if n >= 2:
                        dve.wait_ge(sem("turned"), n - 1)
                    dst = QR[:, n % 2, :]
                lt = t - NCT
                if kind in ("q", "k"):
                    if t >= NCT:
                        rope(dst.rearrange("p (h f) -> p h f", h=2 * DH), src.rearrange("p (h f) -> p h f", h=2 * DH),
                             2 * DH, DHD // 2, lt, 0, None)
                    else:
                        st(cp(dst, src))
                elif kind == "v":
                    st(cp(VV[:, t, :], src))
                elif kind == "m":
                    dve.wait_ge(sem("m_ms"), t + 1)
                    if t >= NCT:
                        st(V.reciprocal(sml[:, 16 + t:17 + t], sml[:, 16 + t:17 + t]))
                    st(V.reciprocal(sml[:, 24 + t:25 + t], sml[:, 24 + t:25 + t]))
                    st.settle()
                    if t >= NCT:
                        st(ts(dst[:, 0:QRANK], src[:, 0:QRANK], sml[:, 16 + t:17 + t], None, ALU.mult))
                    st(ts(dst[:, QRANK:QRANK + KVRANK], src[:, QRANK:QRANK + KVRANK], sml[:, 24 + t:25 + t], None, ALU.mult))
                    kr = src[:, QRANK + KVRANK:QRANK + KVRANK + MR]
                    if t >= NCT:
                        rope(KR[:, t:t + 1, :], kr.unsqueeze(1), 1, MR // 2, lt, 32, None)
                    else:
                        st(cp(KR[:, t, :], kr))
                elif kind == "uq":
                    s3 = src[:, 0:MH * MQ].rearrange("p (h f) -> p h f", h=MH)
                    d3 = dst[:, 0:MH * MQ].rearrange("p (h f) -> p h f", h=MH)
                    st(cp(d3[:, :, 0:MN], s3[:, :, 0:MN]))
                    rope(d3[:, :, MN:], s3[:, :, MN:], MH, MR // 2, lt, 32, None)
                else:
                    s3 = src.rearrange("p (h f) -> p h f", h=MH)
                    d3 = dst[:, 0:MH * MQ].rearrange("p (h f) -> p h f", h=MH)
                    st(cp(d3[:, :, 0:MN], s3[:, :, 0:MN]))
                    st(cp(d3[:, :, MN:], bc(KR[:, t, :], MH, 1)))
                    st(cp(MVV[:, t, :].rearrange("p (h f) -> p h f", h=MH), s3[:, :, MN:]))
                st.settle()
                if n is not None:
                    cp(sml[:, 506:507], epsb[:, :]).then_inc(sem("qr"), 1)
                cp(sml[:, 507:508], epsb[:, :]).then_inc(sem("z_free"), 1)

            s5_setup(0)
            dve.wait_ge(sem("rope_t"), 2)
            for t in range(NCT, NT):
                evacuate(("q", t))
            s5_scan(0)
            for t in range(NT):
                evacuate(("k", t))
            s5_add(0)
            s5_setup(1)
            for t in range(NT):
                evacuate(("v", t))
            s5_scan(1)
            for t in range(NT):
                evacuate(("m", t))
            s5_add(1)

            dve.wait_ge(sem("y_in"), 32)
            for h in range(2):
                st(stt(YT[:, h], UT[:, h, :, NCC:], cols[:, R_SD + h:R_SD + h + 1], YT[:, h], ALU.mult, ALU.add))
            st.settle()
            st(tt(yt1, YT, YT, ALU.mult))
            st.settle()
            st(ts(yt1, yt1, 0.044715, 1.0, ALU.mult, ALU.add))
            st.settle()
            tt(yt1, yt1, YT, ALU.mult).then_inc(sem("gelu_in"), 1)
            dve.wait_ge(sem("tanh"), 1)
            st(ts(yt1, yt1, 0.5, 0.5, ALU.mult, ALU.add))
            st.settle()
            tt(YG, yt1, YT, ALU.mult).then_inc(sem("yg"), 1)
            dve.wait_ge(sem("yg"), 1)
            for mo in range(2):
                dve.wait_ge(sem("s5_sig"), mo + 1)
                tt(mix[:, mo, :].rearrange("p (c j) -> p j c", j=CH), YG[:, mo], yt1[:, mo], ALU.mult).then_inc(
                    sem("s5_mix"), 1)
            for kind, first in (("uq", NCT), ("ukv", 0)):
                for t in range(first, NT):
                    evacuate((kind, t))

            dve.wait_ge(sem("s5_mix"), 2)
            cp(silu_cb, silu_c[:, :, 0:1].to_broadcast([P, KD, P])).then_inc(sem("silu_cb"), 1)

            def maxima(b):
                kind = blocks[b][0]
                for m in range(2 if kind == "d" else 1):
                    u = unit0[b] + m
                    dve.wait_ge(sem("scores"), u + 1)
                    base = 1024 * (u % 2)
                    st(V.tensor_reduce(sml[:, 112 + u:113 + u], PS[:, base:base + TOK], AX.X, ALU.max))
                    st.settle()
                    ts(sml[:, 64 + u:65 + u], sml[:, 112 + u:113 + u], -(DSCALE if kind == "d" else MSCALE), None,
                       ALU.mult).then_inc(sem("nmax"), 1)

            def combine(b):
                kind = blocks[b][0]
                u = unit0[b]
                p0, p1 = pbuf[:, 2 * (b % 2), :], pbuf[:, 2 * (b % 2) + 1, :]
                dve.wait_ge(sem("probs"), u + 1)
                st(V.reciprocal(sml[:, 208 + u:209 + u], sml[:, 160 + u:161 + u]))
                st.settle()
                if kind == "l":
                    ts(p0, p0, sml[:, 208 + u:209 + u], None, ALU.mult).then_inc(sem("pc"), 1)
                    return
                st(ts(p0, p0, sml[:, 208 + u:209 + u], None, ALU.mult))
                dve.wait_ge(sem("probs"), u + 2)
                st(V.reciprocal(sml[:, 209 + u:210 + u], sml[:, 161 + u:162 + u]))
                st.settle()
                st(tt(sml[:, 209 + u:210 + u], sml[:, 209 + u:210 + u], sml[:, 493:494], ALU.mult))
                st.settle()
                stt(p1, p1, sml[:, 209 + u:210 + u], p0, ALU.mult, ALU.add).then_inc(sem("pc"), 1)

            def head_out(hd):
                if hd < DH:
                    dve.wait_ge(sem("rms"), hd + 1)
                    V.reciprocal(rms, rms).then_inc(sem("b7_free"), 1)
                    dve.wait_ge(sem("b7_free"), LG[("rms", hd)] + 1)
                    stt(mix[:, 2 + hd, :], bank(6), sml[:, 494:495], rms, ALU.mult, ALU.mult).then_inc(sem("o_free"), 1)
                else:
                    dve.wait_ge(sem("pv"), hd + 1)
                    s = slice(MV * (hd % 2), MV * (hd % 2) + MV)
                    cp(mix[s, 6 + (hd - DH) // 2, :], PS[s, 3072:3584]).then_inc(sem("o_free"), 1)

            maxima(0)
            for b in range(len(blocks)):
                combine(b)
                if b + 1 < len(blocks):
                    maxima(b + 1)
                if b in late_at:
                    term, half = late_at[b]
                    i = late.index(late_at[b])
                    if term in (F_SH, F_SC):
                        mod_cols(4 + i, 2 * term + half, 7, "b7_free")
                    else:
                        dve.wait_ge(sem("mod_wide"), i - 3)
                        dve.wait_ge(sem("gm_in" if term == M_G else "gf_in"), 16)
                        g = (GM[:, :] if term == M_G else GF)[:, 512 * half:512 * half + 512]
                        tt(g, g, bank(7), ALU.add).then_inc(sem("b7_free"), 1)
                if b % 4 == 0 and b >= 4:
                    head_out(b // 4 - 1)
            dve.wait_ge(sem("b7_free"), n7)
            stt(gfc[:, :], modc[:, 8 * F_SC:8 * F_SC + 8, 0], 1.0, cols[:, R_GFFN:R_GFFN + 8], ALU.add, ALU.mult).then_inc(
                sem("gfc"), 1)
            head_out(NHD - 1)

            dve.wait_ge(sem("xr_in"), 16 * NLT)
            def add_mixer(t):
                for half in range(2):
                    c = slice(512 * half, 512 * half + 512)
                    i = 2 * t + half
                    dve.wait_ge(sem("op"), i + 1)
                    tmp = ot1[:, 512 * (i % 2):512 * (i % 2) + 512]
                    st(tt(tmp, bank(i % 4), GM[:, c], ALU.mult))
                    st.settle()
                    tt(XN[:, t, c], XN[:, t, c], tmp, ALU.add).then_inc(sem("xn"), 1)

            dve.wait_ge(sem("gfc"), 1)
            add_mixer(0)
            for t in range(NLT):
                if t + 1 < NLT:
                    add_mixer(t + 1)
                dve.wait_ge(sem("xn_ms"), t + 1)
                st(V.reciprocal(sml[:, 36 + t:37 + t], sml[:, 32 + t:33 + t]))
                st.settle()
                if t >= 2:
                    dve.wait_ge(sem("xhf_tr"), t - 1)
                    dve.wait_ge(sem(f"xh_out{t % 2}"), 16)
                ts(xhf[:, t % 2, :], XN[:, t, :], sml[:, 36 + t:37 + t], None, ALU.mult).then_inc(sem("xhf"), 1)
                if t >= 1:
                    for t2 in ([t - 1] if t < NLT - 1 else [t - 1, t]):
                        dve.wait_ge(sem("xhf_tr"), t2 + 1)
                        for k in range(4, KD):
                            ins = ts(hfT[:, k, t2 * P:(t2 + 1) * P], bank(5 + 2 * (t2 % 2), P, (k - 4) * P),
                                     gfc[:, k:k + 1], modc[:, 8 * F_SH + k, 0:1], ALU.mult, ALU.add)
                        ins.then_inc(sem("hfT_d"), 1)

            st(ts(tri_inc[0:NE, :], ident[0:NE, 0:NE], 1.0, None, ALU.mult))
            st(ts(tri128[0:NE, :], tri[0:NE, 0:NE], float(P), None, ALU.mult))
            st.settle()
            st(tt(tri_inc[0:NE, :], tri_inc[0:NE, :], tri[0:NE, 0:NE], ALU.add))
            dve.wait_ge(sem("small_in"), 16 * 7)
            dve.wait_ge(sem("logits"), 1)
            st(tt(logit, bank(0, 144).rearrange("p (t e) -> p t e", t=NLT), bc(brt[:, :], NLT, 1), ALU.add))
            st.settle()

            def first_max(dst, x, n, top, tmp):
                st(V.tensor_reduce(top, x, AX.X, ALU.max))
                st.settle()
                st(tt(tmp, x, bc(top, n, 2), ALU.is_equal))
                st.settle()
                st(ts(tmp, tmp, -64.0, 64.0, ALU.mult, ALU.add))
                st.settle()
                st(tt(tmp, tmp, bc(io_f[:, 0:n], NLT, 1), ALU.add))
                st.settle()
                st(V.tensor_reduce(wts[:, 7, :], tmp, AX.X, ALU.min))
                st.settle()
                st(tt(dst, bc(io_f[:, 0:n], NLT, 1), bc(wts[:, 7, :], n, 2), ALU.is_equal))
                st.settle()

            gl, el = logit[:, :, 0:NGR], logit[:, :, NGR:]
            first_max(goh, gl, NGR, wts[:, 2, :], gra)
            tt(gra, gl, bc(wts[:, 2, :], NGR, 2), ALU.subtract).then_inc(sem("g_in"), 1)
            e4 = emsk.rearrange("p t (g e) -> p (t g) e", g=NGR)
            st(ts(rb[:, :, 0:NGR], goh, 1e30, -1e30, ALU.mult, ALU.add))
            st(cp(ra, el))
            st.settle()
            st(tt(e4, ra.rearrange("p t (g e) -> p (t g) e", g=NGR), bc(goh.rearrange("p t g -> p (t g)"), EPG, 2), ALU.mult))
            st(cp(gidxf, rb[:, :, 0:NGR]))
            st.settle()
            st(tt(e4, e4, bc(gidxf.rearrange("p t g -> p (t g)"), EPG, 2), ALU.add))
            st.settle()
            first_max(oneh[:, 0], emsk, NE, wts[:, 5, :], ra)
            st(ts(ra, oneh[:, 0], -2e30, None, ALU.mult))
            st.settle()
            st(tt(emsk, emsk, ra, ALU.add))
            st.settle()
            first_max(oneh[:, 1], emsk, NE, wts[:, 6, :], ra)
            tt(mask, oneh[:, 0], oneh[:, 1], ALU.add).then_inc(sem("mask"), 1)
            tt(wts[:, 4, :], wts[:, 6, :], wts[:, 5, :], ALU.subtract).then_inc(sem("e_in"), 1)
            dve.wait_ge(sem("cnt"), 1)
            for i in range(LAT // P):
                st(ts(nbt[0:NE, i:i + 1], PS[0:NE, 2560:2561], float(P * i), None, ALU.is_gt))
            st.settle()
            st(V.tensor_reduce(nbv[0:NE], nbt[0:NE, :], AX.X, ALU.add))
            st.settle()
            cp(nb_b[0:NE, :], nbv[0:NE].to_broadcast([NE, P])).then_inc(sem("nb"), 1)
            dve.wait_ge(sem("g_exp"), 1)
            dve.wait_ge(sem("e_exp"), 1)
            st(V.tensor_reduce(wts[:, 3, :], gra, AX.X, ALU.add))
            st(ts(wts[:, 2, :], wts[:, 4, :], 1.0, None, ALU.add))
            st.settle()
            st(tt(wts[:, 3, :], wts[:, 3, :], wts[:, 2, :], ALU.mult))
            st.settle()
            st(V.reciprocal(wts[:, 0, :], wts[:, 3, :]))
            st.settle()
            st(tt(wts[:, 1, :], wts[:, 4, :], wts[:, 0, :], ALU.mult))
            dve.wait_ge(sem("ends"), 1)
            st(cp(endv[0:NE], PS[0:NE, 2562:2563]))
            st.settle()
            st(ts(cmpb[0:NE, 0:NBLK], io_f[0:NE, :], endv[0:NE], None, ALU.is_ge))
            cp(cmpb[0:NE, NBLK:NBLK + 1], nbv[0:NE]).then_inc(sem("cmp"), 1)
            dve.wait_ge(sem("place"), 1)
            for k in range(TOPK):
                st(tt(ra, oneh[:, k], bank(6, NLT * NE).rearrange("p (t e) -> p t e", t=NLT), ALU.mult))
                st.settle()
                st(V.tensor_reduce(rb[:, k, 0:NLT], ra, AX.X, ALU.add))
                st.settle()
            st(ts(ra[:, 0:TOPK, 0:NLT], rb[:, 0:TOPK, 0:NLT], -(P - 1) / 2.0, 1.0 / P, ALU.add, ALU.mult))
            st.settle()
            st(ts(ra[:, 0:TOPK, 0:NLT], ra[:, 0:TOPK, 0:NLT], MAGIC, MAGIC, ALU.add, ALU.subtract))
            st(ts(rb[:, 0:TOPK, 0:NLT], rb[:, 0:TOPK, 0:NLT], float(NBLK), None, ALU.mult))
            st.settle()
            st(ts(ra[:, 0:TOPK, 0:NLT], ra[:, 0:TOPK, 0:NLT], float(P * NBLK - 1), None, ALU.mult))
            st.settle()
            tt(pos_k[:, :, :], rb[:, 0:TOPK, 0:NLT], ra[:, 0:TOPK, 0:NLT], ALU.subtract).then_inc(sem("pos_k"), 1)
            dve.wait_ge(sem("bt"), 1)
            st(cp(btab[:, 0:NBLK], PS[0:1, 3584:3584 + NBLK]))
            ts(btab[:, NBLK:], PS[0:1, 3584 + NBLK:3584 + NBLK + 1], -2.0, None, ALU.add).then_inc(sem("routed"), 1)

            dve.wait_ge(sem("routed"), 1)
            last2 = dve.value_load(btab[0:1, NBLK:NBLK + 1], min_val=LAT * TOPK // P - 2, max_val=NBLK - 2)

            def rows_T(b):
                dve.wait_ge(sem("hg_tr"), b + 1)
                for k in range(4, KD):
                    ins = ts(hgT[:, k, :], bank(1, P, (k - 4) * P), gfc[:, k:k + 1], modc[:, 8 * F_SH + k, 0:1],
                             ALU.mult, ALU.add)
                ins.then_inc(sem("hgT_d"), 1)

            def hidden(b):
                dve.wait_ge(sem("sg"), b + 1)
                dve.wait_ge(sem("w3_used"), b + 1)
                tt(hid, sg, bank(3), ALU.mult).then_inc(sem("hid"), 1)

            def results(b):
                dve.wait_ge(sem("w2_used"), b + 1)
                if not isinstance(b, int) or b >= 1:
                    dve.wait_ge(sem("y_sc"), 16 * b)
                for n in range(2):
                    tt(ysb[:, 512 * n:512 * n + 512], bank(5 + n), GF[:, 512 * n:512 * n + 512], ALU.mult).then_inc(
                        sem("ysb"), 1)

            rows_T(0)
            hidden(0)
            rows_T(1)
            hidden(1)
            rows_T(2)
            results(0)
            with dve.Fori(2, last2 + 1) as b:
                hidden(b)
                rows_T(b + 1)
                results(b - 1)
            hidden(last2 + 1)
            results(last2)
            results(last2 + 1)

            def last_norm(t):
                dve.wait_ge(sem("f_ms"), t + 1)
                st(V.reciprocal(sml[:, 44 + t:45 + t], sml[:, 40 + t:41 + t]))
                st.settle()
                if t >= 2:
                    dve.wait_ge(sem(f"out_done{t % 2}"), 16)
                stt(fin[:, t % 2, :], XN[:, t, :], sml[:, 44 + t:45 + t], fng, ALU.mult, ALU.mult).then_inc(sem("fin"), 1)

            dve.wait_ge(sem("fng_in"), 16)
            for t in range(NLT):
                dve.wait_ge(sem(f"yk_in{t % 2}"), 32 * (t // 2 + 1))
                y0, y1 = yk[:, t % 2, 0, :], yk[:, t % 2, 1, :]
                st(stt(XN[:, t, :], y0, wts[:, 0, t:t + 1], XN[:, t, :], ALU.mult, ALU.add))
                st.settle()
                stt(XN[:, t, :], y1, wts[:, 1, t:t + 1], XN[:, t, :], ALU.mult, ALU.add).then_inc(sem("x_out"), 1)
                if t >= 1:
                    last_norm(t - 1)
            last_norm(NLT - 1)


_INS = ["x", "c", "ctx", "c_ctx", "w_mod", "b_mod", "norm_mix_g", "norm_ffn_g", "w_in", "s5_a_re", "s5_a_im",
        "s5_log_step", "s5_b_re", "s5_b_im", "s5_c_re", "s5_c_im", "s5_d", "s5_w_glu", "s5_b_glu", "diff_lambda",
        "diff_subln_g", "mla_q_norm_g", "mla_w_uq", "mla_kv_norm_g", "mla_w_ukv", "w_out", "moe_w_group",
        "moe_b_group", "moe_w_router", "moe_b_router", "moe_w1", "moe_w3", "moe_w2", "final_norm_g"]


def kernel(**inputs):
    import numpy as _np
    import concourse.bacc as _bacc
    from concourse import mybir as _mybir
    from concourse.bass_utils import run_bass_kernel_spmd as _run

    nc = _bacc.Bacc("TRN2", target_bir_lowering=False, num_devices=1)
    arrays, args = {}, {}
    for name in _INS:
        v = _np.ascontiguousarray(inputs[name])
        arrays[f"in_{name}"] = v
        args[name] = nc.dram_tensor(f"in_{name}", v.shape, _mybir.dt.from_np(v.dtype), kind="ExternalInput").ap()
    out = nc.dram_tensor("out", (1, LAT, D), F32, kind="ExternalOutput").ap()
    build(nc, args, out)
    r = _run(nc, [arrays], core_ids=[0])
    return r.results[0]["out"]
```

```python
import math
from contextlib import ExitStack

import concourse.bass as bass
from concourse import mybir

F32 = mybir.dt.float32
I32 = mybir.dt.int32
ALU = mybir.AluOpType
ACT = mybir.ActivationFunctionType
AX = mybir.AxisListType
P = 128

D = 1024
KD = D // P
LAT, CTX = 512, 256
TOK = CTX + LAT
NT, NCT = TOK // P, CTX // P
NLT = LAT // P
GRID_W = 64
EPS = 1e-6
ROPE_BASE = 10000.0

S5W, GRP, NG, NS = 256, 16, 16, 64
NPAIR = NG // 2
CH = 8
NCH = TOK // CH
NCC = CTX // CH
NCL = LAT // CH
NPOW = CH + 1
KW = (2 * CH - 1) * GRP

DH, DHD = 4, 64
MH, MN, MR, MV = 4, 64, 32, 64
MQ = MN + MR
QRANK, KVRANK = 256, 128
DSCALE = DHD ** -0.5
MSCALE = MQ ** -0.5
LAM_INIT = 0.8 - 0.6 * math.exp(-0.3 * 0)

NE, EPG, NGR = 32, 8, 4
TOPK = 2
NBLK = NE + (LAT * TOPK - NE) // P
SLOT_NONE = 65535

MAGIC = 1.5 * 2.0 ** 23
TWO_PI_DOWN = 6.283185
INV_2PI = 1.0 / (2.0 * math.pi)

R_C, R_CC, R_BMOD, R_GMIX, R_GFFN = 0, 8, 16, 64, 72
R_SD, R_BGLU, R_QN, R_KVN, R_SUB, R_ARE, R_AIM, NROW = 80, 82, 84, 86, 87, 88, 104, 120

M_SH, M_SC, M_G, F_SH, F_SC, F_G = range(6)

Z_Q, Z_K, Z_V, Z_M = 256, 768, 1280, 1792
Z_ALL = 2208


def stream_plan():
    mod = lambda term: [("mod", 2 * term), ("mod", 2 * term + 1)]
    first = mod(M_SH) + mod(M_SC) + [("in", Z_Q - S5W, S5W), ("in", Z_Q, 512), ("in", Z_K, 512), ("in", Z_V, 512),
                                     ("in", Z_M, Z_ALL - Z_M)]
    return first + mod(F_SH) + mod(F_SC) + mod(M_G) + [("out", 0), ("out", 1)] + mod(F_G)


def build(nc, a, out):
    ctx = ExitStack()
    sems = {}

    def sem(name):
        if name not in sems:
            sems[name] = ctx.enter_context(nc.semaphore(name))
        return sems[name]

    class Chain:

        def __init__(self, eng, name):
            self.eng, self.sem, self.n = eng, sem(name), 0

        def __call__(self, ins):
            self.n += 1
            ins.then_inc(self.sem, 1)
            return ins

        def settle(self):
            self.eng.wait_ge(self.sem, self.n)

    with ctx:
        def sb(name, shape, dt=F32):
            return ctx.enter_context(nc.sbuf_tensor(name, shape, dt))

        RING = 3
        W = sb("W", [P, RING, 4096])
        HTR = sb("HTR", [P, 6144])
        QKV = sb("QKV", [P, 8192])
        MP = sb("MP", [P, 7168])
        S5R = sb("S5R", [P, 9984])
        ZR = sb("ZR", [P, 1984])
        CST = sb("CST", [P, 3 * P])
        ident, ones, tri = CST[:, 0:P], CST[:, P:2 * P], CST[:, 2 * P:3 * P]
        rows = sb("rows", [P, P])
        cols = sb("cols", [P, NROW])
        silu_c = sb("silu_c", [P, KD, 2])
        silu_t = sb("silu_t", [P, 2 * KD])
        silu_cb = S5R[:, 8704:9728].rearrange("p (k n) -> p k n", k=KD)
        modrow_of = {mixer: buf.rearrange("p (b n) -> p b n", b=2)
                     for mixer, buf in ((True, S5R[0:2, 7680:8704]), (False, HTR[0:2, 0:1024]))}
        modc = sb("modc", [P, 48, 2])
        gmc = sb("gmc", [P, KD, 2])
        gfc = sb("gfc", [P, KD])
        GM = sb("GM", [P, D])
        wglu = sb("wglu", [P, 2, S5W])
        wuq = sb("wuq", [P, 2, MH * MQ])
        wukv = sb("wukv", [P, MH * (MN + MV)])
        wrt = sb("wrt", [P, KD, NGR + NE])
        brt = sb("brt", [P, NGR + NE])
        lamr = S5R[:, 0:4 * DHD]
        sml = sb("sml", [P, 512])
        turn = sb("turn", [P, 3, NLT, 48])
        freq = sb("freq", [P, 24])
        pos_i = sb("pos_i", [P, 2, NLT], I32)
        pos_f = sb("pos_f", [P, 2, NLT])
        lst = sb("lst", [16, 2])
        lsb = sb("lsb", [16, 2, NS])
        mul_i = sb("mul_i", [P, 2, NPOW + NCH], I32)
        mul_f = sb("mul_f", [P, 2, NPOW + NCH])
        s5p = sb("s5p", [P, 12, 16])
        epsb = sb("epsb", [P, 1])
        QR = sb("QR", [P, 2, 512])
        io_i = sb("io_i", [P, NBLK], I32)
        io_f = sb("io_f", [P, NBLK])
        pair_i = sb("pair_i", [P, TOPK, NLT, 2], I32)
        slots = sb("slots", [P, NBLK, 2], I32)
        btab = sb("btab", [1, NBLK + 1], I32)
        pos_k = sb("pos_k", [P, TOPK, NLT], I32)
        gidx = sb("gidx", [P, 1], I32)
        sidx = sb("sidx", [P, 1], I32)
        sidx_last = sb("sidx_last", [P, 1], I32)
        held = sb("held", [1, 8])

        PS = ctx.enter_context(nc.psum_tensor("PS", [P, 4096], F32))

        def bank(b, n=512, off=0):
            return PS[:, 512 * b + off:512 * b + off + n]

        hT = HTR[:, :].rearrange("p (k t) -> p k t", k=KD)
        xs = QKV[:, 0:6144].rearrange("p (t d) -> p t d", t=NT)
        xh = MP[:, 5120:7168].rearrange("p (b d) -> p b d", b=2)
        QT = QKV[:, 0:2048].rearrange("p (h t) -> p h t", h=DH)
        KT = QKV[:, 2048:5120].rearrange("p (h t) -> p h t", h=DH)
        VV = QKV[:, 5120:8192].rearrange("p (t e) -> p t e", t=NT)
        mix = MP[:, 0:4096].rearrange("p (k t) -> p k t", k=KD)
        pbuf = MP[:, 4096:7168].rearrange("p (b s) -> p b s", b=4)
        pT = HTR[:, :].rearrange("p (b k q) -> p b k q", b=2, k=NT)
        MQT = S5R[:, 0:2048].rearrange("p (h t) -> p h t", h=MH)
        MKT = S5R[:, 2048:5120].rearrange("p (h t) -> p h t", h=MH)
        MVV = S5R[:, 5120:6656].rearrange("p (t e) -> p t e", t=NT)
        sq = S5R[:, 6656:7168]
        ssq = S5R[:, 7168:7168 + DH * NLT]
        mod_acc = S5R[:, 7680:8704].rearrange("p (b n) -> p b n", b=2)
        CQT = ZR[:, 0:1024].rearrange("p (k t) -> p k t", k=2)
        CKVT = ZR[:, 1024:1792]
        KR = ZR[:, 1792:1984].rearrange("p (t r) -> p t r", t=NT)
        UT = S5R[:, 0:1536].rearrange("p (h j c) -> p h j c", h=2, j=CH)
        UU = S5R[:, 1536:3072].rearrange("p (g c) -> p g c", g=NG)
        yacc = S5R[:, 3072:4096].rearrange("p (g c) -> p g c", g=NG)
        CL = S5R[:, 4096:6400].rearrange("p (r q k n) -> p r q k n", r=2, q=NPAIR, k=NPOW)
        PBT = S5R[:, 6400:8448].rearrange("p (r q s) -> p r q s", r=2, q=NPAIR)
        TPL = S5R[:, 6400:8448].rearrange("p (g m) -> p g m", g=NG)
        ECS = S5R[:, 8448:9984].rearrange("p (r q c) -> p r q c", r=2, q=NPAIR)
        X0 = 1024
        st1 = MP[:, X0:X0 + 1152]
        st2 = MP[:, X0 + 1152:X0 + 2304]
        PB = MP[:, X0 + 2304:X0 + 4352].rearrange("p (r q i n) -> p r q i n", r=2, q=NPAIR, i=CH)
        ksb = MP[0:2 * GRP, X0 + 2304:X0 + 3328].rearrange("p (q m) -> p q m", q=NPAIR)
        GG = MP[:, X0:X0 + 1536].rearrange("p (r q c) -> p r q c", r=2, q=NPAIR)
        gt1 = MP[:, X0 + 1536:X0 + 2304].rearrange("p (q c) -> p q c", q=NPAIR)
        gt2 = MP[:, X0 + 2304:X0 + 3072].rearrange("p (q c) -> p q c", q=NPAIR)
        HH = MP[:, X0 + 3072:X0 + 3072 + 2 * NPAIR * (NCH + 1)].rearrange("p (r q c) -> p r q c", r=2, q=NPAIR)
        BC = MP[:, 0:1024].rearrange("p (r q n) -> p r q n", r=4, q=16)
        cn = QR[:, :, :].rearrange("p b (i s) -> p (b i) s", i=4)
        YT = S5R[:, 6400:7424].rearrange("p (h j c) -> p h j c", h=2, j=CH)
        YG = S5R[:, 7424:8448].rearrange("p (h j c) -> p h j c", h=2, j=CH)
        yt1 = S5R[:, 8448:9472].rearrange("p (h j c) -> p h j c", h=2, j=CH)
        LP = MP[:, 6928:7072].rearrange("p (r q k) -> p r q k", r=2, q=NPAIR)
        EM = MP[:, 7072:7144].rearrange("p (q k) -> p q k", q=NPAIR)
        BBar = ZR[:, 0:512].rearrange("p (r q m) -> p r q m", r=2, q=NPAIR)
        XN = QKV[:, 0:4096].rearrange("p (t d) -> p t d", t=NLT)
        GF = QKV[:, 4096:5120]
        fng = QKV[:, 5120:6144]
        ot1 = QKV[:, 6144:7168]
        hfT = HTR[:, 0:4096].rearrange("p (k t) -> p k t", k=KD)
        xhf = S5R[:, 0:4096].rearrange("p (t d) -> p t d", t=NLT)
        hg = S5R[:, 2048:3072]
        hgT = S5R[:, 3072:4096].rearrange("p (k s) -> p k s", k=KD)
        hid = S5R[:, 4096:4608]
        hidT = S5R[:, 4608:5120].rearrange("p (k s) -> p k s", k=4)
        ysb = S5R[:, 5120:6144]
        ysb_last = S5R[:, 6656:7680]
        sg = S5R[:, 6144:6656]
        rt = S5R[:, 6656:9984]
        logit = rt[:, 0:144].rearrange("p (t e) -> p t e", t=NLT)
        mask = rt[:, 144:272].rearrange("p (t e) -> p t e", t=NLT)
        oneh = rt[:, 272:528].rearrange("p (k t e) -> p k t e", k=TOPK, t=NLT)
        emsk = rt[:, 528:656].rearrange("p (t e) -> p t e", t=NLT)
        ra = rt[:, 656:784].rearrange("p (t e) -> p t e", t=NLT)
        rb = rt[:, 784:912].rearrange("p (t e) -> p t e", t=NLT)
        tri_inc, tri128 = rt[:, 1000:1032], rt[:, 1032:1064]
        nb_b, nbv, endv = rt[:, 1064:1192], rt[:, 1192:1193], rt[:, 1193:1194]
        nbt = rt[:, 1194:1198]
        cmpb = rt[:, 1200:1200 + NBLK + 1]
        goh = rt[:, 1260:1276].rearrange("p (t g) -> p t g", t=NLT)
        gra = rt[:, 1276:1292].rearrange("p (t g) -> p t g", t=NLT)
        gidxf = rt[:, 1292:1308].rearrange("p (t g) -> p t g", t=NLT)
        junk, junk2 = rt[:, 2304:3328], HTR[:, 4096:5120]
        rp = MP[:, 5648:6672].rearrange("p (i n) -> p i n", i=4)
        jk = MP[:, 6672:6928]
        wts = sb("wts", [P, 8, NLT])
        yk_of = [buf[:, 2048 * i:2048 * i + 2048].rearrange("p (k d) -> p k d", k=TOPK) for buf in (MP, HTR) for i in range(2)]

        def dram(name, shape, dt=F32):
            return nc.dram_tensor(name, shape, dt).ap()

        u_d = dram("u_d", [2 * P, CH, NCH])
        k_d = dram("k_d", [2, 2 * GRP, NPAIR, KW])
        y_d = dram("y_d", [2 * P, CH, NCL])
        xh_d = dram("xh_d", [LAT, D])
        slot_d = dram("slot_d", [NBLK * P, 2], I32)
        pair_d = dram("pair_d", [TOPK * LAT, D])

        plan = stream_plan()
        NL = len(plan)
        at = {what: n for n, what in enumerate(plan)}
        W1S, W3S, W2S = NL % RING, (NL + 1) % RING, (NL + 2) % RING
        w1s = W[:, W1S, :].rearrange("p (k h) -> p k h", k=KD)
        w3s = W[:, W3S, :].rearrange("p (k h) -> p k h", k=KD)
        w2s = W[:, W2S, :].rearrange("p (k d) -> p k d", k=4)
        w2_last = W[:, W1S, :].rearrange("p (k d) -> p k d", k=4)

        def wslot(n, width=512):
            return W[:, n % RING, 0:KD * width].rearrange("p (k n) -> p k n", k=KD)

        ztiles = [("u", h) for h in range(4)]
        ztiles += [("q", t) for t in range(NCT, NT)] + [("k", t) for t in range(NT)]
        ztiles += [("v", t) for t in range(NT)] + [("m", t) for t in range(NT)]
        ztiles += [("uq", t) for t in range(NCT, NT)] + [("ukv", t) for t in range(NT)]
        zi = {w: n for n, w in enumerate(ztiles)}
        turns = [w for w in ztiles if w[0] in ("q", "k", "m", "uq", "ukv")]
        ti = {w: n for n, w in enumerate(turns)}

        blocks = [("d", h, t) for h in range(DH) for t in range(NLT)] + [("l", h, t) for h in range(MH) for t in range(NLT)]
        units = [(b, m) for b, w in enumerate(blocks) for m in range(2 if w[0] == "d" else 1)]
        unit0 = {b: min(u for u, (bb, _) in enumerate(units) if bb == b) for b in range(len(blocks))}
        NHD = DH + MH
        six = {}
        for hd in range(NHD - 1):
            six[4 * hd + 4] = ("o", hd)
        for h in range(DH):
            six[4 * h + 5] = ("ss", h)
        for h, b in enumerate((21, 22, 25, 26)):
            six[b] = ("root", h)
        six[len(blocks)] = ("o", NHD - 1)
        six_n = {what: n for n, (b, what) in enumerate(sorted(six.items()))}
        assert len(six) == NHD + 2 * DH

        plan_mod = [what for what in plan if what[0] == "mod" and what[1] // 2 in (M_SH, M_SC, F_SH)]
        by_pool = [what for what in plan if what[0] == "mod" and what[1] // 2 in (F_SC, M_G)]
        summed_at = {6 * n + 6: n for n in range(len(by_pool))}

        def used(n):
            what = plan[n]
            if what[0] == "out":
                return sem("op"), 2 * NLT
            if what[0] == "in":
                kind = "uqkvm"[[Z_Q - S5W, Z_Q, Z_K, Z_V, Z_M].index(what[1])]
                return sem("z"), max(i for w, i in zi.items() if w[0] == kind) + 1
            if what in by_pool:
                return sem("mod_acc"), by_pool.index(what) + 1
            if what in plan_mod:
                return sem("mod_two"), plan_mod.index(what) + 1
            return sem("mod_wide"), what[1] - 2 * F_G + 1

        block = ctx.enter_context(nc.Block())

        @block.sync
        def _(sp):
            sp.dma_start(rows[R_C:R_C + 8], a["c"][0].rearrange("(r e) -> r e", e=P)).then_inc(sem("c_in"), 16)
            sp.dma_start(rows[R_CC:R_CC + 8], a["c_ctx"].rearrange("(r e) -> r e", e=P)).then_inc(sem("c_in"), 16)

            def load_tokens(t):
                src = a["ctx"][0, t * P:(t + 1) * P, :] if t < NCT else a["x"][0, (t - NCT) * P:(t - NCT + 1) * P, :]
                sp.dma_start(xs[:, t, :], src).then_inc(sem(f"tile_in{t}"), 16)

            for n, what in enumerate(plan):
                if n == 2:
                    sp.wait_ge(sem("rows_in"), 16 * 10)
                if n in (RING, RING + 1):
                    for t in (range(2) if n == RING else range(2, NT)):
                        load_tokens(t)
                if n >= RING:
                    sp.wait_ge(*used(n - RING))
                if what == ("out", 1):
                    sp.wait_ge(sem("scores"), unit0[DH * NLT])
                    for t in range(NLT):
                        sp.dma_start(XN[:, t, :], a["x"][0, t * P:(t + 1) * P, :]).then_inc(sem("xr_in"), 16)
                    sp.dma_start(GF, a["b_mod"][0][F_G * D:(F_G + 1) * D].partition_broadcast(P)).then_inc(sem("gf_in"), 16)
                if what[0] == "mod":
                    src = a["w_mod"][0][:, 512 * what[1]:512 * (what[1] + 1)]
                elif what[0] == "in":
                    src = a["w_in"][0][:, what[1]:what[1] + what[2]]
                else:
                    src = a["w_out"][0][:, 512 * what[1]:512 * (what[1] + 1)]
                sp.dma_start(wslot(n, src.shape[1]), src.rearrange("(k p) n -> p k n", p=P)).then_inc(
                    sem(f"ring_in{n % RING}"), 16)
            sp.wait_ge(sem("b6"), six_n[("o", DH - 1)] + 1)
            sp.dma_start(fng, a["final_norm_g"].partition_broadcast(P)).then_inc(sem("fng_in"), 16)

            sp.wait_ge(sem("routed"), 1)
            last2 = sp.value_load(btab[0:1, NBLK:NBLK + 1], min_val=LAT * TOPK // P - 2, max_val=NBLK - 2)

            def load(dst, name, b, used, loaded, count):
                e = sp.value_load(btab[0:1, b:b + 1] if isinstance(b, int) else btab[0:1, bass.ds(b, 1)],
                                  min_val=0, max_val=NE - 1)
                if used is not None:
                    sp.wait_ge(sem(used), count)
                src = a[name][0][bass.ds(e, 1)].rearrange("e (k p) n -> p (e k) n", p=P)
                sp.dma_start(dst, src).then_inc(sem(loaded), 16)

            sp.wait_ge(*used(NL - 3))
            load(w1s, "moe_w1", 0, None, "w1_in", 0)
            sp.wait_ge(*used(NL - 2))
            sp.wait_ge(sem("hg_in"), 16)
            load(w3s, "moe_w3", 0, None, "w3_in", 0)
            sp.wait_ge(*used(NL - 1))
            load(w2s, "moe_w2", 0, None, "w2_in", 0)
            load(w1s, "moe_w1", 1, "w1_used", "w1_in", 1)
            load(w3s, "moe_w3", 1, "w3_used", "w3_in", 1)
            with sp.Fori(2, last2 + 2) as b:
                load(w1s, "moe_w1", b, "w1_used", "w1_in", b)
                load(w3s, "moe_w3", b, "w3_used", "w3_in", b)
                load(w2s, "moe_w2", b - 1, "w2_used", "w2_in", b - 1)
            load(w2_last, "moe_w2", last2 + 1, "w1_used", "w2_last", last2 + 2)

            sp.wait_ge(sem("moe_done"), 1)
            for t in range(NLT):
                for k in range(TOPK):
                    sp.dma_start(yk_of[t][:, k, :], pair_d[k * LAT + t * P:k * LAT + (t + 1) * P, :]).then_inc(
                        sem(f"tile_in{t}"), 16)
            for t in range(NLT):
                sp.wait_ge(*((sem("fin"), t + 1) if t < 2 else (sem("fin_v"), t - 1)))
                sp.dma_start(out[0, t * P:(t + 1) * P, :], XN[:, t, :]).then_inc(sem("out_done"), 16)
            sp.wait_ge(sem("out_done"), 16 * NLT)

        @block.gpsimd
        def _(pool):
            st = Chain(pool, "pool_steps")
            st(pool.memset(CST[:, 0:P], 0.0))
            st(pool.memset(ones, 1.0))
            st(pool.memset(epsb[:, :], EPS))
            st(pool.memset(held[:, :], 0.0))
            st.settle()
            pool.affine_select(out=ident, in_=ident, compare_op=ALU.not_equal, fill=1.0, base=0,
                               pattern=[[-1, P]], channel_multiplier=1).then_inc(sem("ident"), 1)
            st(pool.affine_select(out=tri, in_=ones, compare_op=ALU.is_gt, fill=0.0, base=0,
                                  pattern=[[1, P]], channel_multiplier=-1))
            for nf, off in ((16, 0), (8, 16)):
                for i in range(nf):
                    st(pool.memset(freq[:, off + i:off + i + 1], float(ROPE_BASE ** (-i / nf) * INV_2PI)))
            for half in range(2):
                r = slice(GRID_W * half, GRID_W * half + GRID_W)
                st.settle()
                st(pool.iota(pos_i[r, 0, :], pattern=[[2, NLT]], base=half, channel_multiplier=0))
                st(pool.iota(pos_i[r, 1, :], pattern=[[0, NLT]], base=0, channel_multiplier=1))
            st.settle()
            for d in range(2):
                st(pool.iota(mul_i[:, d, 0:NPOW], pattern=[[1 if d == 0 else -1, NPOW]], base=0 if d == 0 else CH,
                             channel_multiplier=0))
            st(pool.iota(mul_i[:, 0, NPOW:], pattern=[[CH, NCH]], base=0, channel_multiplier=0))
            st(pool.iota(mul_i[:, 1, NPOW:NPOW + NCC], pattern=[[-CH, NCC]], base=CH * (NCC - 1), channel_multiplier=0))
            st(pool.iota(mul_i[:, 1, NPOW + NCC:], pattern=[[-CH, NCL]], base=CH * (NCH - 1), channel_multiplier=0))
            st(pool.iota(io_i[:, :], pattern=[[1, NBLK]], base=0, channel_multiplier=0))
            for k in range(TOPK):
                st(pool.iota(pair_i[:, k, :, 0], pattern=[[P, NLT]], base=0, channel_multiplier=1))
                st(pool.iota(pair_i[:, k, :, 1], pattern=[[P, NLT]], base=k * LAT, channel_multiplier=1))
            st(pool.memset(slots[:, :, :], SLOT_NONE))
            st.settle()
            pool.memset(epsb[:, :], EPS).then_inc(sem("consts"), 1)
            pool.dma_start(slot_d.rearrange("(r b) c -> r b c", r=P), slots[:, :, :]).then_inc(sem("slots_clear"), 16)
            pool.memset(S5R[0:2 * GRP, 4096:4096 + 7 * NPAIR * GRP], 0.0).then_inc(sem("kz"), 1)
            pool.wait_ge(sem("kz"), 1)
            kz = S5R[0:2 * GRP, 4096:4096 + 7 * NPAIR * GRP].rearrange("p (q m) -> p q m", q=NPAIR)
            pool.dma_start(k_d[0][:, :, 0:7 * GRP], kz).then_inc(sem("kpad_clear"), 16)
            pool.dma_start(k_d[1][:, :, 8 * GRP:15 * GRP], kz).then_inc(sem("kpad_clear"), 16)

            pool.wait_ge(sem("z_free"), 4)
            for h in range(2):
                pool.dma_start(u_d[h * P:(h + 1) * P], UT[:, h]).then_inc(sem("u_out"), 16)
            pool.wait_ge(sem("u_out"), 32)
            uv = u_d.rearrange("(g n) j c -> j n g c", n=GRP)
            for i in range(CH):
                pool.dma_start(UU[GRP * i:GRP * (i + 1)], uv[CH - 1 - i]).then_inc(sem("u_in"), 16)
            pool.wait_ge(sem("kpad_clear"), 32)
            for d in range(2):
                pool.wait_ge(sem("ksb"), 2 * (d + 1))
                lo = (7 if d == 0 else 0) * GRP
                pool.dma_start(k_d[d][:, :, lo:lo + P], ksb).then_inc(sem("k_out"), 16)
                pool.wait_ge(sem("k_out"), 16 * (d + 1))
                pool.wait_ge(sem("bu"), 4 * (d + 1))
                for i in range(CH):
                    pool.dma_start(TPL[GRP * i:GRP * (i + 1)].rearrange("n (q g) m -> n q g m", g=2),
                                   k_d[d].rearrange("(g n) q m -> n q g m", g=2)[:, :, :, GRP * i:GRP * i + P]).then_inc(
                        sem("t_in"), 16)
            pool.wait_ge(sem("yacc"), 4)
            yv = y_d.rearrange("(g n) j c -> j n g c", n=GRP)
            for j in range(CH):
                pool.dma_start(yv[j], yacc[GRP * j:GRP * (j + 1)]).then_inc(sem("y_out"), 16)
            pool.wait_ge(sem("y_out"), 16 * CH)
            for h in range(2):
                pool.dma_start(YT[:, h], y_d[h * P:(h + 1) * P]).then_inc(sem("y_in"), 16)

            pool.wait_ge(sem("s5_mix"), 2)
            pool.wait_ge(sem("turned"), len(turns))
            for n, what in enumerate(by_pool):
                w = wslot(at[what])
                pool.wait_ge(sem(f"ring_in{at[what] % RING}"), 16 * (at[what] // RING + 1))
                if n >= 1:
                    pool.wait_ge(sem("mod_acc"), n)
                if n >= 2:
                    pool.wait_ge(sem("mod_sum"), n - 1)
                acc = mod_acc[:, n % 2, :]
                st(pool.tensor_scalar(acc, w[:, 0, :], silu_c[:, 0, 0:1], None, ALU.mult))
                for k in range(1, KD):
                    st(pool.tensor_scalar(QR[:, k % 2, :], w[:, k, :], silu_c[:, k, 0:1], None, ALU.mult))
                    st.settle()
                    ins = pool.tensor_tensor(acc, acc, QR[:, k % 2, :], ALU.add)
                    if k < KD - 1:
                        st(ins)
                ins.then_inc(sem("mod_acc"), 1)

            for t in range(NLT):
                pool.wait_ge(sem("xhf"), t + 1)
                pool.dma_start(xh_d[t * P:(t + 1) * P, :], xhf[:, t, :]).then_inc(sem("xh_out"), 16)
            pool.wait_ge(sem("xh_out"), 16 * NLT)
            pool.wait_ge(sem("xhf_tr"), NLT)
            pool.memset(hg, 0.0).then_inc(sem("hg_clear"), 1)
            pool.wait_ge(sem("slots_clear"), 16)
            for k in range(TOPK):
                pool.wait_ge(sem("pos_k"), k + 1)
                for t in range(NLT):
                    pool.indirect_dma_start(slot_d, bass.IndirectOffsetOnAxis(pos_k[:, k, t:t + 1], 0),
                                            pair_i[:, k, t, :], None, bounds_check=NBLK * P - 1,
                                            oob_is_err=False).then_inc(sem("slot_out"), 16)
            pool.wait_ge(sem("slot_out"), 16 * TOPK * NLT)
            pool.dma_start(slots[:, :, :], slot_d.rearrange("(r b) c -> r b c", r=P)).then_inc(sem("slot_in"), 16)
            pool.wait_ge(sem("slot_in"), 16)
            pool.wait_ge(sem("routed"), 1)
            pool.wait_ge(sem("hg_clear"), 1)
            last2 = pool.value_load(btab[0:1, NBLK:NBLK + 1], min_val=LAT * TOPK // P - 2, max_val=NBLK - 2)

            cells = {}

            def hold(sm, count):
                pool.wait_ge(sm, count)
                if not isinstance(count, int):
                    cell = cells.setdefault(sm.name, len(cells) + 1)
                    pool.tensor_tensor(held[:, cell:cell + 1], held[:, 0:1], held[:, 0:1], ALU.add)

            def entry(b, c):
                return slots[:, b:b + 1, c] if isinstance(b, int) else slots[:, bass.ds(b, 1), c]

            def gather(b):
                pool.tensor_copy(gidx[:, :], entry(b, 0)).then_inc(sem("gidx"), 1)
                hold(sem("gidx"), b + 1)
                pool.indirect_dma_start(hg, None, xh_d, bass.IndirectOffsetOnAxis(gidx[:, 0:1], 0),
                                        bounds_check=LAT - 1, oob_is_err=False).then_inc(sem("hg_in"), 16)

            def scatter(b, ysb=ysb, sidx=sidx, last=False):
                if not isinstance(b, int) and not last:
                    hold(sem("y_sc"), 16 * b)
                pool.tensor_copy(sidx[:, :], entry(b, 1)).then_inc(sem("sidx"), 1)
                hold(sem("sidx"), b + 1)
                hold(sem("ysb"), 2 * b + 2)
                pool.indirect_dma_start(pair_d, bass.IndirectOffsetOnAxis(sidx[:, 0:1], 0), ysb, None,
                                        bounds_check=TOPK * LAT - 1, oob_is_err=False).then_inc(sem("y_sc"), 16)

            gather(0)
            hold(sem("hg_tr"), 1)
            gather(1)
            hold(sem("hg_tr"), 2)
            gather(2)
            scatter(0)
            with pool.Fori(1, last2) as b:
                hold(sem("hg_tr"), b + 2)
                gather(b + 2)
                scatter(b)
            scatter(last2)
            scatter(last2 + 1, ysb_last, sidx_last, True)
            hold(sem("y_sc"), 16 * (last2 + 2))
            pool.memset(gidx[:, :], 0).then_inc(sem("moe_done"), 1)
            pool.wait_ge(sem("fng_in"), 16)
            for t in range(2):
                pool.wait_ge(sem("normed"), t + 1)
                pool.tensor_tensor(XN[:, t, :], XN[:, t, :], fng, ALU.mult).then_inc(sem("fin"), 1)

        @block.tensor
        def _(pe):
            mm, tr = pe.matmul, pe.transpose
            pe.wait_ge(sem("ident"), 1)
            pe.wait_ge(sem("c_in"), 32)
            tr(bank(1, R_BMOD), rows[0:R_BMOD, :], ident[0:R_BMOD, 0:R_BMOD]).then_inc(sem("c_t"), 1)

            def ring_wait(n):
                pe.wait_ge(sem(f"ring_in{n % RING}"), 16 * (n // RING + 1))

            def mod_rows(n, dst):
                ring_wait(n)
                for k in range(KD):
                    ins = mm(dst, silu_c[:, k, :], wslot(n)[:, k, :], start=(k == 0), stop=(k == KD - 1))
                ins.then_inc(sem("mod_two"), 1)

            def turn_mod(i, b):
                pe.wait_ge(sem("modrow"), i + 1)
                for j in range(4):
                    ins = tr(bank(b, 2, 2 * j), modrow_of[i < 4][:, i % 2, j * P:(j + 1) * P], ident[0:2, 0:2])
                ins.then_inc(sem("modt"), 1)

            pe.wait_ge(sem("silu_c"), 1)
            for n in range(4):
                if n >= 2:
                    pe.wait_ge(sem("modrow"), n - 1)
                mod_rows(n, PS[0:2, 512 * (6 + n % 2):512 * (7 + n % 2)])
                if n == 1:
                    pe.wait_ge(sem("rows_in"), 16 * 10)
                    tr(bank(0, NROW), rows[0:NROW, :], ident[0:NROW, 0:NROW]).then_inc(sem("cols_t"), 1)
                    pe.wait_ge(sem("lsb"), 1)
                    tr(bank(4, 16), lsb[:, :, :].rearrange("p g s -> p (g s)"), ident[0:16, 0:16]).then_inc(sem("ls_t"), 1)
                if n >= 1:
                    pe.wait_ge(sem("modc"), n)
                turn_mod(n, 5)

            for t in range(NT):
                pe.wait_ge(sem("xh"), t + 1)
                if t >= 2:
                    pe.wait_ge(sem("hT_a"), t - 1)
                    pe.wait_ge(sem("hT_d"), t - 1)
                for k in range(KD):
                    ins = tr(bank(2 * (t % 2) + k // 4, P, (k % 4) * P), xh[:, t % 2, k * P:(k + 1) * P], ident)
                ins.then_inc(sem("xh_tr"), 1)
            pe.wait_ge(sem("hT_a"), NT)
            pe.wait_ge(sem("hT_d"), NT)

            def z_bank(w):
                n = zi[w]
                if n >= 4:
                    pe.wait_ge(sem("z_free"), n - 3)
                return bank(n % 4)

            n = at[("in", 0, S5W)]
            ring_wait(n)
            for h in range(4):
                dst = z_bank(("u", h))
                t0, nt = (0, 512) if h % 2 == 0 else (512, 256)
                for k in range(KD):
                    ins = mm(dst[:, 0:nt], wslot(n, S5W)[:, k, (h // 2) * P:(h // 2 + 1) * P], hT[:, k, t0:t0 + nt],
                             start=(k == 0), stop=(k == KD - 1))
                ins.then_inc(sem("z"), 1)

            pe.wait_ge(sem("cn_in"), 16 * 4)
            for i in range(8):
                ins = tr(bank(6 + i // 4, P, (i % 4) * P), cn[:, i, :], ident)
            ins.then_inc(sem("ct_t"), 1)
            pe.wait_ge(sem("bc"), 1)

            def turn_tile(w):
                n = ti[w]
                pe.wait_ge(sem("qr"), n + 1)
                if n >= 2:
                    pe.wait_ge(sem("turned_out"), n - 1)
                b = 4 + n % 2
                src = QR[:, n % 2, :]
                if w[0] in ("q", "k"):
                    for h in range(DH):
                        ins = tr(bank(b, P, h * P), src[:, h * P:(h + 1) * P], ident)
                elif w[0] == "m":
                    lat = w[1] >= NCT
                    for j in range(0 if lat else 2, 3):
                        ins = tr(bank(b, P, j * P), src[:, j * P:(j + 1) * P], ident)
                else:
                    for h in range(MH):
                        ins = tr(PS[0:MQ, 512 * b + h * P:512 * b + (h + 1) * P], src[:, h * MQ:(h + 1) * MQ], ident)
                ins.then_inc(sem("turned"), 1)

            def project(kind, t):
                w = (kind, t)
                dst = z_bank(w)
                tok = slice(t * P, (t + 1) * P)
                if kind in "qkvm":
                    col, width = {"q": (Z_Q, 512), "k": (Z_K, 512), "v": (Z_V, 512), "m": (Z_M, Z_ALL - Z_M)}[kind]
                    n = at[("in", col, width)]
                    ring_wait(n)
                    c0 = QRANK if kind == "m" and t < NCT else 0
                    for k in range(KD):
                        ins = mm(dst[:, c0:width], hT[:, k, tok], wslot(n, width)[:, k, c0:width],
                                 start=(k == 0), stop=(k == KD - 1))
                elif kind == "uq":
                    lt = slice((t - NCT) * P, (t - NCT + 1) * P)
                    for k in range(2):
                        ins = mm(dst[:, 0:MH * MQ], CQT[:, k, lt], wuq[:, k, :], start=(k == 0), stop=(k == 1))
                else:
                    ins = mm(dst, CKVT[:, tok], wukv[:, :], start=True, stop=True)
                ins.then_inc(sem("z"), 1)

            def s5_kernel(d):
                pe.wait_ge(sem("pb"), d + 1)
                if d == 1:
                    pe.wait_ge(sem("yacc"), 2)
                for c in range(4):
                    if c >= 2:
                        pe.wait_ge(sem("pbt"), 4 * d + c - 1)
                    for j in range(4):
                        r, q = divmod(4 * c + j, NPAIR)
                        ins = tr(bank(6 + c % 2, P, j * P), PB[:, r, q].rearrange("p i n -> p (i n)"), ident)
                    ins.then_inc(sem("pb_t"), 1)
                pe.wait_ge(sem("cl"), d + 1)
                k0 = 0 if d == 0 else 1
                for c in range(2):
                    pe.wait_ge(sem("pbt"), 4 * d + c + 3)
                    for j in range(4):
                        q = 4 * c + j
                        for r in range(2):
                            ins = mm(PS[0:2 * GRP, 512 * (6 + c) + j * P:512 * (6 + c) + (j + 1) * P], BBar[:, r, q, :],
                                     CL[:, r, q, k0:k0 + CH, :].rearrange("p k n -> p (k n)"),
                                     start=(r == 0), stop=(r == 1))
                    ins.then_inc(sem("kk"), 1)

            def s5_inputs(d):
                pe.wait_ge(sem("pbt"), 4 * (d + 1))
                pe.wait_ge(sem("u_in"), 16 * CH)
                for c in range(4):
                    r, hq = divmod(c, 2)
                    if c < 2:
                        pe.wait_ge(sem("ksb"), 2 * d + c + 1)
                    else:
                        pe.wait_ge(sem("bu_out"), 4 * d + c - 1)
                    for j in range(4):
                        q = 4 * hq + j
                        for g2 in range(2):
                            at0 = 512 * (6 + c % 2) + j * NCH
                            ins = mm(PS[NS * g2:NS * g2 + NS, at0:at0 + NCH],
                                     PBT[:, r, q, NS * g2:NS * g2 + NS], UU[:, 2 * q + g2, :], start=True, stop=True)
                    ins.then_inc(sem("bu"), 1)

            def s5_outputs(d):
                pe.wait_ge(sem("t_in"), 16 * CH * (d + 1))
                pe.wait_ge(sem("hh"), d + 1)
                k0, c0 = (1, NCC - 1) if d == 0 else (0, NCC + 1)
                for g2 in range(2):
                    if d == 1:
                        pe.wait_ge(sem("yacc"), 2)
                    s = slice(NS * g2, NS * g2 + NS)
                    for q in range(NPAIR):
                        dst = bank(7 - g2, NCL, q * NCL)
                        mm(dst, TPL[:, 2 * q + g2, :], UU[:, 2 * q + g2, NCC:NCH], start=True, stop=False)
                        for r in range(2):
                            ins = mm(dst, CL[s, r, q, k0:k0 + CH, :].rearrange("p k n -> p (k n)"),
                                     HH[s, r, q, c0:c0 + NCL], start=False, stop=(r == 1))
                    ins.then_inc(sem("yy"), 1)

            for t in range(NCT, NT):
                project("q", t)
            s5_kernel(0)
            for t in range(NCT, NT):
                turn_tile(("q", t))
                if t < NT - 1:
                    project("k", t - NCT)
            s5_inputs(0)
            for t in range(3, NT):
                project("k", t)
                turn_tile(("k", t - 3))
            s5_outputs(0)
            for t in range(NT):
                project("v", t)
                if t < 3:
                    turn_tile(("k", t + 3))
            s5_kernel(1)
            s5_inputs(1)
            for t in range(4):
                project("m", t)
            s5_outputs(1)
            for t in range(NT):
                turn_tile(("m", t))
                if t + 4 < NT:
                    project("m", t + 4)
                elif t < 4:
                    i = t + 2
                    pe.wait_ge(sem("yacc"), 4)
                    mod_rows(at[plan_mod[i]], PS[0:2, 512 * (6 + i % 2):512 * (7 + i % 2)])
            for i in (4, 5):
                turn_mod(i, 6 + i % 2)
            pe.wait_ge(sem("yg"), 1)
            pe.wait_ge(sem("small_in"), 16 * 7)
            pe.wait_ge(sem("modc"), 6)
            for mo in range(2):
                for k in range(2):
                    ins = mm(bank(6 + mo), wglu[:, k, mo * P:(mo + 1) * P], YG[:, k].rearrange("p j c -> p (j c)"),
                             start=(k == 0), stop=(k == 1))
            ins.then_inc(sem("glu"), 1)

            pe.wait_ge(sem("turned_out"), ti[("m", NT - 1)] + 1)
            pe.wait_ge(sem("s5_mix"), 2)
            up = [("uq", t) for t in range(NCT, NT)] + [("ukv", t) for t in range(NT)]
            for n, w in enumerate(up):
                project(*w)
                if n >= 2:
                    turn_tile(up[n - 2])
            turn_tile(up[-2])
            turn_tile(up[-1])
            pe.wait_ge(sem("turned_out"), len(turns))
            pe.wait_ge(sem("z_free"), len(ztiles))

            def scores(b):
                kind, h, t = blocks[b]
                for m in range(2 if kind == "d" else 1):
                    u = unit0[b] + m
                    if u >= 2:
                        pe.wait_ge(sem("probs"), u - 1)
                    if kind == "d":
                        s, kt, qt = slice(DHD * m, DHD * m + DHD), KT, QT
                    else:
                        s, kt, qt = slice(0, MQ), MKT, MQT
                    base = 1024 * (u % 2)
                    for k0, kn in ((0, 512), (512, TOK - 512)):
                        ins = mm(PS[:, base + k0:base + k0 + kn], qt[s, h, t * P:(t + 1) * P], kt[s, h, k0:k0 + kn],
                                 start=True, stop=True)
                    ins.then_inc(sem("scores"), 1)

            def turn_probs(b):
                pe.wait_ge(sem("pc"), b + 1)
                if b >= 1:
                    pe.wait_ge(sem("pt_out"), b)
                kind, h, t = blocks[b]
                src = pbuf[:, 2 * (b % 2) + (1 if kind == "d" else 0), :]
                for k in range(NT):
                    ins = tr(PS[:, 2048 + k * P:2048 + (k + 1) * P], src[:, k * P:(k + 1) * P], ident)
                ins.then_inc(sem("pt"), 1)

            def bank6(what):
                if six_n[what] >= 1:
                    pe.wait_ge(sem("b6_free"), six_n[what])

            def values(hd):
                pe.wait_ge(sem("pt_out"), 4 * hd + 4)
                bank6(("o", hd))
                for k in range(NT):
                    lhs = VV[:, k, hd * P:(hd + 1) * P] if hd < DH else MVV[:, k, ((hd - DH) // 2) * P:((hd - DH) // 2 + 1) * P]
                    ins = mm(bank(6), lhs, pT[:, hd % 2, k, :], start=(k == 0), stop=(k == NT - 1))
                ins.then_inc(sem("b6"), 1)

            def squares(h):
                bank6(("ss", h))
                pe.wait_ge(sem("sq"), h + 1)
                for t in range(NLT):
                    ins = mm(bank(6, 1, t), sq[:, t * P:(t + 1) * P], ones[:, 0:1], start=True, stop=True)
                ins.then_inc(sem("b6"), 1)

            def roots(h):
                bank6(("root", h))
                pe.wait_ge(sem("diag"), h + 1)
                mm(bank(6), ones, sq, start=True, stop=True).then_inc(sem("b6"), 1)

            def wide_rows(what, b, part):
                n = at[what]
                if part == 0:
                    ring_wait(n)
                for k in range(KD // 2 * part, KD // 2 * (part + 1)):
                    ins = mm(bank(b), silu_cb[:, k, :], wslot(n)[:, k, :], start=(k == 0), stop=(k == KD - 1))
                if part == 1:
                    ins.then_inc(sem("mod_wide"), 1)

            def sum_rows(n):
                pe.wait_ge(sem("mod_acc"), n + 1)
                if n >= 1:
                    pe.wait_ge(sem("b7_free"), n)
                if n < 2:
                    for j in range(4):
                        ins = mm(bank(7, 1, j), mod_acc[:, n % 2, j * P:(j + 1) * P], ones[:, 0:1], start=True, stop=True)
                else:
                    ins = mm(bank(7), ones, mod_acc[:, n % 2, :], start=True, stop=True)
                ins.then_inc(sem("mod_sum"), 1)

            pe.wait_ge(sem("silu_cb"), 1)
            scores(0)
            for b in range(len(blocks)):
                if b + 1 < len(blocks):
                    scores(b + 1)
                if six.get(b, ("",))[0] == "ss":
                    squares(six[b][1])
                if six.get(b, ("",))[0] == "root":
                    roots(six[b][1])
                if b in summed_at:
                    sum_rows(summed_at[b])
                turn_probs(b)
                if b % 4 == 0 and b >= 4:
                    values(b // 4 - 1)
            values(NHD - 1)

            pe.wait_ge(sem("b6_free"), len(six))
            def turn_normed(t):
                pe.wait_ge(sem("xhf"), t + 1)
                if t >= 2:
                    pe.wait_ge(sem("hfT_a"), t - 1)
                    pe.wait_ge(sem("hfT_d"), t - 1)
                for k in range(KD):
                    ins = tr(bank(4 + 2 * (t % 2) + k // 4, P, (k % 4) * P), xhf[:, t, k * P:(k + 1) * P], ident)
                ins.then_inc(sem("xhf_tr"), 1)

            for t in range(NLT):
                for half in range(2):
                    n = at[("out", half)]
                    if t == 0:
                        ring_wait(n)
                    i = 2 * t + half
                    if i >= 4:
                        pe.wait_ge(sem("xn"), i - 3)
                    for k in range(KD):
                        ins = mm(bank(i % 4), mix[:, k, t * P:(t + 1) * P], wslot(n)[:, k, :], start=(k == 0), stop=(k == KD - 1))
                    ins.then_inc(sem("op"), 1)
                if t >= 1:
                    turn_normed(t - 1)
            pe.wait_ge(sem("xn"), 5)
            for t in range(NLT):
                if t == NLT // 2:
                    turn_normed(NLT - 1)
                pe.wait_ge(sem("hfT_a"), t + 1)
                pe.wait_ge(sem("hfT_d"), t + 1)
                for k in range(KD):
                    ins = mm(bank(0, NGR + NE, t * (NGR + NE)), hfT[:, k, t * P:(t + 1) * P], wrt[:, k, :],
                             start=(k == 0), stop=(k == KD - 1))
            ins.then_inc(sem("logits"), 1)
            pe.wait_ge(sem("xn"), 2 * NLT)
            for part in range(2):
                wide_rows(("mod", 2 * F_G), 2, part)
            wide_rows(("mod", 2 * F_G + 1), 3, 0)
            pe.wait_ge(sem("mask"), 1)
            for t in range(NLT):
                ins = mm(PS[0:NE, 2560:2561], mask[:, t, :], ones[:, 0:1], start=(t == 0), stop=(t == NLT - 1))
            ins.then_inc(sem("cnt"), 1)
            pe.wait_ge(sem("nb"), 1)
            mm(PS[0:NE, 2562:2563], tri_inc[0:NE, :], nbv[0:NE, 0:1], start=True, stop=True).then_inc(sem("ends"), 1)
            for t in range(NLT):
                dst = bank(6, NE, t * NE)
                mm(dst, nb_b[0:NE, :], tri128[0:NE, :], start=True, stop=False)
                for t2 in range(t):
                    mm(dst, ones, mask[:, t2, :], start=False, stop=False)
                ins = mm(dst, tri, mask[:, t, :], start=False, stop=True)
            ins.then_inc(sem("place"), 1)
            pe.wait_ge(sem("cmp"), 1)
            mm(PS[0:1, 3584:3584 + NBLK + 1], ones[0:NE, 0:1], cmpb[0:NE, :], start=True, stop=True).then_inc(sem("bt"), 1)
            wide_rows(("mod", 2 * F_G + 1), 3, 1)

            pe.wait_ge(sem("routed"), 1)
            last2 = pe.value_load(btab[0:1, NBLK:NBLK + 1], min_val=LAT * TOPK // P - 2, max_val=NBLK - 2)

            def turn_rows(b):
                pe.wait_ge(sem("hg_in"), 16 * b + 16)
                if not isinstance(b, int) or b >= 1:
                    pe.wait_ge(sem("hgT_a"), b)
                    pe.wait_ge(sem("hgT_d"), b)
                for k in range(KD):
                    ins = tr(bank(k // 4, P, (k % 4) * P), hg[:, k * P:(k + 1) * P], ident)
                ins.then_inc(sem("hg_tr"), 1)

            def up(b):
                pe.wait_ge(sem("hgT_a"), b + 1)
                pe.wait_ge(sem("hgT_d"), b + 1)
                if isinstance(b, int) and b == 0:
                    pe.wait_ge(sem("gf"), 2)
                else:
                    pe.wait_ge(sem("hid"), b)
                pe.wait_ge(sem("w1_in"), 16 * b + 16)
                for k in range(KD):
                    ins = mm(bank(2), hgT[:, k, :], w1s[:, k, :], start=(k == 0), stop=(k == KD - 1))
                ins.then_inc(sem("w1_used"), 1)
                pe.wait_ge(sem("w3_in"), 16 * b + 16)
                for k in range(KD):
                    ins = mm(bank(3), hgT[:, k, :], w3s[:, k, :], start=(k == 0), stop=(k == KD - 1))
                ins.then_inc(sem("w3_used"), 1)

            def turn_hid(b):
                pe.wait_ge(sem("hid"), b + 1)
                for k in range(4):
                    ins = tr(bank(4, P, k * P), hid[:, k * P:(k + 1) * P], ident)
                ins.then_inc(sem("hid_t"), 1)

            def down(b, w2s=w2s, b0=5, last=False):
                pe.wait_ge(sem("hidT"), b + 1)
                if last:
                    pe.wait_ge(sem("w2_last"), 16)
                else:
                    pe.wait_ge(sem("w2_in"), 16 * b + 16)
                    if not isinstance(b, int) or b >= 1:
                        pe.wait_ge(sem("ysb"), 2 * b)
                for n in range(2):
                    for k in range(4):
                        ins = mm(bank(b0 + n), hidT[:, k, :], w2s[:, k, 512 * n:512 * (n + 1)], start=(k == 0), stop=(k == 3))
                ins.then_inc(sem("w2_used"), 1)

            turn_rows(0)
            up(0)
            turn_rows(1)
            turn_hid(0)
            up(1)
            turn_rows(2)
            down(0)
            turn_hid(1)
            with pe.Fori(2, last2 + 1) as b:
                up(b)
                turn_rows(b + 1)
                down(b - 1)
                turn_hid(b)
            up(last2 + 1)
            down(last2)
            turn_hid(last2 + 1)
            down(last2 + 1, w2_last, 0, True)

        @block.scalar
        def _(act):
            A = nc.scalar.activation
            def small(dst, src, name):
                act.dma_start(dst, src).then_inc(sem(name), 16)

            def vec(ap, n):
                return ap.rearrange("(r e) -> r e", e=P)[0:n]
            small(rows[R_BMOD:R_BMOD + 48], vec(a["b_mod"][0], 48), "rows_in")
            act.wait_ge(sem("c_cols"), 1)
            A(silu_t[:, :], cols[:, 0:16], ACT.Sigmoid).then_inc(sem("sig_c"), 1)
            small(rows[R_GMIX:R_GMIX + 8], vec(a["norm_mix_g"][0], 8), "rows_in")
            small(rows[R_GFFN:R_GFFN + 8], vec(a["norm_ffn_g"][0], 8), "rows_in")
            small(rows[R_SD:R_SD + 2], vec(a["s5_d"][0], 2), "rows_in")
            small(rows[R_BGLU:R_BGLU + 2], vec(a["s5_b_glu"][0], 2), "rows_in")
            small(rows[R_QN:R_QN + 2], vec(a["mla_q_norm_g"][0], 2), "rows_in")
            small(rows[R_KVN:R_KVN + 1], vec(a["mla_kv_norm_g"][0], 1), "rows_in")
            small(rows[R_SUB:R_SUB + 1], vec(a["diff_subln_g"][0], 1), "rows_in")
            small(rows[R_ARE:R_ARE + 16], a["s5_a_re"][0].rearrange("d (q g) p -> (d q) (g p)", g=2), "rows_in")
            small(rows[R_AIM:R_AIM + 16], a["s5_a_im"][0].rearrange("d (q g) p -> (d q) (g p)", g=2), "rows_in")
            small(lst[:, :], a["s5_log_step"][0].rearrange("d (q g) -> (d q) g", g=2), "lst_in")
            small(lamr, a["diff_lambda"][0].rearrange("a b -> (a b)").partition_broadcast(P), "lam_in")
            for r, name in enumerate(("s5_b_re", "s5_b_im")):
                small(BC[:, r], a[name][0].rearrange("d (q g) p n -> (g p) (d q) n", g=2), "b_in")
            for r, name in enumerate(("s5_c_re", "s5_c_im")):
                for twice in range(2):
                    small(cn[:, 4 * r:4 * r + 4, NS * twice:NS * (twice + 1)],
                          a[name][0].rearrange("d (h g) n p -> (g n) (d h) p", h=2), "cn_in")

            act.wait_ge(sem("consts"), 1)

            ajk = Chain(act, "act_steps")

            def root_ms(src, n, dst, what, jnk):
                ajk(A(jnk, src, ACT.Square, accum_out=dst))
                ajk.settle()
                A(dst, dst, ACT.Sqrt, scale=1.0 / n, bias=epsb[:, 0:1]).then_inc(sem(what), 1)

            def mod_copy(i, b):
                act.wait_ge(sem("mod_two"), i + 1)
                if i >= 2:
                    act.wait_ge(sem("modt"), i - 1)
                A(modrow_of[i < 4][:, i % 2, :], PS[0:2, 512 * b:512 * b + 512], ACT.Copy).then_inc(sem("modrow"), 1)

            def squares_of(t):
                act.wait_ge(sem(f"tile_in{t}"), 16)
                root_ms(xs[:, t, :], D, sml[:, t:t + 1], "x_ms", junk)

            mod_copy(0, 6)
            mod_copy(1, 7)
            small(GM[:, :], a["b_mod"][0][M_G * D:(M_G + 1) * D].partition_broadcast(P), "gm_in")
            small(wglu[:, :, :], a["s5_w_glu"][0].rearrange("(k p) n -> p k n", p=P), "small_in")
            small(wuq[:, :, :], a["mla_w_uq"][0].rearrange("(k p) n -> p k n", p=P), "small_in")
            small(wukv[:, :], a["mla_w_ukv"][0], "small_in")
            small(wrt[:, :, 0:NGR], a["moe_w_group"][0].rearrange("(k p) n -> p k n", p=P), "small_in")
            small(wrt[:, :, NGR:], a["moe_w_router"][0].rearrange("(k p) n -> p k n", p=P), "small_in")
            small(brt[:, 0:NGR], a["moe_b_group"][0].partition_broadcast(P), "small_in")
            small(brt[:, NGR:], a["moe_b_router"][0].partition_broadcast(P), "small_in")
            for t in range(2):
                squares_of(t)
            mod_copy(2, 6)
            for t in range(2, 4):
                squares_of(t)
            mod_copy(3, 7)
            for t in range(4, NT):
                squares_of(t)

            act.wait_ge(sem("gmc"), 1)
            for t in range(NT):
                act.wait_ge(sem("xh_tr"), t + 1)
                v = 1 if t < NCT else 0
                for k in range(4):
                    ins = A(hT[:, k, t * P:(t + 1) * P], bank(2 * (t % 2), P, k * P), ACT.Identity,
                            scale=gmc[:, k, v:v + 1], bias=modc[:, 8 * M_SH + k, v:v + 1])
                ins.then_inc(sem("hT_a"), 1)

            act.wait_ge(sem("turns"), 1)
            A(turn[:, 2], turn[:, 0], ACT.Sin, scale=TWO_PI_DOWN).then_inc(sem("rope_t"), 1)
            A(turn[:, 1], turn[:, 1], ACT.Sin, scale=TWO_PI_DOWN).then_inc(sem("rope_t"), 1)
            act.wait_ge(sem("ls_t"), 1)
            A(s5p[:, 0, :], bank(4, 16), ACT.Exp).then_inc(sem("step"), 1)
            act.wait_ge(sem("lam_s"), 1)
            A(sml[:, 490:492], sml[:, 490:492], ACT.Exp).then_inc(sem("lam_e"), 1)
            act.wait_ge(sem("ars"), 1)
            A(s5p[:, 3, :], s5p[:, 1, :], ACT.Exp, scale=float(CH)).then_inc(sem("r8"), 1)

            def s5_tables(d):
                act.wait_ge(sem("ang"), d + 1)
                ang = (st2, st1)
                for r in range(2):
                    src = ang[r][:, 0:NPAIR * (NPOW + NCH)].rearrange("p (q m) -> p q m", q=NPAIR)
                    A(LP[:, r], src[:, :, 0:NPOW], ACT.Sin, scale=TWO_PI_DOWN)
                    A(ECS[:, r], src[:, :, NPOW:], ACT.Sin, scale=TWO_PI_DOWN)
                A(EM, EM, ACT.Exp).then_inc(sem("tabs"), 1)

            def turn_out(w):
                n = ti[w]
                act.wait_ge(sem("turned"), n + 1)
                kind, t = w
                b = 4 + n % 2
                src = bank(b).rearrange("p (h t) -> p h t", h=4)
                lt = slice((t - NCT) * P, (t - NCT + 1) * P)
                tok = slice(t * P, (t + 1) * P)
                if kind == "q":
                    ins = A(QT[:, :, lt], src, ACT.Copy)
                elif kind == "k":
                    ins = A(KT[:, :, tok], src, ACT.Copy)
                elif kind == "uq":
                    ins = A(MQT[0:MQ, :, lt], src[0:MQ], ACT.Copy)
                elif kind == "ukv":
                    ins = A(MKT[0:MQ, :, tok], src[0:MQ], ACT.Copy)
                else:
                    if t >= NCT:
                        for j in range(2):
                            A(CQT[:, j, lt], src[:, j], ACT.Copy, scale=cols[:, R_QN + j:R_QN + j + 1])
                    ins = A(CKVT[:, tok], src[:, 2], ACT.Copy, scale=cols[:, R_KVN:R_KVN + 1])
                ins.then_inc(sem("turned_out"), 1)

            def s5_evac(d):
                for c in range(4):
                    act.wait_ge(sem("pb_t"), 4 * d + c + 1)
                    A(PBT[:, c // 2, 4 * (c % 2):4 * (c % 2) + 4].rearrange("p q s -> p (q s)"), bank(6 + c % 2), ACT.Copy).then_inc(
                        sem("pbt"), 1)
                for c in range(2):
                    act.wait_ge(sem("kk"), 2 * d + c + 1)
                    A(ksb[:, 4 * c:4 * c + 4, :].rearrange("p q m -> p (q m)"), PS[0:2 * GRP, 512 * (6 + c):512 * (7 + c)], ACT.Copy).then_inc(
                        sem("ksb"), 1)

            s5_tables(0)
            s5_evac(0)
            for t in range(NCT, NT):
                turn_out(("q", t))
            for t in range(NT):
                turn_out(("k", t))
            s5_tables(1)
            s5_evac(1)
            def squares_of_m(t):
                act.wait_ge(sem("z"), zi[("m", t)] + 1)
                src = bank(zi[("m", t)] % 4)
                if t >= NCT:
                    ajk(A(jk[:, 0:QRANK], src[:, 0:QRANK], ACT.Square, accum_out=sml[:, 16 + t:17 + t]))
                    ajk.settle()
                ajk(A(jk[:, 0:KVRANK], src[:, QRANK:QRANK + KVRANK], ACT.Square, accum_out=sml[:, 24 + t:25 + t]))
                ajk.settle()
                if t >= NCT:
                    A(sml[:, 16 + t:17 + t], sml[:, 16 + t:17 + t], ACT.Sqrt, scale=1.0 / QRANK, bias=epsb[:, 0:1])
                A(sml[:, 24 + t:25 + t], sml[:, 24 + t:25 + t], ACT.Sqrt, scale=1.0 / KVRANK, bias=epsb[:, 0:1]).then_inc(
                    sem("m_ms"), 1)
            squares_of_m(0)
            for t in range(NT):
                if t + 1 < NT:
                    squares_of_m(t + 1)
                if t == 4:
                    act.wait_ge(sem("gelu_in"), 1)
                    A(yt1, yt1, ACT.Tanh, scale=math.sqrt(2.0 / math.pi)).then_inc(sem("tanh"), 1)
                if t >= 4:
                    mod_copy(t, 6 + t % 2)
                turn_out(("m", t))
            act.wait_ge(sem("glu"), 1)
            for mo in range(2):
                A(yt1[:, mo].rearrange("p j c -> p (j c)"), bank(6 + mo), ACT.Sigmoid,
                  bias=cols[:, R_BGLU + mo:R_BGLU + mo + 1]).then_inc(sem("s5_sig"), 1)
            for kind, first in (("uq", NCT), ("ukv", 0)):
                for t in range(first, NT):
                    turn_out((kind, t))

            def probs(b):
                kind, h, t = blocks[b]
                if b >= 2:
                    act.wait_ge(sem("pt"), b - 1)
                for m in range(2 if kind == "d" else 1):
                    u = unit0[b] + m
                    act.wait_ge(sem("nmax"), u + 1)
                    base = 1024 * (u % 2)
                    A(pbuf[:, 2 * (b % 2) + m, :], PS[:, base:base + TOK], ACT.Exp, bias=sml[:, 64 + u:65 + u],
                      scale=DSCALE if kind == "d" else MSCALE, accum_out=sml[:, 160 + u:161 + u]).then_inc(sem("probs"), 1)

            def probs_out(b):
                kind, h, t = blocks[b]
                hd = b // 4
                if hd >= 2:
                    act.wait_ge(sem("b6"), six_n[("o", hd - 2)] + 1)
                act.wait_ge(sem("pt"), b + 1)
                A(pT[:, hd % 2, :, t * P:(t + 1) * P], PS[:, 2048:2048 + TOK].rearrange("p (k q) -> p k q", k=NT), ACT.Copy).then_inc(sem("pt_out"), 1)

            def head_out(hd):
                act.wait_ge(sem("b6"), six_n[("o", hd)] + 1)
                if hd < DH:
                    A(mix[:, 2 + hd, :], bank(6), ACT.Copy).then_inc(sem("b6_free"), 1)
                    if hd >= 1:
                        act.wait_ge(sem("b6"), six_n[("ss", hd - 1)] + 1)
                    act.wait_ge(sem("b6_free"), six_n[("o", hd)] + 1)
                    A(sq, mix[:, 2 + hd, :], ACT.Square).then_inc(sem("sq"), 1)
                else:
                    r = slice(MV * (hd % 2), MV * (hd % 2) + MV)
                    A(mix[r, 6 + (hd - DH) // 2, :], PS[r, 3072:3584], ACT.Copy).then_inc(sem("b6_free"), 1)

            probs(0)
            for b in range(len(blocks)):
                if b + 1 < len(blocks):
                    probs(b + 1)
                probs_out(b)
                if b % 4 == 0 and b >= 4:
                    head_out(b // 4 - 1)
                if b == 4 * DH + 3:
                    act.wait_ge(sem("ssq"), DH)
                    A(ssq, ssq, ACT.Sqrt, scale=1.0 / P, bias=epsb[:, 0:1]).then_inc(sem("rms"), 1)
            head_out(NHD - 1)

            act.wait_ge(sem("gfc"), 1)
            for t in range(NLT):
                act.wait_ge(sem("xn"), 2 * t + 2)
                root_ms(XN[:, t, :], D, sml[:, 32 + t:33 + t], "xn_ms", junk2)
                if t >= 1:
                    for t2 in ([t - 1] if t < NLT - 1 else [t - 1, t]):
                        act.wait_ge(sem("xhf_tr"), t2 + 1)
                        for k in range(4):
                            ins = A(hfT[:, k, t2 * P:(t2 + 1) * P], bank(4 + 2 * (t2 % 2), P, k * P), ACT.Identity,
                                    scale=gfc[:, k:k + 1], bias=modc[:, 8 * F_SH + k, 0:1])
                        ins.then_inc(sem("hfT_a"), 1)
            act.wait_ge(sem("g_in"), 1)
            A(gra, gra, ACT.Exp).then_inc(sem("g_exp"), 1)
            act.wait_ge(sem("e_in"), 1)
            A(wts[:, 4, :], wts[:, 4, :], ACT.Exp).then_inc(sem("e_exp"), 1)

            act.wait_ge(sem("routed"), 1)
            last2 = act.value_load(btab[0:1, NBLK:NBLK + 1], min_val=LAT * TOPK // P - 2, max_val=NBLK - 2)

            def rows_T(b):
                act.wait_ge(sem("hg_tr"), b + 1)
                for k in range(4):
                    ins = A(hgT[:, k, :], bank(0, P, k * P), ACT.Identity, scale=gfc[:, k:k + 1],
                            bias=modc[:, 8 * F_SH + k, 0:1])
                ins.then_inc(sem("hgT_a"), 1)

            def silu(b):
                act.wait_ge(sem("w1_used"), b + 1)
                if not isinstance(b, int) or b >= 1:
                    act.wait_ge(sem("hid"), b)
                A(sg, bank(2), ACT.Silu).then_inc(sem("sg"), 1)

            def hidden_T(b):
                act.wait_ge(sem("hid_t"), b + 1)
                A(hidT.rearrange("p k s -> p (k s)"), bank(4), ACT.Copy).then_inc(sem("hidT"), 1)

            rows_T(0)
            silu(0)
            rows_T(1)
            hidden_T(0)
            silu(1)
            rows_T(2)
            hidden_T(1)
            with act.Fori(2, last2 + 1) as b:
                silu(b)
                rows_T(b + 1)
                hidden_T(b)
            silu(last2 + 1)
            hidden_T(last2 + 1)
            def scale(t):
                act.wait_ge(sem("f_root"), t + 1)
                A(XN[:, t, :], XN[:, t, :], ACT.Copy, scale=sml[:, 44 + t:45 + t]).then_inc(sem("normed"), 1)

            for t in range(NLT):
                act.wait_ge(sem("x_out"), t + 1)
                root_ms(XN[:, t, :], D, sml[:, 40 + t:41 + t], "f_ms", junk2)
                if 1 <= t <= 2:
                    scale(t - 1)

        @block.vector
        def _(dve):
            V = nc.vector
            st = Chain(dve, "dve_steps")
            tt, ts, stt, cp = V.tensor_tensor, V.tensor_scalar, V.scalar_tensor_tensor, V.tensor_copy

            def bc(ap, n, axis):
                x = ap.unsqueeze(axis)
                shape = list(x.shape)
                shape[axis] = n
                return x.to_broadcast(shape)

            def fraction(x, tmp):
                st(ts(tmp, x, MAGIC, MAGIC, ALU.add, ALU.subtract))
                st.settle()
                st(tt(x, x, tmp, ALU.subtract))
                st.settle()

            dve.wait_ge(sem("c_t"), 1)
            cp(cols[:, 0:R_BMOD], bank(1, R_BMOD)).then_inc(sem("c_cols"), 1)
            dve.wait_ge(sem("c_cols"), 1)
            dve.wait_ge(sem("sig_c"), 1)
            tt(silu_c[:, :, :], silu_t[:, :].rearrange("p (v k) -> p k v", v=2),
               cols[:, 0:16].rearrange("p (v k) -> p k v", v=2), ALU.mult).then_inc(sem("silu_c"), 1)
            dve.wait_ge(sem("lst_in"), 16)
            cp(lsb[:, :, :], bc(lst[:, :], NS, 2)).then_inc(sem("lsb"), 1)
            dve.wait_ge(sem("cols_t"), 1)
            cp(cols[:, R_BMOD:], bank(0, NROW - R_BMOD, R_BMOD)).then_inc(sem("cols"), 1)
            dve.wait_ge(sem("cols"), 1)

            def mod_cols(i, chunk, b, freed):
                dve.wait_ge(sem("modt"), i + 1)
                ins = tt(modc[:, 4 * chunk:4 * chunk + 4, :], bank(b, 8).rearrange("p (j v) -> p j v", v=2),
                         bc(cols[:, R_BMOD + 4 * chunk:R_BMOD + 4 * chunk + 4], 2, 2), ALU.add)
                ins.then_inc(sem(freed), 1)

            for n in (0, 1):
                mod_cols(n, n, 5, "modc")
            for t in range(NT):
                dve.wait_ge(sem("x_ms"), t + 1)
                st(V.reciprocal(sml[:, 8 + t:9 + t], sml[:, t:t + 1]))
                st.settle()
                if t >= 2:
                    dve.wait_ge(sem("xh_tr"), t - 1)
                ts(xh[:, t % 2, :], xs[:, t, :], sml[:, 8 + t:9 + t], None, ALU.mult).then_inc(sem("xh"), 1)
                if t == 1:
                    for n in (2, 3):
                        mod_cols(n, n, 5, "modc")
                    dve.wait_ge(sem("modc"), 4)
                    for v in range(2):
                        st(stt(gmc[:, :, v], modc[:, 8 * M_SC:8 * M_SC + 8, v], 1.0, cols[:, R_GMIX:R_GMIX + 8],
                               ALU.add, ALU.mult))
                    st.settle()
                    cp(sml[:, 500:501], epsb[:, :]).then_inc(sem("gmc"), 1)
                if t >= 1:
                    for t2 in ([t - 1] if t < NT - 1 else [t - 1, t]):
                        dve.wait_ge(sem("xh_tr"), t2 + 1)
                        v = 1 if t2 < NCT else 0
                        for k in range(4, KD):
                            ins = ts(hT[:, k, t2 * P:(t2 + 1) * P], bank(2 * (t2 % 2) + 1, P, (k - 4) * P),
                                     gmc[:, k, v:v + 1], modc[:, 8 * M_SH + k, v:v + 1], ALU.mult, ALU.add)
                        ins.then_inc(sem("hT_d"), 1)

            st(cp(pos_f[:, :, :], pos_i[:, :, :]))
            st(cp(mul_f[:, :, :], mul_i[:, :, :]))
            st(cp(io_f[:, :], io_i[:, :]))
            st.settle()
            for axis in range(2):
                for f0, nf, o in ((0, 16, 16 * axis), (16, 8, 32 + 8 * axis)):
                    st(tt(turn[:, 0, :, o:o + nf], bc(pos_f[:, axis, :], nf, 2), bc(freq[:, f0:f0 + nf], NLT, 1), ALU.mult))
            st.settle()
            fraction(turn[:, 0], turn[:, 1])
            st(ts(turn[:, 1], turn[:, 0], 0.25, None, ALU.add))
            st.settle()
            fraction(turn[:, 1], turn[:, 2])
            cp(sml[:, 501:502], epsb[:, :]).then_inc(sem("turns"), 1)
            dve.wait_ge(sem("lam_in"), 16)
            lv = lamr.rearrange("p (a b s) -> p a b s", a=2, b=2)
            st(tt(rp[:, 0, 0:128].rearrange("p (a s) -> p a s", a=2), lv[:, :, 0], lv[:, :, 1], ALU.mult))
            st.settle()
            V.tensor_reduce(sml[:, 490:492], rp[:, 0, 0:128].rearrange("p (a s) -> p a s", a=2), AX.X, ALU.add).then_inc(
                sem("lam_s"), 1)
            dve.wait_ge(sem("lam_e"), 1)
            st(tt(sml[:, 492:493], sml[:, 491:492], sml[:, 490:491], ALU.subtract))
            st.settle()
            st(ts(sml[:, 493:494], sml[:, 492:493], LAM_INIT, None, ALU.subtract))
            st(ts(sml[:, 494:495], cols[:, R_SUB:R_SUB + 1], 1.0 - LAM_INIT, None, ALU.mult))

            AREC, AIMC = cols[:, R_ARE:R_ARE + 16], cols[:, R_AIM:R_AIM + 16]
            dve.wait_ge(sem("step"), 1)
            st(tt(s5p[:, 2, :], AIMC, s5p[:, 0, :], ALU.mult))
            tt(s5p[:, 1, :], AREC, s5p[:, 0, :], ALU.mult).then_inc(sem("ars"), 1)
            st.settle()
            st(ts(s5p[:, 2, :], s5p[:, 2, :], INV_2PI, None, ALU.mult))
            st.settle()
            fraction(s5p[:, 2, :], s5p[:, 4, :])
            st(tt(s5p[:, 4, :], AREC, AREC, ALU.mult))
            st(tt(s5p[:, 5, :], AIMC, AIMC, ALU.mult))
            st.settle()
            st(tt(s5p[:, 4, :], s5p[:, 4, :], s5p[:, 5, :], ALU.add))
            st.settle()
            st(V.reciprocal(s5p[:, 4, :], s5p[:, 4, :]))
            dve.wait_ge(sem("ct_t"), 1)
            ctv = PS[:, 3072:4096].rearrange("p (i q g n) -> p i q g n", i=8, q=4, g=2)
            for g2 in range(2):
                s = slice(NS * g2, NS * g2 + NS)
                for i in range(8):
                    r, d, hf = i // 4, i // 2 % 2, i % 2
                    ins = cp(BC[s, 2 + r, NPAIR * d + 4 * hf:NPAIR * d + 4 * hf + 4, :], ctv[s, i, :, g2, :])
                    if (g2, i) != (1, 7):
                        st(ins)
            ins.then_inc(sem("bc"), 1)

            for h in range(4):
                dve.wait_ge(sem("z"), h + 1)
                c0, nc_ = (0, 64) if h % 2 == 0 else (64, 32)
                cp(UT[:, h // 2, :, c0:c0 + nc_], bank(h, nc_ * CH).rearrange("p (c j) -> p j c", j=CH)).then_inc(
                    sem("z_free"), 1)

            st(V.memset(ZR[:, 0:512], 0.0))
            s5p_b = MP[:, X0 + 4352:X0 + 4608]

            def s5_setup(d, between=lambda i: None):
                q0 = NPAIR * d
                nm = NPOW + NCH
                sin_a = st1[:, 0:NPAIR * nm].rearrange("p (q m) -> p q m", q=NPAIR)
                cos_a = st2[:, 0:NPAIR * nm].rearrange("p (q m) -> p q m", q=NPAIR)
                tmp = MP[:, X0 + 2304:X0 + 2304 + NPAIR * nm].rearrange("p (q m) -> p q m", q=NPAIR)
                st(tt(sin_a, bc(s5p[:, 2, q0:q0 + NPAIR], nm, 2), bc(mul_f[:, d, :], NPAIR, 1), ALU.mult))
                st(tt(EM, bc(s5p[:, 1, q0:q0 + NPAIR], NPOW, 2), bc(mul_f[:, d, 0:NPOW], NPAIR, 1), ALU.mult))
                st.settle()
                fraction(sin_a, tmp)
                st(ts(cos_a, sin_a, 0.25, None, ALU.add))
                st.settle()
                fraction(cos_a, tmp)
                cp(sml[:, 502:503], epsb[:, :]).then_inc(sem("ang"), 1)
                between(0)
                dve.wait_ge(sem("tabs"), d + 1)
                for r in range(2):
                    st(tt(LP[:, r], LP[:, r], EM, ALU.mult))
                st.settle()
                one = 1 if d == 0 else CH - 1
                x, y = s5p[:, 5, 0:8], LP[:, 1, :, one]
                ar, ai, iv = AREC[:, q0:q0 + NPAIR], AIMC[:, q0:q0 + NPAIR], s5p[:, 4, q0:q0 + NPAIR]
                st(ts(x, LP[:, 0, :, one], 1.0, None, ALU.subtract))
                st.settle()
                f = [s5p[:, 6 + i, 0:8] for i in range(6)]
                st(tt(f[0], x, ar, ALU.mult))
                st(tt(f[1], y, ai, ALU.mult))
                st(tt(f[2], y, ar, ALU.mult))
                st(tt(f[3], x, ai, ALU.mult))
                st.settle()
                st(tt(f[0], f[0], f[1], ALU.add))
                st(tt(f[2], f[2], f[3], ALU.subtract))
                st.settle()
                st(tt(f[4], f[0], iv, ALU.mult))
                st(tt(f[5], f[2], iv, ALU.mult))
                st.settle()
                dve.wait_ge(sem("b_in"), 32)
                br, bi = BC[:, 0, q0:q0 + NPAIR, :], BC[:, 1, q0:q0 + NPAIR, :]
                cr, ci = bc(f[4], GRP, 2), bc(f[5], GRP, 2)
                t = [st1[:, 128 * i:128 * i + 128].rearrange("p (q n) -> p q n", q=NPAIR) for i in range(4)]
                st(tt(t[0], br, cr, ALU.mult))
                st(tt(t[1], bi, ci, ALU.mult))
                st(tt(t[2], bi, cr, ALU.mult))
                st(tt(t[3], br, ci, ALU.mult))
                st.settle()
                bb = [s5p_b[:, 128 * i:128 * i + 128].rearrange("p (q n) -> p q n", q=NPAIR) for i in range(2)]
                st(tt(bb[0], t[0], t[1], ALU.subtract))
                st(tt(bb[1], t[2], t[3], ALU.add))
                st.settle()
                for g2 in range(2):
                    s = slice(NS * g2, NS * g2 + NS)
                    for r in range(2):
                        st(cp(BBar[s, r, :, GRP * g2:GRP * (g2 + 1)], bb[r][s]))

                def times_powers(dst, x0, k0, nk, negate):
                    a0 = st1[:, 0:NPAIR * nk * GRP].rearrange("p (q k n) -> p q k n", q=NPAIR, k=nk)
                    a1 = st2[:, 0:NPAIR * nk * GRP].rearrange("p (q k n) -> p q k n", q=NPAIR, k=nk)
                    lr, li = (bc(LP[:, r, :, k0:k0 + nk], GRP, 3) for r in range(2))
                    xr, xi = (bc(x0[r], nk, 2) for r in range(2))
                    st(tt(a0, lr, xr, ALU.mult))
                    st(tt(a1, li, xi, ALU.mult))
                    st.settle()
                    st(tt(dst[0], a0, a1, ALU.subtract))
                    st.settle()
                    st(tt(a0, lr, xi, ALU.mult))
                    st(tt(a1, li, xr, ALU.mult))
                    st.settle()
                    if negate:
                        st(stt(dst[1].rearrange("p q k n -> p (q k n)"), a0.rearrange("p q k n -> p (q k n)"), -1.0,
                               a1.rearrange("p q k n -> p (q k n)"), ALU.mult, ALU.subtract))
                    else:
                        st(tt(dst[1], a0, a1, ALU.add))
                    st.settle()

                k0 = 0 if d == 0 else 1
                between(1)
                times_powers([PB[:, 0], PB[:, 1]], bb, k0, CH, False)
                cp(sml[:, 503:504], epsb[:, :]).then_inc(sem("pb"), 1)
                if d == 0:
                    dve.wait_ge(sem("bc"), 1)
                times_powers([CL[:, 0], CL[:, 1]], [BC[:, 2, q0:q0 + NPAIR, :], BC[:, 3, q0:q0 + NPAIR, :]], 0, NPOW, True)
                cp(sml[:, 504:505], epsb[:, :]).then_inc(sem("cl"), 1)

            def s5_scan(d):
                for c in range(4):
                    r, hq = divmod(c, 2)
                    dve.wait_ge(sem("bu"), 4 * d + c + 1)
                    if c == 0:
                        dve.wait_ge(sem("k_out"), 16 * (d + 1))
                    cp(GG[:, r, 4 * hq:4 * hq + 4, :], bank(6 + c % 2, 4 * NCH).rearrange("p (q c) -> p q c", q=4)).then_inc(
                        sem("bu_out"), 1)
                dve.wait_ge(sem("bu_out"), 4 * (d + 1))
                dve.wait_ge(sem("r8"), 1)
                co, si = ECS[:, 0], ECS[:, 1]
                st(tt(gt1, GG[:, 0], co, ALU.mult))
                st(tt(gt2, GG[:, 1], si, ALU.mult))
                st.settle()
                st(tt(gt1, gt1, gt2, ALU.add))
                st.settle()
                st(tt(gt2, GG[:, 0], si, ALU.mult))
                st(tt(GG[:, 1], GG[:, 1], co, ALU.mult))
                st.settle()
                st(tt(GG[:, 1], GG[:, 1], gt2, ALU.subtract))
                st(cp(GG[:, 0], gt1))
                st.settle()
                runs = [(0, NCH, False)] if d == 0 else [(0, NCC, True), (NCC, NCH, True)]
                for n, (c0, c1, back) in enumerate(runs):
                    for q in range(NPAIR):
                        decay = s5p[:, 3, NPAIR * d + q:NPAIR * d + q + 1].to_broadcast([P, c1 - c0])
                        for r in range(2):
                            x = GG[:, r, q, c0:c1]
                            if back:
                                x = x[:, ::-1]
                            st(V.tensor_tensor_scan(x, decay, x, 0.0 if n == 0 else GG[:, r, q, 0:1], ALU.mult, ALU.add))
                    st.settle()
                for r in range(2):
                    st(tt(gt1, GG[:, 0], ECS[:, r], ALU.mult))
                    st(tt(gt2, GG[:, 1], ECS[:, 1 - r], ALU.mult))
                    st.settle()
                    st(tt(HH[:, r, :, 0:NCH], gt1, gt2, ALU.add if r else ALU.subtract))
                    st.settle()
                if d == 1:
                    st(cp(HH[:, :, :, NCH], HH[:, :, :, 0]))
                    st.settle()
                cp(sml[:, 505:506], epsb[:, :]).then_inc(sem("hh"), 1)

            def s5_add(d):
                for h in range(2):
                    dve.wait_ge(sem("yy"), 2 * d + h + 1)
                    dst = yacc.rearrange("p (q g) c -> p q g c", g=2)[:, :, h, :]
                    src = bank(7 - h).rearrange("p (q c) -> p q c", q=NPAIR)
                    if d == 0:
                        cp(dst, src).then_inc(sem("yacc"), 1)
                    else:
                        tt(dst, src, dst, ALU.add).then_inc(sem("yacc"), 1)

            def rope(dst, src, nh, nf, t, f0):
                even, odd = src.rearrange("p h (f two) -> p h f two", two=2)[:, :, :, 0], \
                    src.rearrange("p h (f two) -> p h f two", two=2)[:, :, :, 1]
                de, do = dst.rearrange("p h (f two) -> p h f two", two=2)[:, :, :, 0], \
                    dst.rearrange("p h (f two) -> p h f two", two=2)[:, :, :, 1]
                c, s = (bc(turn[:, i, t, f0:f0 + nf], nh, 1) for i in (1, 2))
                r = [rp[:, i, 0:nh * nf].rearrange("p (h f) -> p h f", h=nh) for i in range(4)]
                st(tt(r[0], even, c, ALU.mult))
                st(tt(r[1], odd, s, ALU.mult))
                st(tt(r[2], even, s, ALU.mult))
                st(tt(r[3], odd, c, ALU.mult))
                st.settle()
                st(tt(de, r[0], r[1], ALU.subtract))
                st(tt(do, r[2], r[3], ALU.add))
                st.settle()

            def evacuate(w):
                kind, t = w
                dve.wait_ge(sem("z"), zi[w] + 1)
                src = bank(zi[w] % 4)
                n = ti.get(w)
                if n is not None:
                    if n >= 2:
                        dve.wait_ge(sem("turned"), n - 1)
                    dst = QR[:, n % 2, :]
                lt = t - NCT
                if kind in ("q", "k"):
                    if t >= NCT:
                        rope(dst.rearrange("p (h f) -> p h f", h=2 * DH), src.rearrange("p (h f) -> p h f", h=2 * DH),
                             2 * DH, DHD // 2, lt, 0)
                    else:
                        st(cp(dst, src))
                elif kind == "v":
                    st(cp(VV[:, t, :], src))
                elif kind == "m":
                    dve.wait_ge(sem("m_ms"), t + 1)
                    if t >= NCT:
                        st(V.reciprocal(sml[:, 16 + t:17 + t], sml[:, 16 + t:17 + t]))
                    st(V.reciprocal(sml[:, 24 + t:25 + t], sml[:, 24 + t:25 + t]))
                    st.settle()
                    if t >= NCT:
                        st(ts(dst[:, 0:QRANK], src[:, 0:QRANK], sml[:, 16 + t:17 + t], None, ALU.mult))
                    st(ts(dst[:, QRANK:QRANK + KVRANK], src[:, QRANK:QRANK + KVRANK], sml[:, 24 + t:25 + t], None, ALU.mult))
                    kr = src[:, QRANK + KVRANK:QRANK + KVRANK + MR]
                    if t >= NCT:
                        rope(KR[:, t:t + 1, :], kr.unsqueeze(1), 1, MR // 2, lt, 32)
                    else:
                        st(cp(KR[:, t, :], kr))
                elif kind == "uq":
                    s3 = src[:, 0:MH * MQ].rearrange("p (h f) -> p h f", h=MH)
                    d3 = dst[:, 0:MH * MQ].rearrange("p (h f) -> p h f", h=MH)
                    st(cp(d3[:, :, 0:MN], s3[:, :, 0:MN]))
                    rope(d3[:, :, MN:], s3[:, :, MN:], MH, MR // 2, lt, 32)
                else:
                    s3 = src.rearrange("p (h f) -> p h f", h=MH)
                    d3 = dst[:, 0:MH * MQ].rearrange("p (h f) -> p h f", h=MH)
                    st(cp(d3[:, :, 0:MN], s3[:, :, 0:MN]))
                    st(cp(d3[:, :, MN:], bc(KR[:, t, :], MH, 1)))
                    st(cp(MVV[:, t, :].rearrange("p (h f) -> p h f", h=MH), s3[:, :, MN:]))
                st.settle()
                if n is not None:
                    cp(sml[:, 506:507], epsb[:, :]).then_inc(sem("qr"), 1)
                cp(sml[:, 507:508], epsb[:, :]).then_inc(sem("z_free"), 1)

            dve.wait_ge(sem("kpad_clear"), 32)
            s5_setup(0)
            dve.wait_ge(sem("rope_t"), 2)
            for t in range(NCT, NT):
                evacuate(("q", t))
            for t in range(2):
                evacuate(("k", t))
            s5_scan(0)
            for t in range(2, NT):
                evacuate(("k", t))
            s5_add(0)
            s5_setup(1, lambda i: evacuate(("v", i)))
            for t in range(2, NT):
                evacuate(("v", t))
            s5_scan(1)
            s5_add(1)
            for t in range(4):
                evacuate(("m", t))

            dve.wait_ge(sem("y_in"), 32)
            for h in range(2):
                st(stt(YT[:, h], UT[:, h, :, NCC:], cols[:, R_SD + h:R_SD + h + 1], YT[:, h], ALU.mult, ALU.add))
            st.settle()
            st(tt(yt1, YT, YT, ALU.mult))
            st.settle()
            st(ts(yt1, yt1, 0.044715, 1.0, ALU.mult, ALU.add))
            st.settle()
            tt(yt1, yt1, YT, ALU.mult).then_inc(sem("gelu_in"), 1)
            evacuate(("m", NT - 2))
            dve.wait_ge(sem("tanh"), 1)
            st(ts(yt1, yt1, 0.5, 0.5, ALU.mult, ALU.add))
            st.settle()
            tt(YG, yt1, YT, ALU.mult).then_inc(sem("yg"), 1)
            evacuate(("m", NT - 1))
            dve.wait_ge(sem("yg"), 1)
            for i in (4, 5):
                mod_cols(i, plan_mod[i][1], 6 + i % 2, "modc")
            for mo in range(2):
                dve.wait_ge(sem("s5_sig"), mo + 1)
                tt(mix[:, mo, :].rearrange("p (c j) -> p j c", j=CH), YG[:, mo], yt1[:, mo], ALU.mult).then_inc(
                    sem("s5_mix"), 1)
            for kind, first in (("uq", NCT), ("ukv", 0)):
                for t in range(first, NT):
                    evacuate((kind, t))

            dve.wait_ge(sem("s5_mix"), 2)
            cp(silu_cb, silu_c[:, :, 0:1].to_broadcast([P, KD, P])).then_inc(sem("silu_cb"), 1)

            def maxima(b):
                kind = blocks[b][0]
                for m in range(2 if kind == "d" else 1):
                    u = unit0[b] + m
                    dve.wait_ge(sem("scores"), u + 1)
                    base = 1024 * (u % 2)
                    st(V.tensor_reduce(sml[:, 112 + u:113 + u], PS[:, base:base + TOK], AX.X, ALU.max))
                    st.settle()
                    ts(sml[:, 64 + u:65 + u], sml[:, 112 + u:113 + u], -(DSCALE if kind == "d" else MSCALE), None,
                       ALU.mult).then_inc(sem("nmax"), 1)

            def combine(b):
                kind = blocks[b][0]
                u = unit0[b]
                p0, p1 = pbuf[:, 2 * (b % 2), :], pbuf[:, 2 * (b % 2) + 1, :]
                dve.wait_ge(sem("probs"), u + 1)
                st(V.reciprocal(sml[:, 208 + u:209 + u], sml[:, 160 + u:161 + u]))
                st.settle()
                if kind == "l":
                    ts(p0, p0, sml[:, 208 + u:209 + u], None, ALU.mult).then_inc(sem("pc"), 1)
                    return
                st(ts(p0, p0, sml[:, 208 + u:209 + u], None, ALU.mult))
                dve.wait_ge(sem("probs"), u + 2)
                st(V.reciprocal(sml[:, 209 + u:210 + u], sml[:, 161 + u:162 + u]))
                st.settle()
                st(tt(sml[:, 209 + u:210 + u], sml[:, 209 + u:210 + u], sml[:, 493:494], ALU.mult))
                st.settle()
                stt(p1, p1, sml[:, 209 + u:210 + u], p0, ALU.mult, ALU.add).then_inc(sem("pc"), 1)

            def diagonal(h):
                dve.wait_ge(sem("b6"), six_n[("ss", DH - 1) if h == 0 else ("root", h - 1)] + 1)
                tt(sq.rearrange("p (t n) -> p t n", t=NLT), bc(ident, NLT, 1), bc(ssq[:, NLT * h:NLT * h + NLT], P, 2),
                   ALU.mult).then_inc(sem("diag"), 1)

            maxima(0)
            for b in range(len(blocks)):
                combine(b)
                if b + 1 < len(blocks):
                    maxima(b + 1)
                if b in summed_at:
                    n = summed_at[b]
                    dve.wait_ge(sem("mod_sum"), n + 1)
                    half = n % 2
                    if n < 2:
                        c = 4 * by_pool[n][1]
                        tt(modc[:, c:c + 4, 0], bank(7, 4), cols[:, R_BMOD + c:R_BMOD + c + 4], ALU.add).then_inc(
                            sem("b7_free"), 1)
                    else:
                        dve.wait_ge(sem("gm_in"), 16)
                        g = GM[:, 512 * half:512 * half + 512]
                        tt(g, g, bank(7), ALU.add).then_inc(sem("b7_free"), 1)
                    if n == 1:
                        dve.wait_ge(sem("b7_free"), 2)
                        stt(gfc[:, :], modc[:, 8 * F_SC:8 * F_SC + 8, 0], 1.0, cols[:, R_GFFN:R_GFFN + 8], ALU.add,
                            ALU.mult).then_inc(sem("gfc"), 1)
                what = six.get(b, ("", 0))
                if what[0] == "ss":
                    h = what[1]
                    dve.wait_ge(sem("b6"), six_n[what] + 1)
                    cp(ssq[:, NLT * h:NLT * h + NLT], bank(6, NLT)).then_inc(sem("b6_free"), 1)
                    dve.wait_ge(sem("b6_free"), six_n[what] + 1)
                    cp(sml[:, 508:509], epsb[:, :]).then_inc(sem("ssq"), 1)
                if b == 4 * DH + 4:
                    dve.wait_ge(sem("rms"), 1)
                    st(V.reciprocal(ssq, ssq))
                    st.settle()
                    diagonal(0)
                if what[0] == "root":
                    h = what[1]
                    dve.wait_ge(sem("b6"), six_n[what] + 1)
                    stt(mix[:, 2 + h, :], mix[:, 2 + h, :], sml[:, 494:495], bank(6), ALU.mult, ALU.mult).then_inc(
                        sem("b6_free"), 1)
                    if h + 1 < DH:
                        diagonal(h + 1)

            dve.wait_ge(sem("xr_in"), 16 * NLT)
            dve.wait_ge(sem("b7_free"), len(by_pool))
            def add_mixer(t):
                for half in range(2):
                    c = slice(512 * half, 512 * half + 512)
                    i = 2 * t + half
                    dve.wait_ge(sem("op"), i + 1)
                    tmp = ot1[:, 512 * (i % 2):512 * (i % 2) + 512]
                    st(tt(tmp, bank(i % 4), GM[:, c], ALU.mult))
                    st.settle()
                    tt(XN[:, t, c], XN[:, t, c], tmp, ALU.add).then_inc(sem("xn"), 1)

            dve.wait_ge(sem("gfc"), 1)
            for t in range(NLT):
                add_mixer(t)
                dve.wait_ge(sem("xn_ms"), t + 1)
                st(V.reciprocal(sml[:, 36 + t:37 + t], sml[:, 32 + t:33 + t]))
                st.settle()
                ts(xhf[:, t, :], XN[:, t, :], sml[:, 36 + t:37 + t], None, ALU.mult).then_inc(sem("xhf"), 1)
                if t >= 1:
                    for t2 in ([t - 1] if t < NLT - 1 else [t - 1, t]):
                        dve.wait_ge(sem("xhf_tr"), t2 + 1)
                        for k in range(4, KD):
                            ins = ts(hfT[:, k, t2 * P:(t2 + 1) * P], bank(5 + 2 * (t2 % 2), P, (k - 4) * P),
                                     gfc[:, k:k + 1], modc[:, 8 * F_SH + k, 0:1], ALU.mult, ALU.add)
                        ins.then_inc(sem("hfT_d"), 1)

            st(ts(tri_inc[0:NE, :], ident[0:NE, 0:NE], 1.0, None, ALU.mult))
            st(ts(tri128[0:NE, :], tri[0:NE, 0:NE], float(P), None, ALU.mult))
            st.settle()
            st(tt(tri_inc[0:NE, :], tri_inc[0:NE, :], tri[0:NE, 0:NE], ALU.add))
            dve.wait_ge(sem("small_in"), 16 * 7)
            dve.wait_ge(sem("logits"), 1)
            st(tt(logit, bank(0, 144).rearrange("p (t e) -> p t e", t=NLT), bc(brt[:, :], NLT, 1), ALU.add))
            st.settle()

            def first_max(dst, x, n, top, tmp):
                st(V.tensor_reduce(top, x, AX.X, ALU.max))
                st.settle()
                st(tt(tmp, x, bc(top, n, 2), ALU.is_equal))
                st.settle()
                st(ts(tmp, tmp, -64.0, 64.0, ALU.mult, ALU.add))
                st.settle()
                st(tt(tmp, tmp, bc(io_f[:, 0:n], NLT, 1), ALU.add))
                st.settle()
                st(V.tensor_reduce(wts[:, 7, :], tmp, AX.X, ALU.min))
                st.settle()
                st(tt(dst, bc(io_f[:, 0:n], NLT, 1), bc(wts[:, 7, :], n, 2), ALU.is_equal))
                st.settle()

            gl, el = logit[:, :, 0:NGR], logit[:, :, NGR:]
            first_max(goh, gl, NGR, wts[:, 2, :], gra)
            tt(gra, gl, bc(wts[:, 2, :], NGR, 2), ALU.subtract).then_inc(sem("g_in"), 1)
            e4 = emsk.rearrange("p t (g e) -> p (t g) e", g=NGR)
            st(ts(rb[:, :, 0:NGR], goh, 1e30, -1e30, ALU.mult, ALU.add))
            st(cp(ra, el))
            st.settle()
            st(tt(e4, ra.rearrange("p t (g e) -> p (t g) e", g=NGR), bc(goh.rearrange("p t g -> p (t g)"), EPG, 2), ALU.mult))
            st(cp(gidxf, rb[:, :, 0:NGR]))
            st.settle()
            st(tt(e4, e4, bc(gidxf.rearrange("p t g -> p (t g)"), EPG, 2), ALU.add))
            st.settle()
            first_max(oneh[:, 0], emsk, NE, wts[:, 5, :], ra)
            st(ts(ra, oneh[:, 0], -2e30, None, ALU.mult))
            st.settle()
            st(tt(emsk, emsk, ra, ALU.add))
            st.settle()
            first_max(oneh[:, 1], emsk, NE, wts[:, 6, :], ra)
            tt(mask, oneh[:, 0], oneh[:, 1], ALU.add).then_inc(sem("mask"), 1)
            tt(wts[:, 4, :], wts[:, 6, :], wts[:, 5, :], ALU.subtract).then_inc(sem("e_in"), 1)
            dve.wait_ge(sem("cnt"), 1)
            for i in range(LAT // P):
                st(ts(nbt[0:NE, i:i + 1], PS[0:NE, 2560:2561], float(P * i), None, ALU.is_gt))
            st.settle()
            st(V.tensor_reduce(nbv[0:NE], nbt[0:NE, :], AX.X, ALU.add))
            st.settle()
            cp(nb_b[0:NE, :], nbv[0:NE].to_broadcast([NE, P])).then_inc(sem("nb"), 1)
            dve.wait_ge(sem("g_exp"), 1)
            dve.wait_ge(sem("e_exp"), 1)
            st(V.tensor_reduce(wts[:, 3, :], gra, AX.X, ALU.add))
            st(ts(wts[:, 2, :], wts[:, 4, :], 1.0, None, ALU.add))
            st.settle()
            st(tt(wts[:, 3, :], wts[:, 3, :], wts[:, 2, :], ALU.mult))
            st.settle()
            st(V.reciprocal(wts[:, 0, :], wts[:, 3, :]))
            st.settle()
            st(tt(wts[:, 1, :], wts[:, 4, :], wts[:, 0, :], ALU.mult))
            dve.wait_ge(sem("ends"), 1)
            st(cp(endv[0:NE], PS[0:NE, 2562:2563]))
            st.settle()
            st(ts(cmpb[0:NE, 0:NBLK], io_f[0:NE, :], endv[0:NE], None, ALU.is_ge))
            cp(cmpb[0:NE, NBLK:NBLK + 1], nbv[0:NE]).then_inc(sem("cmp"), 1)
            dve.wait_ge(sem("place"), 1)
            for k in range(TOPK):
                pos, blk = rb[:, k, 0:NLT], rb[:, 2 + k, 0:NLT]
                st(tt(ra, oneh[:, k], bank(6, NLT * NE).rearrange("p (t e) -> p t e", t=NLT), ALU.mult))
                st.settle()
                st(V.tensor_reduce(pos, ra, AX.X, ALU.add))
                st.settle()
                st(ts(blk, pos, -(P - 1) / 2.0, 1.0 / P, ALU.add, ALU.mult))
                st(ts(pos, pos, float(NBLK), None, ALU.mult))
                st.settle()
                st(ts(blk, blk, MAGIC, MAGIC, ALU.add, ALU.subtract))
                st.settle()
                stt(pos_k[:, k, :], blk, -float(P * NBLK - 1), pos, ALU.mult, ALU.add).then_inc(sem("pos_k"), 1)
            dve.wait_ge(sem("bt"), 1)
            st(cp(btab[:, 0:NBLK], PS[0:1, 3584:3584 + NBLK]))
            ts(btab[:, NBLK:], PS[0:1, 3584 + NBLK:3584 + NBLK + 1], -2.0, None, ALU.add).then_inc(sem("routed"), 1)

            dve.wait_ge(sem("gf_in"), 16)
            for half in range(2):
                dve.wait_ge(sem("mod_wide"), half + 1)
                tt(GF[:, 512 * half:512 * half + 512], GF[:, 512 * half:512 * half + 512], bank(2 + half), ALU.add).then_inc(
                    sem("gf"), 1)
            dve.wait_ge(sem("gf"), 2)

            dve.wait_ge(sem("routed"), 1)
            last2 = dve.value_load(btab[0:1, NBLK:NBLK + 1], min_val=LAT * TOPK // P - 2, max_val=NBLK - 2)

            def rows_T(b):
                dve.wait_ge(sem("hg_tr"), b + 1)
                for k in range(4, KD):
                    ins = ts(hgT[:, k, :], bank(1, P, (k - 4) * P), gfc[:, k:k + 1], modc[:, 8 * F_SH + k, 0:1],
                             ALU.mult, ALU.add)
                ins.then_inc(sem("hgT_d"), 1)

            def hidden(b):
                dve.wait_ge(sem("sg"), b + 1)
                dve.wait_ge(sem("w3_used"), b + 1)
                tt(hid, sg, bank(3), ALU.mult).then_inc(sem("hid"), 1)

            def results(b, ysb=ysb, last=False):
                dve.wait_ge(sem("w2_used"), b + 1)
                if not last and (not isinstance(b, int) or b >= 1):
                    dve.wait_ge(sem("y_sc"), 16 * b)
                for n in range(2):
                    tt(ysb[:, 512 * n:512 * n + 512], bank((0 if last else 5) + n), GF[:, 512 * n:512 * n + 512], ALU.mult).then_inc(
                        sem("ysb"), 1)

            rows_T(0)
            hidden(0)
            rows_T(1)
            hidden(1)
            rows_T(2)
            results(0)
            with dve.Fori(2, last2 + 1) as b:
                hidden(b)
                rows_T(b + 1)
                results(b - 1)
            hidden(last2 + 1)
            results(last2)
            results(last2 + 1, ysb_last, True)

            def last_root(t):
                dve.wait_ge(sem("f_ms"), t + 1)
                V.reciprocal(sml[:, 44 + t:45 + t], sml[:, 40 + t:41 + t]).then_inc(sem("f_root"), 1)

            for t in range(NLT):
                dve.wait_ge(sem(f"tile_in{t}"), 16 + 16 * TOPK)
                y0, y1 = yk_of[t][:, 0, :], yk_of[t][:, 1, :]
                st(stt(XN[:, t, :], y0, wts[:, 0, t:t + 1], XN[:, t, :], ALU.mult, ALU.add))
                st.settle()
                stt(XN[:, t, :], y1, wts[:, 1, t:t + 1], XN[:, t, :], ALU.mult, ALU.add).then_inc(sem("x_out"), 1)
                if t >= 1:
                    last_root(t - 1)
            dve.wait_ge(sem("fng_in"), 16)
            for t in range(2, NLT):
                if t == NLT - 1:
                    last_root(t)
                dve.wait_ge(sem("f_root"), t + 1)
                stt(XN[:, t, :], XN[:, t, :], sml[:, 44 + t:45 + t], fng, ALU.mult, ALU.mult).then_inc(sem("fin_v"), 1)


_INS = ["x", "c", "ctx", "c_ctx", "w_mod", "b_mod", "norm_mix_g", "norm_ffn_g", "w_in", "s5_a_re", "s5_a_im",
        "s5_log_step", "s5_b_re", "s5_b_im", "s5_c_re", "s5_c_im", "s5_d", "s5_w_glu", "s5_b_glu", "diff_lambda",
        "diff_subln_g", "mla_q_norm_g", "mla_w_uq", "mla_kv_norm_g", "mla_w_ukv", "w_out", "moe_w_group",
        "moe_b_group", "moe_w_router", "moe_b_router", "moe_w1", "moe_w3", "moe_w2", "final_norm_g"]


def kernel(**inputs):
    import numpy as _np
    import concourse.bacc as _bacc
    from concourse import mybir as _mybir
    from concourse.bass_utils import run_bass_kernel_spmd as _run

    nc = _bacc.Bacc("TRN2", target_bir_lowering=False, num_devices=1)
    arrays, args = {}, {}
    for name in _INS:
        v = _np.ascontiguousarray(inputs[name])
        arrays[f"in_{name}"] = v
        args[name] = nc.dram_tensor(f"in_{name}", v.shape, _mybir.dt.from_np(v.dtype), kind="ExternalInput").ap()
    out = nc.dram_tensor("out", (1, LAT, D), F32, kind="ExternalOutput").ap()
    build(nc, args, out)
    r = _run(nc, [arrays], core_ids=[0])
    return r.results[0]["out"]
```
